# Optimizing a Trainium2 kernel written in Bass

```python
import jax, jax.numpy as jnp
from jax import lax
import numpy as np
import math

D_MODEL = 1024
BATCH = 1
SEQ = 256
DEPTH = 2

N_HEADS = 16
HEAD_DIM = 64
N_KV_HEADS = 4
ROT_DIM = HEAD_DIM // 4
ROPE_THETA = 500000.0
MOBA_BLOCK = 256
MOBA_TOPK = 3
MOBA_QCHUNK = 32
WINDOW = 128
D_FF = 2816
CONV_W = 3
N_A = DEPTH // 2
N_B = DEPTH - N_A
EPS = 1e-6
NEG = -1e30


def rmsnorm(x, g):
    xf = x.astype(jnp.float32)
    y = xf * lax.rsqrt(jnp.mean(xf * xf, axis=-1, keepdims=True) + EPS)
    return (y * g.astype(jnp.float32)).astype(x.dtype)

def rope_tables(positions):
    inv_freq = ROPE_THETA ** (-jnp.arange(0, ROT_DIM, 2, dtype=jnp.float32) / ROT_DIM)
    ang = positions.astype(jnp.float32)[..., None] * inv_freq
    return jnp.cos(ang)[:, :, None, :], jnp.sin(ang)[:, :, None, :]

def partial_rope(x, cos, sin):
    half = ROT_DIM // 2
    x1 = x[..., :half].astype(jnp.float32)
    x2 = x[..., half:ROT_DIM].astype(jnp.float32)
    r1 = (x1 * cos - x2 * sin).astype(x.dtype)
    r2 = (x2 * cos + x1 * sin).astype(x.dtype)
    return jnp.concatenate([r1, r2, x[..., ROT_DIM:]], axis=-1)

def moba_attention(q, k, v):
    B_, H_, S_, dh = q.shape
    nb = -(-S_ // MOBA_BLOCK)
    pad = nb * MOBA_BLOCK - S_
    kp = jnp.pad(k, ((0, 0), (0, 0), (0, pad), (0, 0)))
    vp = jnp.pad(v, ((0, 0), (0, 0), (0, pad), (0, 0)))
    kb = kp.reshape(B_, H_, nb, MOBA_BLOCK, dh)
    vb = vp.reshape(B_, H_, nb, MOBA_BLOCK, dh)
    k_mean = jnp.mean(kb.astype(jnp.float32), axis=3)
    q_blk = jnp.arange(S_) // MOBA_BLOCK
    gate = jnp.einsum('bhsd,bhnd->bhsn', q.astype(jnp.float32), k_mean)
    past = jnp.arange(nb)[None, :] < q_blk[:, None]
    gate = jnp.where(past, gate, NEG)
    n_sel = min(MOBA_TOPK, nb)
    _, sel_idx = lax.top_k(gate, n_sel)
    sel_valid = jnp.arange(n_sel)[None, :] < q_blk[:, None]
    scale = HEAD_DIM ** -0.5
    bi = jnp.arange(B_)[:, None, None, None]
    hi = jnp.arange(H_)[None, :, None, None]
    qpos_local = jnp.arange(MOBA_QCHUNK)
    kpos_local = jnp.arange(MOBA_BLOCK)

    def chunk(c):
        q0 = c * MOBA_QCHUNK
        qc = lax.dynamic_slice_in_dim(q, q0, MOBA_QCHUNK, axis=2)
        idx = lax.dynamic_slice_in_dim(sel_idx, q0, MOBA_QCHUNK, axis=2)
        valid = lax.dynamic_slice_in_dim(sel_valid, q0, MOBA_QCHUNK, axis=0)
        k_g = kb[bi, hi, idx]
        v_g = vb[bi, hi, idx]
        l_sel = jnp.einsum('bhqd,bhqnpd->bhqnp', qc, k_g).astype(jnp.float32) * scale
        l_sel = jnp.where(valid[None, None, :, :, None], l_sel, NEG)
        l_sel = l_sel.reshape(B_, H_, MOBA_QCHUNK, n_sel * MOBA_BLOCK)
        own0 = (q0 // MOBA_BLOCK) * MOBA_BLOCK
        k_own = lax.dynamic_slice_in_dim(kp, own0, MOBA_BLOCK, axis=2)
        v_own = lax.dynamic_slice_in_dim(vp, own0, MOBA_BLOCK, axis=2)
        l_own = jnp.einsum('bhqd,bhpd->bhqp', qc, k_own).astype(jnp.float32) * scale
        causal = (own0 + kpos_local)[None, :] <= (q0 + qpos_local)[:, None]
        l_own = jnp.where(causal, l_own, NEG)
        p = jax.nn.softmax(jnp.concatenate([l_sel, l_own], axis=-1), axis=-1).astype(v.dtype)
        p_sel = p[..., :n_sel * MOBA_BLOCK].reshape(B_, H_, MOBA_QCHUNK, n_sel, MOBA_BLOCK)
        p_own = p[..., n_sel * MOBA_BLOCK:]
        return (jnp.einsum('bhqnp,bhqnpd->bhqd', p_sel, v_g)
                + jnp.einsum('bhqp,bhpd->bhqd', p_own, v_own))

    out = lax.map(chunk, jnp.arange(S_ // MOBA_QCHUNK))
    return out.transpose(1, 2, 0, 3, 4).reshape(B_, H_, S_, dh)

def swa_sink_attention(q, k, v, sinks):
    B_, Hq, S_, dh = q.shape
    G = Hq // N_KV_HEADS
    nq = S_ // WINDOW
    qb = q.reshape(B_, N_KV_HEADS, G, nq, WINDOW, dh)
    kb = k.reshape(B_, N_KV_HEADS, nq, WINDOW, dh)
    vb = v.reshape(B_, N_KV_HEADS, nq, WINDOW, dh)
    kcat = jnp.concatenate([jnp.pad(kb, ((0, 0), (0, 0), (1, 0), (0, 0), (0, 0)))[:, :, :-1], kb], axis=3)
    vcat = jnp.concatenate([jnp.pad(vb, ((0, 0), (0, 0), (1, 0), (0, 0), (0, 0)))[:, :, :-1], vb], axis=3)
    logits = jnp.einsum('bkgnqd,bknpd->bkgnqp', qb, kcat).astype(jnp.float32) * (HEAD_DIM ** -0.5)
    rel = (jnp.arange(WINDOW)[:, None] + WINDOW) - jnp.arange(2 * WINDOW)[None, :]
    band = (rel >= 0) & (rel < WINDOW)
    key_pos = jnp.arange(nq)[:, None, None] * WINDOW - WINDOW + jnp.arange(2 * WINDOW)[None, None, :]
    mask = band[None] & (key_pos >= 0)
    logits = jnp.where(mask, logits, NEG)
    sink = sinks.astype(jnp.float32).reshape(N_KV_HEADS, G)[None, :, :, None, None, None]
    m = jnp.maximum(jnp.max(logits, axis=-1, keepdims=True), sink)
    e = jnp.exp(logits - m)
    p = e / (jnp.sum(e, axis=-1, keepdims=True) + jnp.exp(sink - m))
    out = jnp.einsum('bkgnqp,bknpd->bkgnqd', p.astype(v.dtype), vcat)
    return out.reshape(B_, Hq, S_, dh)

def conv_ffn(h, w_up, conv_w, conv_b, w_down):
    S_ = h.shape[1]
    u = h @ w_up
    up = jnp.pad(u, ((0, 0), (CONV_W - 1, 0), (0, 0)))
    u = conv_b + sum(conv_w[j] * up[:, j:j + S_] for j in range(CONV_W))
    gate, val = jnp.split(u, 2, axis=-1)
    return (jax.nn.silu(gate) * val) @ w_down

def first_inputs(seed: int = 0) -> dict:
    key = jax.random.key(seed)
    ks = jax.random.split(key, 20)
    D = D_MODEL
    kv_w = 2 * N_KV_HEADS * HEAD_DIM
    res_scale = (2 * DEPTH) ** -0.5

    def nrm(k, shape, fan_in, extra=1.0):
        return jax.random.normal(k, shape, jnp.float32) * (fan_in ** -0.5) * extra

    def gain(k, shape):
        return 1.0 + 0.02 * jax.random.normal(k, shape, jnp.float32)

    offset = jax.random.randint(ks[1], (BATCH, 1), 0, 1024, dtype=jnp.int32)
    positions = offset + jnp.arange(SEQ, dtype=jnp.int32)[None, :]
    return {
        'x': jax.random.normal(ks[0], (BATCH, SEQ, D), jnp.float32),
        'positions': positions,
        'attn_norm': gain(ks[2], (DEPTH, D)),
        'w_qkv_a': nrm(ks[3], (N_A, D, 3 * N_HEADS * HEAD_DIM), D),
        'w_o_a': nrm(ks[4], (N_A, N_HEADS * HEAD_DIM, D), N_HEADS * HEAD_DIM, res_scale),
        'kv_norm': gain(ks[5], (D,)),
        'w_kv_b': nrm(ks[6], (D, kv_w), D),
        'w_q_b': nrm(ks[7], (N_B, D, N_HEADS * HEAD_DIM), D),
        'sinks_b': 0.5 * jax.random.normal(ks[8], (N_B, N_HEADS), jnp.float32),
        'w_o_b': nrm(ks[9], (N_B, N_HEADS * HEAD_DIM, D), N_HEADS * HEAD_DIM, res_scale),
        'ffn_norm': gain(ks[10], (DEPTH, D)),
        'w_up': nrm(ks[11], (DEPTH, D, 2 * D_FF), D),
        'conv_w': nrm(ks[12], (DEPTH, CONV_W, 2 * D_FF), CONV_W),
        'conv_b': 0.01 * jax.random.normal(ks[13], (DEPTH, 2 * D_FF), jnp.float32),
        'w_down': nrm(ks[14], (DEPTH, D_FF, D), D_FF, res_scale),
        'final_norm': gain(ks[15], (D,)),
    }

def first_block(x, positions, attn_norm, w_qkv_a, w_o_a, kv_norm, w_kv_b, w_q_b, sinks_b,
              w_o_b, ffn_norm, w_up, conv_w, conv_b, w_down, final_norm):
    B_, S_, _ = x.shape
    cos, sin = rope_tables(positions)

    def heads(t, n):
        return t.reshape(B_, S_, n, HEAD_DIM)

    def to_bhsd(t):
        return t.transpose(0, 2, 1, 3)

    shared_k = None
    shared_v = None
    for l in range(DEPTH):
        if l < N_A:
            h = rmsnorm(x, attn_norm[l])
            q, k, v = jnp.split(h @ w_qkv_a[l], 3, axis=-1)
            q = partial_rope(heads(q, N_HEADS), cos, sin)
            k = partial_rope(heads(k, N_HEADS), cos, sin)
            o = moba_attention(to_bhsd(q), to_bhsd(k), to_bhsd(heads(v, N_HEADS)))
            w_o = w_o_a[l]
        else:
            if l == N_A:
                hk = rmsnorm(x, kv_norm)
                k, v = jnp.split(hk @ w_kv_b, 2, axis=-1)
                shared_k = to_bhsd(partial_rope(heads(k, N_KV_HEADS), cos, sin))
                shared_v = to_bhsd(heads(v, N_KV_HEADS))
            i = l - N_A
            h = rmsnorm(x, attn_norm[l])
            q = partial_rope(heads(h @ w_q_b[i], N_HEADS), cos, sin)
            o = swa_sink_attention(to_bhsd(q), shared_k, shared_v, sinks_b[i])
            w_o = w_o_b[i]
        x = x + o.transpose(0, 2, 1, 3).reshape(B_, S_, N_HEADS * HEAD_DIM) @ w_o
        x = x + conv_ffn(rmsnorm(x, ffn_norm[l]), w_up[l], conv_w[l], conv_b[l], w_down[l])
    return rmsnorm(x, final_norm)


DEPTH_2 = 1

CHUNK = 64
A_HEADS = 8
A_DK = 128
A_DV = 256
CONV_W_2 = 4
B_HEADS = 4
B_DK = 256
B_DV = 512
ROPE_BASE = 10000.0
D_FF_2 = 4 * D_MODEL

A_QK = A_HEADS * A_DK
A_V = A_HEADS * A_DV
B_QK = B_HEADS * B_DK
B_V = B_HEADS * B_DV
IN_SIZES = (A_QK, A_QK, A_V, A_V, A_HEADS, A_HEADS, B_QK, B_QK, B_V, B_V, D_MODEL, D_MODEL)
D_IN = sum(IN_SIZES)


def rmsnorm_2(x, w):
    xf = x.astype(jnp.float32)
    y = xf * lax.rsqrt(jnp.mean(xf * xf, axis=-1, keepdims=True) + EPS)
    return (y * w.astype(jnp.float32)).astype(x.dtype)

def l2norm(x):
    xf = x.astype(jnp.float32)
    return (xf * lax.rsqrt(jnp.sum(xf * xf, axis=-1, keepdims=True) + EPS)).astype(x.dtype)

def _split_cols(t, sizes):
    out, start = [], 0
    for s in sizes:
        out.append(t[..., start:start + s])
        start += s
    return out

def causal_depthwise_conv(x, w):
    k_taps, s = w.shape[0], x.shape[1]
    xp = jnp.pad(x, ((0, 0), (k_taps - 1, 0), (0, 0)))
    y = xp[:, 0:s] * w[0]
    for j in range(1, k_taps):
        y = y + xp[:, j:j + s] * w[j]
    return y

def rotary(t, positions):
    d = t.shape[-1]
    inv_freq = ROPE_BASE ** (-jnp.arange(0, d, 2, dtype=jnp.float32) / d)
    ang = positions.astype(jnp.float32)[:, None] * inv_freq[None, :]
    cos = jnp.cos(ang)[None, :, None, :]
    sin = jnp.sin(ang)[None, :, None, :]
    t1, t2 = t[..., :d // 2], t[..., d // 2:]
    return jnp.concatenate([t1 * cos - t2 * sin, t1 * sin + t2 * cos], axis=-1).astype(t.dtype)

def to_chunks(t):
    b, s, h = t.shape[:3]
    t = t.reshape(b, s // CHUNK, CHUNK, h, *t.shape[3:])
    return jnp.moveaxis(t, 3, 1)

def from_chunks(t):
    t = jnp.moveaxis(t, 1, 3)
    return t.reshape(t.shape[0], t.shape[1] * t.shape[2], *t.shape[3:])

def chunk_gated_delta_rule(q, k, v, beta, g):
    dtype = v.dtype
    q, k, v = (to_chunks(t.astype(jnp.float32)) for t in (q, k, v))
    beta, g = (to_chunks(t.astype(jnp.float32)) for t in (beta, g))
    g_cum = jnp.cumsum(g, axis=-1)
    idx = jnp.arange(CHUNK)
    causal = idx[:, None] >= idx[None, :]
    strict = idx[:, None] > idx[None, :]
    decay = jnp.exp(jnp.where(causal, g_cum[..., :, None] - g_cum[..., None, :], -jnp.inf))
    k_beta = k * beta[..., None]
    lower = jnp.where(strict, jnp.einsum('bhncd,bhnmd->bhncm', k_beta, k) * decay, 0.0)
    eye = jnp.broadcast_to(jnp.eye(CHUNK, dtype=jnp.float32), lower.shape)
    t_inv = lax.linalg.triangular_solve(lower, eye, left_side=True, lower=True, unit_diagonal=True)
    u = jnp.einsum('bhncm,bhnme->bhnce', t_inv, v * beta[..., None])
    w = jnp.einsum('bhncm,bhnmd->bhncd', t_inv, k_beta * jnp.exp(g_cum)[..., None])
    attn = jnp.where(causal, jnp.einsum('bhncd,bhnmd->bhncm', q, k) * decay, 0.0)
    q_exp = q * jnp.exp(g_cum)[..., None]
    g_last = g_cum[..., -1:]
    k_dec = k * jnp.exp(g_last - g_cum)[..., None]
    last_dec = jnp.exp(g_last[..., 0])

    def step(state, inp):
        qe, ww, uu, aqk, kd, ld = inp
        v_new = uu - jnp.einsum('bhck,bhkv->bhcv', ww, state)
        o = jnp.einsum('bhck,bhkv->bhcv', qe, state) + jnp.einsum('bhcm,bhmv->bhcv', aqk, v_new)
        state = state * ld[..., None, None] + jnp.einsum('bhck,bhcv->bhkv', kd, v_new)
        return state, o

    b, h = q.shape[0], q.shape[1]
    state0 = jnp.zeros((b, h, q.shape[-1], v.shape[-1]), jnp.float32)
    xs = tuple(jnp.moveaxis(t, 2, 0) for t in (q_exp, w, u, attn, k_dec, last_dec))
    _, o = lax.scan(step, state0, xs)
    return from_chunks(jnp.moveaxis(o, 0, 2)).astype(dtype)

def chunk_retention(q, k, v):
    dtype = v.dtype
    q, k, v = (to_chunks(t.astype(jnp.float32)) for t in (q, k, v))
    h = q.shape[1]
    log_gamma = jnp.log1p(-jnp.exp2(-5.0 - jnp.arange(h, dtype=jnp.float32)))
    pos = jnp.arange(CHUNK, dtype=jnp.float32)
    dist = jnp.abs(pos[:, None] - pos[None, :])
    intra = jnp.exp(log_gamma[:, None, None] * dist)
    scores = jnp.einsum('bhncd,bhnmd->bhncm', q, k) * intra[None, :, None]
    o_intra = jnp.einsum('bhncm,bhnme->bhnce', scores, v)
    q_dec = jnp.exp(log_gamma[:, None] * (pos + 1.0))[None, :, :, None]
    k_dec = jnp.exp(log_gamma[:, None] * (CHUNK - 1.0 - pos))[None, :, :, None]
    chunk_dec = jnp.exp(log_gamma * CHUNK)[None, :, None, None]

    def step(state, inp):
        qc, kc, vc = inp
        o = jnp.einsum('bhcd,bhde->bhce', qc * q_dec, state)
        state = state * chunk_dec + jnp.einsum('bhcd,bhce->bhde', kc * k_dec, vc)
        return state, o

    state0 = jnp.zeros((q.shape[0], h, q.shape[-1], v.shape[-1]), jnp.float32)
    xs = tuple(jnp.moveaxis(t, 2, 0) for t in (q, k, v))
    _, o_inter = lax.scan(step, state0, xs)
    o = o_intra + jnp.moveaxis(o_inter, 0, 2)
    return from_chunks(o).astype(dtype)

def hybrid_layer(x, n_mix_pre, n_mix_post, n_mlp_pre, n_mlp_post, w_in, conv_a, a_log, dt_bias,
                 norm_a, norm_b, w_br_a, w_br_b, w_out, w_up, w_down):
    b, s, _ = x.shape
    xn = rmsnorm_2(x, n_mix_pre)
    proj = xn @ w_in
    qa, ka, va, za, beta_logit, a_dt, qb, kb, vb, gb, gate_a, gate_b = _split_cols(proj, IN_SIZES)

    qkv = jax.nn.silu(causal_depthwise_conv(jnp.concatenate([qa, ka, va], axis=-1), conv_a))
    qa, ka, va = _split_cols(qkv, (A_QK, A_QK, A_V))
    qa = l2norm(qa.reshape(b, s, A_HEADS, A_DK)) * (A_DK ** -0.5)
    ka = l2norm(ka.reshape(b, s, A_HEADS, A_DK))
    va = va.reshape(b, s, A_HEADS, A_DV)
    beta = jax.nn.sigmoid(beta_logit)
    g = -jnp.exp(a_log) * jax.nn.softplus(a_dt + dt_bias)
    oa = chunk_gated_delta_rule(qa, ka, va, beta, g)
    oa = rmsnorm_2(oa, norm_a) * jax.nn.silu(za.reshape(b, s, A_HEADS, A_DV))
    ya = oa.reshape(b, s, A_V) @ w_br_a

    positions = jnp.arange(s)
    qb = rotary(qb.reshape(b, s, B_HEADS, B_DK), positions)
    kb = rotary(kb.reshape(b, s, B_HEADS, B_DK), positions) * (B_DK ** -0.5)
    vb = vb.reshape(b, s, B_HEADS, B_DV)
    ob = chunk_retention(qb, kb, vb)
    ob = rmsnorm_2(ob, norm_b.reshape(B_HEADS, B_DV)) * jax.nn.silu(gb.reshape(b, s, B_HEADS, B_DV))
    yb = ob.reshape(b, s, B_V) @ w_br_b

    mix = (jax.nn.sigmoid(gate_a) * ya + jax.nn.sigmoid(gate_b) * yb) @ w_out
    x = x + rmsnorm_2(mix, n_mix_post)

    hn = rmsnorm_2(x, n_mlp_pre)
    ff = jnp.square(jax.nn.relu(hn @ w_up)) @ w_down
    return x + rmsnorm_2(ff, n_mlp_post)

def second_inputs(seed: int = 0) -> dict:
    key = jax.random.key(seed)
    ks = jax.random.split(key, 16)
    L = DEPTH_2

    def nrm(k, shape, fan_in):
        return jax.random.normal(k, shape, jnp.float32) * fan_in ** -0.5

    def gain(k, shape):
        return 1.0 + 0.05 * jax.random.normal(k, shape, jnp.float32)

    x = jax.random.normal(ks[0], (BATCH, SEQ, D_MODEL), jnp.float32)
    dt = jnp.exp(jax.random.uniform(ks[8], (L, A_HEADS), jnp.float32,
                                    minval=math.log(1e-3), maxval=math.log(1e-1)))
    dt_bias = dt + jnp.log(-jnp.expm1(-dt))
    a_log = jnp.log(jax.random.uniform(ks[9], (L, A_HEADS), jnp.float32, minval=1.0, maxval=16.0))
    return {
        "x": x,
        "norm_mix_pre": gain(ks[1], (L, D_MODEL)),
        "norm_mix_post": gain(ks[2], (L, D_MODEL)),
        "norm_mlp_pre": gain(ks[3], (L, D_MODEL)),
        "norm_mlp_post": gain(ks[4], (L, D_MODEL)),
        "w_in": nrm(ks[5], (L, D_MODEL, D_IN), D_MODEL),
        "conv_a": nrm(ks[6], (L, CONV_W_2, 2 * A_QK + A_V), CONV_W_2),
        "a_log": a_log,
        "dt_bias": dt_bias,
        "norm_a": gain(ks[7], (L, A_DV)),
        "norm_b": gain(ks[10], (L, B_V)),
        "w_br_a": nrm(ks[11], (L, A_V, D_MODEL), A_V),
        "w_br_b": nrm(ks[12], (L, B_V, D_MODEL), B_V),
        "w_out": nrm(ks[13], (L, D_MODEL, D_MODEL), D_MODEL),
        "w_up": nrm(ks[14], (L, D_MODEL, D_FF_2), D_MODEL),
        "w_down": nrm(ks[15], (L, D_FF_2, D_MODEL), D_FF_2),
    }

def second_block(x, norm_mix_pre, norm_mix_post, norm_mlp_pre, norm_mlp_post, w_in, conv_a, a_log,
              dt_bias, norm_a, norm_b, w_br_a, w_br_b, w_out, w_up, w_down):
    for l in range(DEPTH_2):
        x = hybrid_layer(x, norm_mix_pre[l], norm_mix_post[l], norm_mlp_pre[l], norm_mlp_post[l],
                         w_in[l], conv_a[l], a_log[l], dt_bias[l], norm_a[l], norm_b[l],
                         w_br_a[l], w_br_b[l], w_out[l], w_up[l], w_down[l])
    return x


def setup_inputs(seed=0):
    out = dict(first_inputs(seed))
    for name, value in second_inputs(seed + 1).items():
        if name != "x":
            out[name + "_2"] = value
    return out


def reference(
    x, positions, attn_norm, w_qkv_a, w_o_a, kv_norm, w_kv_b, w_q_b, sinks_b, w_o_b, ffn_norm,
    w_up, conv_w, conv_b, w_down, final_norm, norm_mix_pre_2, norm_mix_post_2, norm_mlp_pre_2,
    norm_mlp_post_2, w_in_2, conv_a_2, a_log_2, dt_bias_2, norm_a_2, norm_b_2, w_br_a_2,
    w_br_b_2, w_out_2, w_up_2, w_down_2,
):
    x = first_block(
        x, positions, attn_norm, w_qkv_a, w_o_a, kv_norm, w_kv_b, w_q_b, sinks_b, w_o_b,
        ffn_norm, w_up, conv_w, conv_b, w_down, final_norm,
    )
    return second_block(
        x, norm_mix_pre_2, norm_mix_post_2, norm_mlp_pre_2, norm_mlp_post_2, w_in_2, conv_a_2,
        a_log_2, dt_bias_2, norm_a_2, norm_b_2, w_br_a_2, w_br_b_2, w_out_2, w_up_2, w_down_2,
    )


_drawn_inputs = setup_inputs


def setup_inputs(seed=0):
    import zlib

    import numpy as np

    out = dict(_drawn_inputs(seed))
    spreads = {}
    factors = {'attn_norm': 8.0, 'kv_norm': 8.0, 'sinks_b': 46.691, 'ffn_norm': 2.977, 'conv_b': 5.948}
    for name, (base, spread) in spreads.items():
        noise = np.random.default_rng([zlib.crc32(name.encode()), seed]).standard_normal(out[name].shape)
        drawn = base * np.exp(spread * noise) if base else spread * noise
        out[name] = __import__('jax').numpy.asarray(drawn.astype(out[name].dtype))
    for name, factor in factors.items():
        out[name] = (out[name] * factor).astype(out[name].dtype)
    return out
```

```python
from contextlib import ExitStack, contextmanager

import numpy as np

import concourse.bass as bass
from concourse import mybir

F32 = mybir.dt.float32
F32R = mybir.dt.float32r
I32 = mybir.dt.int32
ALU = mybir.AluOpType
ACT = mybir.ActivationFunctionType
AX = mybir.AxisListType
ENG = mybir.EngineType

P = 128
S = 256
NT = S // P
D = 1024
KD = D // P
EPS = 1e-6
NEG = -1e30
HEADS, HD, KV_HEADS, ROT = 16, 64, 4, 16
GROUPS = 4
GH = HEADS // GROUPS
F_TILES = 2816 // P
F_LAPS = F_TILES // 2
A_HEADS, A_DK, A_DV = 8, 128, 256
B_HEADS, B_DK, B_DV = 4, 256, 512
RET_CHUNK = 64
FF2 = 4096
M_LAPS = FF2 // (4 * P)
UNIT = 2048
SLOTS = 4
RAW = 2
LEAD = 64
LEVELS = 7

C_QA, C_KA, C_VA, C_ZA, C_BA, C_QB, C_KB, C_VB, C_GB, C_GA2, C_GB2 = (
    0, 1024, 2048, 4096, 6144, 6160, 7184, 8208, 10256, 12304, 13328)


def constants():
    r = np.arange(P)
    row, col = r[:, None], r[None, :]
    f = np.float32
    out = {}
    out["ident"] = (row == col).astype(f)
    rot = np.zeros((P, P), f)
    for h in range(0, P, HD):
        for j in range(ROT // 2):
            rot[h + j + ROT // 2, h + j] = -1.0
            rot[h + j, h + j + ROT // 2] = 1.0
    out["rot"] = rot
    freq = np.zeros((P, 1), f)
    inv = np.power(f(500000.0), (-np.arange(0, ROT, 2).astype(f) / f(ROT))).astype(f)
    for h in range(0, P, HD):
        freq[h:h + ROT, 0] = np.concatenate([inv, inv])
    out["freq"] = freq
    causal = np.where(col <= row, 0.0, NEG).astype(f)
    band = np.where(col > row, 0.0, NEG).astype(f)
    out["mask_full"] = np.concatenate([causal, np.zeros((P, P), f), causal], 1)
    out["mask_window"] = np.concatenate([causal, band, causal], 1)
    out["upper"] = (row <= col).astype(f)
    out["lower_strict"] = (row > col).astype(f)
    lev = []
    for b in range(LEVELS):
        w = 1 << b
        lev.append(((row // (2 * w) == col // (2 * w)) & (row // w % 2 == 1) & (col // w % 2 == 0)).astype(f))
    out["levels"] = np.concatenate(lev, 1)
    out["level0_t"] = lev[0].T.copy()
    ret = []
    for h in range(B_HEADS):
        lg = np.log1p(-np.exp2(f(-5.0 - h))).astype(f)
        m, c = np.arange(S)[:, None], np.arange(S)[None, :]
        w = np.exp(lg * np.abs(c - m).astype(f)).astype(f) * (m // RET_CHUNK <= c // RET_CHUNK) * f(B_DK ** -0.5)
        ret.append(np.concatenate([w[0:P, :], w[P:S, P:S]], 1).astype(f))
    out["retain"] = np.concatenate(ret, 1)
    fb = np.power(f(10000.0), (-np.arange(0, B_DK, 2).astype(f) / f(B_DK))).astype(f)
    ang = (np.arange(S).astype(f)[None, :] * fb[:, None]).astype(f)
    out["cos_b"], out["sin_b"] = np.cos(ang).astype(f), np.sin(ang).astype(f)
    return {k: np.ascontiguousarray(v, f) for k, v in out.items()}


def cols_unit(w, *starts_and_widths):
    w = np.concatenate([w[:, a:a + n] for a, n in starts_and_widths], 1)
    return w.reshape(KD, P, -1).transpose(1, 0, 2).reshape(P, -1)


def rows_unit(w, k, kn, n, nn):
    return w[k * P:(k + kn) * P, n:n + nn].reshape(kn, P, nn).transpose(1, 0, 2).reshape(P, -1)


def square_units(w, kt):
    return [rows_unit(w, k, 4, n, 512) for n in range(0, D, 512) for k in range(0, kt, 4)]


def ffn_units(w_up, w_down):
    up = [[cols_unit(w_up, (256 * j, 256)), cols_unit(w_up, (F_TILES * P + 256 * j, 256))] for j in range(F_LAPS)]
    down = [[rows_unit(w_down, 2 * j, 2, 0, D)] for j in range(F_LAPS)]
    out = list(up[0])
    for j in range(1, F_LAPS):
        out += up[j] + down[j - 1]
    return out + down[-1]


def weight_stream(i):
    u = []
    for g in range(GROUPS):
        u += [cols_unit(i["w_qkv_a"][0], (part * D + 256 * g, 256)) for part in range(3)]
    u += square_units(i["w_o_a"][0], KD)
    u += ffn_units(i["w_up"][0], i["w_down"][0])
    for g in range(GROUPS):
        u.append(cols_unit(i["w_q_b"][0], (256 * g, 256)))
        kv = cols_unit(i["w_kv_b"], (HD * g, HD), (HD * g, HD), (KV_HEADS * HD + HD * g, HD))
        u.append(np.concatenate([kv, np.zeros((P, UNIT - kv.shape[1]), np.float32)], 1))
    u += square_units(i["w_o_b"][0], KD)
    u += ffn_units(i["w_up"][1], i["w_down"][1])
    w = i["w_in_2"][0]
    for h in range(A_HEADS):
        u += [cols_unit(w, (C_QA + P * h, P), (C_KA + P * h, P)), cols_unit(w, (C_VA + 256 * h, 256)),
              cols_unit(w, (C_ZA + 256 * h, 256)), cols_unit(w, (C_VB + 256 * h, 256))]
    u += square_units(i["w_br_a_2"][0], 2 * KD)
    u += square_units(w[:, C_GA2:C_GA2 + D], KD)
    for h in range(B_HEADS):
        u += [cols_unit(w, (C_QB + 256 * h, 256)), cols_unit(w, (C_KB + 256 * h, 256)),
              cols_unit(w, (C_GB + 512 * h, 256)), cols_unit(w, (C_GB + 512 * h + 256, 256))]
    u += square_units(i["w_br_b_2"][0], 2 * KD)
    u += square_units(w[:, C_GB2:C_GB2 + D], KD)
    u += square_units(i["w_out_2"][0], KD)
    up = [[cols_unit(i["w_up_2"][0], (512 * j, 256)), cols_unit(i["w_up_2"][0], (512 * j + 256, 256))]
          for j in range(M_LAPS)]
    down = [[rows_unit(i["w_down_2"][0], 4 * j + 2 * a, 2, 0, D) for a in range(2)] for j in range(M_LAPS)]
    u += up[0]
    for j in range(1, M_LAPS):
        u += up[j] + down[j - 1]
    u += down[-1]
    return np.stack(u)


STREAM = [("attn_a", GROUPS, 3), ("wo_a", 1, 4),
          ("ffn_a_first", 1, 2), ("ffn_a", F_LAPS - 1, 3), ("ffn_a_last", 1, 1),
          ("attn_b", GROUPS, 2), ("wo_b", 1, 4),
          ("ffn_b_first", 1, 2), ("ffn_b", F_LAPS - 1, 3), ("ffn_b_last", 1, 1),
          ("delta", A_HEADS, 4), ("br_a", 2, 4), ("gate_a", 1, 4),
          ("retention", B_HEADS, 4), ("br_b", 2, 4), ("gate_b", 1, 4), ("w_out", 1, 4),
          ("mlp_first", 1, 2), ("mlp", M_LAPS - 1, 4), ("mlp_last", 1, 2)]


class Mark:

    def __init__(self, lane, loop, offset):
        self.lane, self.loop, self.offset = lane, loop, offset


class Lane:

    def __init__(self, eng, sem):
        self.eng, self.sem = eng, sem
        self.start = 0
        self.k = 0

    def done(self, ins, name=None):
        ins.then_inc(self.sem, 1)
        self.k += 1
        m = Mark(self, Lane.loop, self.k if Lane.loop else self.start + self.k)
        if Lane.loop and Lane.loop.starts.get(self) is None:
            raise AssertionError
        if name:
            Lane.names[name] = m
            if Lane.loop:
                Lane.loop.seen[name] = (self, self.k)
        return m

    def wait(self, *marks):
        for m in marks:
            if isinstance(m, str):
                m = Lane.names[m]
            if m is None or (m.lane is self and self.eng is Lane.pe_eng):
                continue
            self.eng.wait_ge(m.lane.sem, value_of(m))

    def wait_last_lap(self, *names):
        for n in names:
            if Lane.loop is None:
                if n in Lane.names:
                    self.wait(n)
                continue
            lane, k = Lane.loop.plan_names[n]
            if lane is self and self.eng is Lane.pe_eng:
                continue
            base = Lane.loop.starts[lane] + k - Lane.loop.per[lane]
            self.eng.wait_ge(lane.sem, Lane.loop.i * Lane.loop.per[lane] + base)


def value_of(m):
    if m.loop is None:
        return m.offset
    lp = m.loop
    if lp is Lane.loop:
        return lp.i * lp.per[m.lane] + (lp.starts[m.lane] + m.offset)
    return (lp.n - 1) * lp.per[m.lane] + lp.starts[m.lane] + m.offset


class Loop:
    pass


Lane.loop = None
Lane.names = {}


def program(nc, a, out, plan, stop=None, debug=None):
    new_plan = {}
    with ExitStack() as ctx:
        def sb(name, shape, dt=F32, scope=ctx):
            name = f"sb_{name}"
            return scope.enter_context(nc.sbuf_tensor(name, shape, dt))

        def sem(name):
            return ctx.enter_context(nc.semaphore(name))

        pe, act, dve, pool = (Lane(e, sem(n)) for e, n in (
            (nc.tensor, "pe_done"), (nc.scalar, "act_done"), (nc.vector, "dve_done"), (nc.gpsimd, "pool_done")))
        LANES = (pe, act, dve, pool)
        for ln in LANES:
            ln.eng.sem_inc(ln.sem, LEAD)
            ln.start = LEAD
        Lane.pe_eng = nc.tensor
        Lane.loop, Lane.names = None, {}
        T, A, V, G = nc.tensor, nc.scalar, nc.vector, nc.gpsimd

        @contextmanager
        def laps(tag, n):
            lp = Loop()
            lp.n = n
            known = plan.get(tag, {"per": [1000] * 4, "names": {}})
            lp.per = dict(zip(LANES, known["per"]))
            lp.plan_names = {k: (LANES[x], y) for k, (x, y) in known["names"].items()}
            if not known["names"]:
                lp.plan_names = _Guess(LANES)
            lp.starts = {ln: ln.start + ln.k for ln in LANES}
            lp.seen = {}
            for ln in LANES:
                ln.start, ln.k = ln.start + ln.k, 0
            with nc.Fori(0, n, engines=[ENG.PE, ENG.Activation, ENG.DVE, ENG.Pool]) as i:
                lp.i = i
                Lane.loop = lp
                yield i
            Lane.loop = None
            new_plan[tag] = {"per": [ln.k for ln in LANES],
                             "names": {k: (LANES.index(x), y) for k, (x, y) in lp.seen.items()}}
            for ln in LANES:
                ln.start, ln.k = ln.start + n * ln.k, 0

        raw = sb("raw", [P, RAW, UNIT])
        w_hi = sb("w_hi", [P, SLOTS, UNIT], F32R)
        w_lo = sb("w_lo", [P, SLOTS, UNIT], F32R)
        raw_in = [sem(f"raw_in{r}") for r in range(RAW)]
        hi_done, lo_done = sem("hi_done"), sem("lo_done")
        unit_done = sem("unit_done")

        cut = {"attn_a": 2, "ffn_a": 5, "ffn_b": 10, "w_out": 17}.get(stop, 99)
        stream = STREAM[:cut]
        info, u0, before, uses = {}, 0, 0, [0] * RAW
        for name, n, r in stream:
            info[name] = (u0, n, r, before, list(uses))
            for s in range(r):
                uses[s % RAW] += n
            u0, before = u0 + n * r, r
        n_units = u0

        def raw_value(name, lap, s):
            _, _, r, _, uses = info[name]
            per = len([x for x in range(r) if x % RAW == s % RAW])
            return (lap * per + (uses[s % RAW] + s // RAW + 1)) * 16

        def prev_raw_user(name, lap_is_first, s):
            _, _, r, before, _ = info[name]
            last = [x for x in range(s) if x % RAW == s % RAW]
            if last:
                return s - last[-1]
            span = before if lap_is_first else r
            last = [x for x in range(span) if x % RAW == s % RAW]
            if not last:
                return span + s - 0 if span else 1
            return s + span - last[-1]

        for name, n, r in stream:
            u0, _, _, before, _ = info[name]

            def load(lap, s, first, u0=u0, r=r, name=name):
                back = prev_raw_user(name, first, s)
                if not (first and u0 + s - back < 0):
                    nc.sync.wait_ge(lo_done, lap * r + (u0 + s - back + 1))
                nc.sync.dma_start(raw[:, s % RAW, :], a["stream"][bass.ds(lap * r + (u0 + s), 1)]
                                  .rearrange("u p n -> (u p) n")).then_inc(raw_in[s % RAW], 16)
            for s in range(r):
                load(0, s, True)
            if n > 1:
                with nc.sync.Fori(1, n) as lap:
                    for s in range(r):
                        load(lap, s, False)

        order = [x[0] for x in stream]

        def split(name, lap, s, first):
            u0, _, r, before, _ = info[name]
            back = before if first else r
            if first and s >= before:
                back = before + s
            if not (first and before == 0):
                A.wait_ge(unit_done, lap * r + (u0 + s - back + 1))
            A.wait_ge(raw_in[s % RAW], raw_value(name, lap, s))
            A.copy(w_hi[:, s, :], raw[:, s % RAW, :]).then_inc(hi_done, 1)
            V.wait_ge(hi_done, lap * r + (u0 + s + 1))
            V.tensor_tensor(w_lo[:, s, :], raw[:, s % RAW, :], w_hi[:, s, :].bitcast(F32),
                            ALU.subtract).then_inc(lo_done, 1)

        class Feed:

            def __init__(self, name, lap, last):
                if last:
                    nxt = order.index(name) + 1
                    self.name = order[nxt] if nxt < len(order) else None
                    self.lap, self.first = 0, True
                else:
                    self.name, self.lap, self.first = name, lap + 1, False
                self.r = info[self.name][2] if self.name else 0
                self.s = 0

            def __call__(self, n=1):
                for _ in range(n):
                    if self.s < self.r:
                        split(self.name, self.lap, self.s, self.first)
                        self.s += 1

        def stage(name, body):
            u0, n, r, _, _ = info[name]

            def run(lap, last):
                def arrived(s):
                    T.wait_ge(lo_done, lap * r + (u0 + s + 1))
                feed = Feed(name, lap, last)
                body(lap, feed, arrived)
                feed(SLOTS)
            if n > 2:
                with laps(name, n - 1) as i:
                    run(i, False)
            else:
                for i in range(n - 1):
                    run(i, False)
            run(n - 1, True)

        bank = [ctx.enter_context(nc.psum_tensor(f"bank{b}", [P, 512], F32)) for b in range(8)]
        x = sb("x", [P, NT, D])
        h_hi = sb("h_hi", [P, KD, S], F32R)
        h_lo = sb("h_lo", [P, KD, S], F32R)
        mid_hi = sb("mid_hi", [P, 2 * KD, S], F32R)
        mid_lo = sb("mid_lo", [P, 2 * KD, S], F32R)
        wide = sb("wide", [P, NT, D])
        row = sb("row", [P, D])
        ident = sb("ident", [P, P])
        gains = sb("gains", [P, 7, KD])
        small = sb("small", [P, 64])
        POOL_CONST = {v: j for j, v in enumerate((-0.5, EPS, 1.0, 1.0 / D, 1.0 / A_DV, 1.0 / B_DV))}
        pool_const = sb("pool_const", [P, len(POOL_CONST), 4])
        zero_r = sb("zero_r", [P, 512], F32R)

        boot, row_in, out_done = sem("boot"), sem("row_in"), sem("out_done")
        row_loads = [0]

        A.dma_start(x[:], a["x"].rearrange("(t p) d -> p t d", p=P)).then_inc(boot, 16)
        A.dma_start(ident[:], a["ident"]).then_inc(boot, 16)
        A.dma_start(gains[:], a["gains"].rearrange("p (a k) -> p a k", k=KD)).then_inc(boot, 16)
        for v, j in POOL_CONST.items():
            pool.wait(pool.done(G.memset(pool_const[:, j, :], v)))
        pool.done(G.memset(zero_r[:].bitcast(F32), 0.0), "zero_r")
        for ln in (act, dve, pe):
            ln.eng.wait_ge(boot, 48)

        phase_loads = [0]
        phase_in = sem("phase_in")

        def phase_load(pairs, after=()):
            act.wait(*after)
            for dst, src in pairs:
                A.dma_start(dst, src).then_inc(phase_in, 16)
                phase_loads[0] += 16
            v = phase_loads[0]
            for ln in (act, dve, pe, pool):
                ln.eng.wait_ge(phase_in, v)

        def bcast(ap, shape):
            return ap.to_broadcast(shape)

        def three(out_ap, l_hi, l_lo, r_hi, r_lo, start, stop, **kw):
            T.matmul(out_ap, l_hi, r_hi, start=start, stop=False, **kw)
            T.matmul(out_ap, l_hi, r_lo, start=False, stop=False, **kw)
            return T.matmul(out_ap, l_lo, r_hi, start=False, stop=stop, **kw)

        def used(ins, name=None):
            ins.then_inc(unit_done, 1)

        def feature_major(s, b, tiles, acts, width=256):
            wh = w_hi[:, s, 0:KD * width].rearrange("p (k n) -> p k n", k=KD)
            wl = w_lo[:, s, 0:KD * width].rearrange("p (k n) -> p k n", k=KD)
            for j in range(tiles):
                for k in range(KD):
                    mm = three(bank[b][:, j * S:(j + 1) * S], wh[:, k, j * P:(j + 1) * P],
                               wl[:, k, j * P:(j + 1) * P], acts[0][:, k, :], acts[1][:, k, :], k == 0, k == KD - 1)
            return mm

        def token_major(s, b, acts, c0=0, cols=256, width=256):
            wh = w_hi[:, s, 0:KD * width].rearrange("p (k n) -> p k n", k=KD)
            wl = w_lo[:, s, 0:KD * width].rearrange("p (k n) -> p k n", k=KD)
            for t in range(NT):
                for k in range(KD):
                    o = bank[b][:, t * cols:(t + 1) * cols]
                    tk = slice(t * P, (t + 1) * P)
                    T.matmul(o, acts[0][:, k, tk], wh[:, k, c0:c0 + cols], start=k == 0, stop=False)
                    T.matmul(o, acts[0][:, k, tk], wl[:, k, c0:c0 + cols], start=False, stop=False)
                    mm = T.matmul(o, acts[1][:, k, tk], wh[:, k, c0:c0 + cols], start=False, stop=k == KD - 1)
            return mm

        def last_two(mm, lane_name=None):
            mm.then_inc(unit_done, 1)

        def square_lap(arrived, kt, n0, acts, banks):
            s = 0
            for n in range(n0):
                for kk in range(0, kt, 4):
                    arrived(s)
                    wh = w_hi[:, s, :].rearrange("p (k n) -> p k n", k=4)
                    wl = w_lo[:, s, :].rearrange("p (k n) -> p k n", k=4)
                    for t in range(NT):
                        tk = slice(t * P, (t + 1) * P)
                        for k in range(4):
                            o = bank[banks[n][t]][:, :]
                            first, last = kk + k == 0, kk + k == kt - 1
                            T.matmul(o, acts[0][:, kk + k, tk], wh[:, k, :], start=first, stop=False)
                            T.matmul(o, acts[0][:, kk + k, tk], wl[:, k, :], start=False, stop=False)
                            mm = T.matmul(o, acts[1][:, kk + k, tk], wh[:, k, :], start=False, stop=last)
                    mm.then_inc(unit_done, 1)
                    s += 1

        def unit_mark(name_of_stage, lap, s):
            u0, _, r, _, _ = info[name_of_stage]
            return lap * r + (u0 + s + 1)

        def rsqrt_col(dst, src, n, scale):
            d = small[:, dst:dst + n]
            m = pool.done(G.tensor_tensor(d, small[:, src:src + n], pool_const[:, POOL_CONST[scale], 0:n], ALU.mult))
            pool.wait(m)
            m = pool.done(G.tensor_tensor(d, d, pool_const[:, POOL_CONST[EPS], 0:n], ALU.add))
            pool.wait(m)
            return pool.done(G.tensor_tensor(d, d, pool_const[:, POOL_CONST[-0.5], 0:n], ALU.pow))

        TR = [4, 5, 6, 7]

        def normed(src, x_marks, targets, free):
            act.wait(*x_marks)
            act.wait(*free)
            for t in range(NT):
                m = act.done(A.activation(wide[:, t, :], src[:, t, :], ACT.Square, accum_out=small[:, t:t + 1]))
            pool.wait(m)
            m = rsqrt_col(2, 0, NT, 1.0 / D)
            dve.wait(m)
            for t in range(NT):
                m = dve.done(V.tensor_scalar(wide[:, t, :], src[:, t, :], small[:, 2 + t:3 + t], None, ALU.mult))
            pe.wait(m)
            pe.wait(*free)
            for b in range(4):
                for k in range(2 * b, 2 * b + 2):
                    for t in range(NT):
                        c = (k % 2) * S + t * P
                        mm = T.transpose(bank[TR[b]][:, c:c + P], wide[:, t, k * P:(k + 1) * P], ident[:])
                m = pe.done(mm)
                act.wait(m)
                for k in range(2 * b, 2 * b + 2):
                    for g, hi, lo in targets:
                        h = act.done(A.activation(hi[:, k, :], bank[TR[b]][:, (k % 2) * S:(k % 2 + 1) * S], ACT.Copy,
                                                  scale=gains[:, g, k:k + 1]))
                dve.wait(h)
                for k in range(2 * b, 2 * b + 2):
                    for g, hi, lo in targets:
                        m = dve.done(V.scalar_tensor_tensor(
                            lo[:, k, :], bank[TR[b]][:, (k % 2) * S:(k % 2 + 1) * S], gains[:, g, k:k + 1],
                            hi[:, k, :].bitcast(F32), ALU.mult, ALU.subtract))
            Lane.names["normed"] = m
            pe.wait(m)

        def add_residual(banks, ready, names):
            for n in range(2):
                for t in range(NT):
                    dve.eng.wait_ge(*ready(n))
                    m = dve.done(V.tensor_tensor(x[:, t, n * 512:(n + 1) * 512], bank[banks[n][t]][:, :],
                                                 x[:, t, n * 512:(n + 1) * 512], ALU.add))
            Lane.names["x"] = m
            return m

        def done_or_dump(name, src=None):
            return stop == name

        feed0 = Feed("attn_a", -1, False)
        feed0.name, feed0.lap, feed0.first, feed0.r = "attn_a", 0, True, info["attn_a"][2]
        feed0(SLOTS)

        b1 = ExitStack()
        ctx.enter_context(b1)
        cos_t, sin_t = sb("cos_t", [P, S], scope=b1), sb("sin_t", [P, S], scope=b1)
        rot = sb("rot", [P, P], scope=b1)
        freq = sb("freq", [P, 1], scope=b1)
        pos_i, pos_f = sb("pos_i", [P, S], I32, scope=b1), sb("pos_f", [P, S], scope=b1)
        turns = sb("turns", [P, S], scope=b1)
        masks = sb("masks", [P, 2, 384], scope=b1)
        sinks = sb("sinks", [P, HEADS], scope=b1)
        conv = sb("conv", [P, 2, F_LAPS, 4, 4], scope=b1)
        phase_load([(rot[:], a["rot"]), (freq[:], a["freq"]),
                    (pos_i[:], a["positions"].partition_broadcast(P).rearrange("p a n -> p (a n)")),
                    (masks[:, 0, :], a["mask_full"]), (masks[:, 1, :], a["mask_window"]),
                    (sinks[:], a["sinks"].partition_broadcast(P).rearrange("p a n -> p (a n)")),
                    (conv[:].rearrange("p a b c d -> p (a b c d)"), a["conv"])])

        two_pi = 6.283185307179586
        c1 = float(np.float32(int(two_pi * 128) / 128))
        c2 = float(np.float32(int((two_pi - c1) * 2 ** 20) / 2 ** 20))
        c3 = float(np.float32(two_pi - c1 - c2))
        magic = 1.5 * 2 ** 23

        def chain(ins):
            m = dve.done(ins)
            dve.wait(m)
            return m
        chain(V.tensor_copy(pos_f[:], pos_i[:]))
        chain(V.tensor_scalar(pos_f[:], pos_f[:], freq[:, 0:1], None, ALU.mult))
        for tab, shift in ((sin_t, 0.0), (cos_t, 0.25)):
            chain(V.tensor_scalar(turns[:], pos_f[:], 1.0 / two_pi, shift, ALU.mult, ALU.add))
            chain(V.tensor_scalar(turns[:], turns[:], magic, None, ALU.add))
            chain(V.tensor_scalar(turns[:], turns[:], magic, None, ALU.subtract))
            chain(V.scalar_tensor_tensor(tab[:], turns[:], -c1, pos_f[:], ALU.mult, ALU.add))
            chain(V.scalar_tensor_tensor(tab[:], turns[:], -c2, tab[:], ALU.mult, ALU.add))
            chain(V.scalar_tensor_tensor(tab[:], turns[:], -c3, tab[:], ALU.mult, ALU.add))
            if shift:
                chain(V.tensor_scalar(tab[:], tab[:], two_pi / 4, None, ALU.add))
            chain(V.tensor_scalar(tab[:], tab[:], float(np.float32(np.pi) - np.float32(3e-7)),
                                  -float(np.float32(np.pi) - np.float32(3e-7)), ALU.min, ALU.max))
            act.wait(Mark(dve, None, dve.start + dve.k))
            m = act.done(A.activation(tab[:], tab[:], ACT.Sin), "tables")
        dve.wait("tables")

        def attention_stage(name, layer, mask_row, grouped):
            scope = ExitStack()
            qk_raw = sb(f"{name}_qk_raw", [P, 2, 512], scope=scope)
            qk_cos = sb(f"{name}_qk_cos", [P, 2, 512], scope=scope)
            qk = sb(f"{name}_qk", [P, 2, 512], scope=scope)
            v = sb(f"{name}_v", [P, NT, 256], scope=scope)
            sc = sb(f"{name}_sc", [P, 2, 384], scope=scope)
            pt = sb(f"{name}_pt", [P, 2, 384], scope=scope)
            kw = 1 if grouped else 2
            kv_acts = (mid_hi[:, KD:2 * KD], mid_lo[:, KD:2 * KD]) if grouped else (h_hi, h_lo)

            def body(g, feed, arrived):
                if grouped:
                    arrived(0)
                    pe.wait_last_lap("rot0")
                    m = feature_major(0, 0, 2, (h_hi, h_lo))
                    m.then_inc(unit_done, 1)
                    arrived(1)
                    pe.wait_last_lap("rot1", "v_copy")
                    feature_major(1, 1, 1, kv_acts, width=192)
                    token_major(1, 2, kv_acts, c0=128, cols=64, width=192).then_inc(unit_done, 1)
                    ready = {0: (unit_done, unit_mark(name, g, 0)), 1: (unit_done, unit_mark(name, g, 1)),
                             2: (unit_done, unit_mark(name, g, 1))}
                else:
                    for s, (free, b) in enumerate((("rot0", 0), ("rot1", 1), ("v_copy", 2))):
                        arrived(s)
                        pe.wait_last_lap(free)
                        if s < 2:
                            mm = feature_major(s, b, 2, (h_hi, h_lo))
                        else:
                            mm = token_major(s, b, (h_hi, h_lo))
                        mm.then_inc(unit_done, 1)
                    ready = {b: (unit_done, unit_mark(name, g, b)) for b in range(3)}
                for j, tiles in ((0, 2), (1, kw)):
                    w = tiles * S
                    A.wait_ge(*ready[j])
                    act.wait_last_lap(f"rotmm{j}")
                    r = act.done(A.copy(qk_raw[:, j, 0:w], bank[j][:, 0:w]))
                    dve.wait(r)
                    dve.wait_last_lap(f"rot{j}")
                    c = dve.done(V.tensor_tensor(
                        qk_cos[:, j, 0:w].rearrange("p (a n) -> p a n", n=S),
                        bank[j][:, 0:w].rearrange("p (a n) -> p a n", n=S),
                        bcast(cos_t[:].unsqueeze(1), [P, tiles, S]), ALU.mult))
                    pe.wait(r)
                    if j == 0:
                        pe.wait_last_lap("rot1")
                    else:
                        pe.wait("rotsin0")
                    mm = pe.done(T.matmul(bank[3][:, 0:w], rot[:], qk_raw[:, j, 0:w], start=True, stop=True), f"rotmm{j}")
                    dve.wait(mm)
                    dve.wait_last_lap("scores_done")
                    m = dve.done(V.tensor_tensor(
                        qk[:, j, 0:w].rearrange("p (a n) -> p a n", n=S),
                        bank[3][:, 0:w].rearrange("p (a n) -> p a n", n=S),
                        bcast(sin_t[:].unsqueeze(1), [P, tiles, S]), ALU.mult), f"rotsin{j}")
                    dve.wait(m, c)
                    dve.done(V.tensor_tensor(qk[:, j, 0:w], qk[:, j, 0:w], qk_cos[:, j, 0:w], ALU.add), f"rot{j}")
                    feed()
                A.wait_ge(*ready[2])
                act.wait_last_lap("pv_done")
                vw = NT * 64 if grouped else NT * 256
                act.done(A.copy(v[:].rearrange("p a n -> p (a n)")[:, 0:vw], bank[2][:, 0:vw]), "v_copy")
                vt = v[:].rearrange("p a n -> p (a n)")[:, 0:vw].rearrange("p (a n) -> p a n", a=NT)
                feed(SLOTS)

                def scores(r):
                    rows = slice(64 * (r % 2), 64 * (r % 2) + 64)
                    q0 = (r // 2) * S
                    k0 = 0 if grouped else q0
                    pe.wait("rot0", "rot1")
                    b = bank[4 + r % 2]
                    if r >= 2:
                        pe.wait(f"masked{r - 2}")
                    else:
                        pe.wait_last_lap(f"masked{r + 2}")
                    T.matmul(b[:, 0:P], qk[rows, 0, q0:q0 + P], qk[rows, 1, k0:k0 + P], start=True, stop=True)
                    mm = pe.done(T.matmul(b[:, P:384], qk[rows, 0, q0 + P:q0 + S], qk[rows, 1, k0:k0 + S],
                                          start=True, stop=True), "scores_done")
                    y = sc[:, r % 2, :]
                    dve.wait(mm)
                    if r >= 2:
                        dve.wait(f"turned{r - 2}")
                    else:
                        dve.wait_last_lap(f"turned{r + 2}")
                    m = dve.done(V.scalar_tensor_tensor(y, b[:, 0:384], HD ** -0.5, masks[:, mask_row, :],
                                                        ALU.mult, ALU.add), f"masked{r}")
                    dve.wait(m)
                    c0 = 8 + 8 * (r % 2)
                    dve.done(V.reduce_max(small[:, c0:c0 + 1], y[:, 0:P], AX.X))
                    m = dve.done(V.reduce_max(small[:, c0 + 1:c0 + 2], y[:, P:384], AX.X))
                    dve.wait(m)
                    neg = small[:, c0 + 2:c0 + 4]
                    if grouped:
                        sink = sinks[:, bass.ds(g * GH + r, 1)]
                        m = dve.done(V.tensor_scalar(neg, small[:, c0:c0 + 2], sink, -1.0, ALU.max, ALU.mult))
                    else:
                        m = dve.done(V.tensor_scalar(neg, small[:, c0:c0 + 2], -1.0, None, ALU.mult))
                    act.wait(m)
                    act.done(A.activation(y[:, 0:P], y[:, 0:P], ACT.Exp, bias=small[:, c0 + 2:c0 + 3],
                                          accum_out=small[:, c0 + 4:c0 + 5]))
                    m = act.done(A.activation(y[:, P:384], y[:, P:384], ACT.Exp, bias=small[:, c0 + 3:c0 + 4],
                                              accum_out=small[:, c0 + 5:c0 + 6]))
                    if grouped:
                        m = act.done(A.activation(small[:, c0 + 6:c0 + 8], neg, ACT.Exp, bias=sink))
                        dve.wait(m)
                        m = dve.done(V.tensor_tensor(small[:, c0 + 4:c0 + 6], small[:, c0 + 4:c0 + 6],
                                                     small[:, c0 + 6:c0 + 8], ALU.add))
                    dve.wait(m)
                    m = dve.done(V.reciprocal(small[:, c0 + 4:c0 + 6], small[:, c0 + 4:c0 + 6]))
                    dve.wait(m)
                    dve.done(V.tensor_scalar(y[:, 0:P], y[:, 0:P], small[:, c0 + 4:c0 + 5], None, ALU.mult))
                    dve.done(V.tensor_scalar(y[:, P:384], y[:, P:384], small[:, c0 + 5:c0 + 6], None, ALU.mult),
                             f"probs{r}")

                def values(r):
                    y, z = sc[:, r % 2, :], pt[:, r % 2, :]
                    pe.wait(f"probs{r}")
                    if r:
                        pe.wait(f"pt{r - 1}")
                    else:
                        pe.wait_last_lap(f"pt{GH - 1}")
                    for c in range(3):
                        mm = T.transpose(bank[6][:, c * P:(c + 1) * P], y[:, c * P:(c + 1) * P], ident[:])
                    mm = pe.done(mm, f"turned{r}")
                    act.wait(mm)
                    if r >= 2:
                        act.wait(f"pv{r - 2}")
                    else:
                        act.wait_last_lap(f"pv{r + 2}")
                    act.done(A.copy(z, bank[6][:, 0:384]), f"pt{r}")
                    pe.wait(f"pt{r}", "v_copy")
                    if r == 0:
                        pe.wait_last_lap("out_lo")
                    d0 = 64 * (r % 2)
                    c0 = 0 if grouped else 64 * r
                    o = bank[7][d0:d0 + 64, (r // 2) * S:(r // 2 + 1) * S]
                    T.matmul(o, vt[:, 0, c0:c0 + 64], z[:, 0:S], start=True, stop=False, skip_group_check=True)
                    mm = T.matmul(o[:, P:S], vt[:, 1, c0:c0 + 64], z[:, S:384], start=False, stop=True,
                                  skip_group_check=True)
                    pe.done(mm, f"pv{r}")
                    if r == GH - 1:
                        Lane.names["pv_done"] = Lane.names[f"pv{r}"]
                        if Lane.loop:
                            Lane.loop.seen["pv_done"] = (pe, pe.k)

                scores(0)
                for r in range(GH):
                    if r + 1 < GH:
                        scores(r + 1)
                    values(r)
                o3 = bank[7][:, :].rearrange("p (a n) -> p a n", n=S)
                act.wait(f"pv{GH - 1}")
                hi = mid_hi[:, bass.ds(g * 2, 2), :]
                m = act.done(A.copy(hi, o3), "out_hi")
                dve.wait(m)
                dve.done(V.tensor_tensor(mid_lo[:, bass.ds(g * 2, 2), :], o3, hi.bitcast(F32), ALU.subtract), "out_lo")
            stage(name, body)
            scope.close()

        def project_out(name, src_mark):
            banks = [(0, 1), (2, 3)]

            def body(lap, feed, arrived):
                pe.wait(*src_mark)
                square_lap(arrived, KD, 2, (mid_hi, mid_lo), banks)
                feed(2)
                add_residual(banks, lambda n: (unit_done, unit_mark(name, lap, 2 * n + 1)), None)
            stage(name, body)

        def ffn(tag, layer):
            scope = ExitStack()
            cv = sb(f"{tag}_cv", [P, 4, S], scope=scope)
            sg = sb(f"{tag}_sg", [P, 2, S], scope=scope)
            gt_hi = sb(f"{tag}_gt_hi", [P, 2, S], F32R, scope=scope)
            gt_lo = sb(f"{tag}_gt_lo", [P, 2, S], F32R, scope=scope)
            acc = [(4, 5), (6, 7)]

            def up(j, jc, arrived, st):
                for s in range(2):
                    arrived(s)
                    pe.wait_last_lap(f"conv{s}")
                    feature_major(s, s, 2, (h_hi, h_lo)).then_inc(unit_done, 1)

            def post(j, jc, st, feed):
                cw = conv[:, layer, bass.ds(jc, 1), :, :].rearrange("p a b c -> p (a b) c")
                for s in range(2):
                    A.wait_ge(unit_done, unit_mark(st, j, s))
                    act.wait_last_lap(f"sg", "gprod")
                    for i in range(2):
                        y = 2 * s + i
                        c = act.done(A.activation(cv[:, y, :], bank[s][:, i * S:(i + 1) * S], ACT.Identity,
                                                  scale=cw[:, y, 2:3], bias=cw[:, y, 3:4]))
                    dve.wait(c)
                    for back in (1, 2):
                        for i in range(2):
                            y = 2 * s + i
                            m = dve.done(V.scalar_tensor_tensor(
                                cv[:, y, back:S], bank[s][:, i * S:(i + 1) * S - back], cw[:, y, 2 - back:3 - back],
                                cv[:, y, back:S], ALU.mult, ALU.add), f"conv{s}")
                        dve.wait(m)
                    if s == 0:
                        act.wait(m)
                        act.done(A.activation(sg[:], cv[:, 0:2, :], ACT.Silu), "sg")
                    feed()
                dve.wait("sg", m)
                m = dve.done(V.tensor_tensor(sg[:], sg[:], cv[:, 2:4, :], ALU.mult), "gprod")

            def split_g(feed):
                act.wait("gprod")
                A.wait_ge(unit_done, Lane.down_value)
                m = act.done(A.copy(gt_hi[:], sg[:]), "gt_hi")
                dve.wait(m)
                dve.done(V.tensor_tensor(gt_lo[:], sg[:], gt_hi[:].bitcast(F32), ALU.subtract), "gt")

            def down(s, arrived):
                arrived(s)
                wh = w_hi[:, s, :].rearrange("p (k n) -> p k n", k=2)
                wl = w_lo[:, s, :].rearrange("p (k n) -> p k n", k=2)
                for k in range(2):
                    for t in range(NT):
                        tk = slice(t * P, (t + 1) * P)
                        for n in range(2):
                            nn = slice(n * 512, (n + 1) * 512)
                            o = bank[acc[t][n]][:, :]
                            T.matmul(o, gt_hi[:, k, tk], wh[:, k, nn], start=False, stop=False, skip_group_check=True)
                            T.matmul(o, gt_hi[:, k, tk], wl[:, k, nn], start=False, stop=False, skip_group_check=True)
                            mm = T.matmul(o, gt_lo[:, k, tk], wh[:, k, nn], start=False, stop=True, skip_group_check=True)
                mm.then_inc(unit_done, 1)

            def first(j, feed, arrived):
                up(j, 0, arrived, f"{tag}_first")
                pe.wait("normed", "zero_r")
                for t in range(NT):
                    for n in range(2):
                        T.matmul(bank[acc[t][n]][:, :], zero_r[:, 0:P], zero_r[:], start=True, stop=True,
                                 skip_group_check=True)
                post(j, 0, f"{tag}_first", feed)
                Lane.down_value = 0
                split_g(feed)
            stage(f"{tag}_first", first)
            pe.wait("conv0", "conv1")
            act.wait("sg", "gprod")

            def middle(j, feed, arrived):
                up(j, j + 1, arrived, tag)
                pe.wait_last_lap("gt")
                down(2, arrived)
                post(j, j + 1, tag, feed)
                feed()
                Lane.down_value = unit_mark(tag, j, 2)
                split_g(feed)
            pe.wait("gt")
            stage(tag, middle)

            def last(j, feed, arrived):
                pe.wait("gt")
                down(0, arrived)
                feed()
                add_residual([(4, 6), (5, 7)], lambda n: (unit_done, unit_mark(f"{tag}_last", j, 0)), None)
            stage(f"{tag}_last", last)
            scope.close()

        def finish(src):
            act.wait(*[Mark(ln, None, ln.start + ln.k) for ln in (act, dve, pool)])
            A.dma_start(out.rearrange("(t p) d -> p t d", p=P), src).then_inc(out_done, 16)
            A.wait_ge(out_done, 16)

        normed(x, (), [(0, h_hi, h_lo)], ())
        attention_stage("attn_a", 0, 0, False)
        project_out("wo_a", ("out_lo",))
        if stop == "attn_a":
            finish(x[:])
            return new_plan
        act.wait("x")
        normed(x, ("x",), [(1, h_hi, h_lo)], ("x", "out_lo"))
        ffn("ffn_a", 0)
        if stop == "ffn_a":
            finish(x[:])
            return new_plan
        normed(x, ("x",), [(2, mid_hi[:, KD:2 * KD], mid_lo[:, KD:2 * KD]), (3, h_hi, h_lo)], ("x",))
        attention_stage("attn_b", 1, 1, True)
        project_out("wo_b", ("out_lo",))
        normed(x, ("x",), [(4, h_hi, h_lo)], ("x", "out_lo"))
        ffn("ffn_b", 1)
        def statistics(src, marks, junk):
            act.wait(*marks)
            for t in range(NT):
                m = act.done(A.activation(junk[:, t, :], src[:, t, :], ACT.Square, accum_out=small[:, t:t + 1]))
            pool.wait(m)
            return rsqrt_col(2, 0, NT, 1.0 / D)

        phase_load([(row[:], a["rows"][0:1, :].partition_broadcast(P).rearrange("p a n -> p (a n)"))])
        m = statistics(x, ("x",), wide)
        dve.wait(m)
        for t in range(NT):
            dve.done(V.scalar_tensor_tensor(x[:, t, :], x[:, t, :], small[:, 2 + t:3 + t], row[:], ALU.mult, ALU.mult), "x")
        if stop == "ffn_b":
            finish(x[:])
            return new_plan
        b1.close()

        everything = lambda: [Mark(ln, None, ln.start + ln.k) for ln in LANES]
        for ln in (act, dve, pool):
            ln.wait(*everything())
        normed(x, ("x",), [(5, h_hi, h_lo)], ("x",))
        b2 = ExitStack()
        ctx.enter_context(b2)
        v_ret = sb("v_ret", [P, NT, B_HEADS * B_DV], scope=b2)
        b3 = ExitStack()
        ctx.enter_context(b3)
        upper, lower = sb("upper", [P, P], scope=b3), sb("lower", [P, P], scope=b3)
        levels = sb("levels", [P, LEVELS, P], scope=b3)
        level0_t = sb("level0_t", [P, P], scope=b3)
        norm_a = sb("norm_a", [P, A_DV], scope=b3)
        conv_a = sb("conv_a", [P, A_HEADS, 4, 4], scope=b3)
        w_ba = sb("w_ba", [P, KD, 2 * A_HEADS], scope=b3)
        ba_hi, ba_lo = sb("ba_hi", [P, KD, 16], F32R, scope=b3), sb("ba_lo", [P, KD, 16], F32R, scope=b3)
        log_bias = sb("log_bias", [P, 2, A_HEADS], scope=b3)
        gate = sb("gate", [P, 6, NT, A_HEADS], scope=b3)
        phase_load([(upper[:], a["upper"]), (lower[:], a["lower_strict"]),
                    (levels[:].rearrange("p a n -> p (a n)"), a["levels"]), (level0_t[:], a["level0_t"]),
                    (norm_a[:], a["norm_a"].partition_broadcast(P).rearrange("p a n -> p (a n)")),
                    (conv_a[:].rearrange("p a b c -> p (a b c)"), a["conv_a"]),
                    (w_ba[:].rearrange("p a b -> p (a b)"), a["w_ba"]),
                    (log_bias[:, 0, :], a["a_log"].partition_broadcast(P).rearrange("p a n -> p (a n)")),
                    (log_bias[:, 1, :], a["dt_bias"].partition_broadcast(P).rearrange("p a n -> p (a n)"))])

        beta, g_log, g_cum, e_cum, t1, t2 = (gate[:, j] for j in range(6))
        chain(V.tensor_copy(ba_hi[:], w_ba[:]))
        m = chain(V.tensor_tensor(ba_lo[:], w_ba[:], ba_hi[:].bitcast(F32), ALU.subtract))
        pe.wait(m, "normed")
        ba = bank[4][:, 0:NT * 16].rearrange("p (t n) -> p t n", t=NT)
        for t in range(NT):
            tk = slice(t * P, (t + 1) * P)
            for k in range(KD):
                mm = three(ba[:, t, :], h_hi[:, k, tk], h_lo[:, k, tk], ba_hi[:, k, :], ba_lo[:, k, :],
                           k == 0, k == KD - 1)
        m = pe.done(mm)
        act.wait(m)
        m = act.done(A.activation(beta, ba[:, :, 0:A_HEADS], ACT.Exp, scale=-1.0))
        dve.wait(m)
        chain(V.tensor_scalar(beta, beta, 1.0, None, ALU.add))
        chain(V.reciprocal(beta, beta))
        chain(V.tensor_tensor(g_log, ba[:, :, A_HEADS:], bcast(log_bias[:, 1:2, :], [P, NT, A_HEADS]), ALU.add))
        m = chain(V.scalar_tensor_tensor(t1, g_log, -1.0, g_log, ALU.mult, ALU.max))
        act.wait(m)
        m = act.done(A.activation(t1, t1, ACT.Exp, scale=-1.0))
        act.wait(m)
        m = act.done(A.activation(t1, t1, ACT.Ln, bias=1.0))
        m = act.done(A.activation(log_bias[:, 0, :], log_bias[:, 0, :], ACT.Exp))
        dve.wait(m)
        chain(V.scalar_tensor_tensor(g_log, g_log, 0.0, t1, ALU.max, ALU.add))
        m = chain(V.scalar_tensor_tensor(g_log, g_log, -1.0, bcast(log_bias[:, 0:1, :], [P, NT, A_HEADS]),
                                         ALU.mult, ALU.mult))
        pe.wait(m)
        gsum = bank[5][:, 0:NT * A_HEADS].rearrange("p (t n) -> p t n", t=NT)
        for t in range(NT):
            mm = T.matmul(gsum[:, t, :], upper[:], g_log[:, t, :], start=True, stop=True)
        m = pe.done(mm)
        act.wait(m)
        m = act.done(A.activation(e_cum, gsum, ACT.Exp))
        m = act.done(A.copy(g_cum, gsum), "gates")
        for ln in (dve, pe):
            ln.wait("gates")

        scope = ExitStack()
        cv = sb("d_conv", [P, 4, S], scope=scope)
        zs = sb("d_z", [P, NT, A_DV], scope=scope)
        qkn = sb("d_qkn", [P, 4, P], scope=scope)
        qkt = sb("d_qkt", [P, 4, P], scope=scope)
        gb = sb("d_gb", [P, NT, P], scope=scope)
        up_dec, lo_dec = sb("d_up_dec", [P, NT, P], scope=scope), sb("d_lo_dec", [P, NT, P], scope=scope)
        e_row = sb("d_e_row", [P, P], scope=scope)
        low = sb("d_low", [P, NT, P], scope=scope)
        low_b = sb("d_low_b", [P, 2, NT, P], scope=scope)
        att = sb("d_att", [P, NT, P], scope=scope)
        xt = sb("d_xt", [P, 4, P], scope=scope)
        z = sb("d_zm", [P, NT, P], scope=scope)
        vbeta = sb("d_vbeta", [P, NT, A_DV], scope=scope)
        kb, kdec, qexp, nwt = (sb(n, [P, P], scope=scope) for n in ("d_kb", "d_kdec", "d_qexp", "d_nwt"))
        vn = sb("d_vn", [P, NT, A_DV], scope=scope)
        state = sb("d_state", [P, A_DV], scope=scope)
        o = sb("d_o", [P, NT, A_DV], scope=scope)

        def last(*names):
            for ln in (pe, act, dve, pool):
                ln.wait_last_lap(*names)

        def delta(hd, feed, arrived):
            for s, free in enumerate(("conv0", "conv1", "zs", "v_ret")):
                arrived(s)
                pe.wait_last_lap(free)
                if s < 2:
                    mm = feature_major(s, s, 2, (h_hi, h_lo))
                else:
                    mm = token_major(s, s, (h_hi, h_lo))
                mm.then_inc(unit_done, 1)
            ready = lambda s: (unit_done, unit_mark("delta", hd, s))
            cw = conv_a[:, bass.ds(hd, 1), :, :].rearrange("p a b c -> p (a b) c")
            act.wait_last_lap("flipped", "v_turned")
            for s in range(2):
                A.wait_ge(*ready(s))
                for i in range(2):
                    y = 2 * s + i
                    c = act.done(A.activation(cv[:, y, :], bank[s][:, i * S:(i + 1) * S], ACT.Copy, scale=cw[:, y, 3:4]))
                dve.wait(c)
                for back in (1, 2, 3):
                    for i in range(2):
                        y = 2 * s + i
                        m = dve.done(V.scalar_tensor_tensor(
                            cv[:, y, back:S], bank[s][:, i * S:(i + 1) * S - back], cw[:, y, 3 - back:4 - back],
                            cv[:, y, back:S], ALU.mult, ALU.add), f"conv{s}")
                    dve.wait(m)
                feed()
            act.wait("conv0", "conv1")
            act.done(A.activation(cv[:], cv[:], ACT.Silu), "silu")
            A.wait_ge(*ready(2))
            act.wait_last_lap("gated")
            act.done(A.activation(zs[:].rearrange("p a n -> p (a n)"), bank[2][:, :], ACT.Silu), "zs")
            A.wait_ge(*ready(3))
            act.done(A.copy(v_ret[:, :, bass.ds(hd * 256, 256)], bank[3][:, :].rearrange("p (t n) -> p t n", t=NT)), "v_ret")
            feed(2)
            pe.wait("silu")
            pe.wait_last_lap("mid_lo", "o")
            for j in range(4):
                mm = T.transpose(bank[4][:, j * P:(j + 1) * P], cv[:, j // 2, (j % 2) * P:(j % 2 + 1) * P], ident[:])
            pe.done(mm, "flipped")
            for t in range(NT):
                for f in range(2):
                    mm = T.transpose(bank[5][:, t * A_DV + f * P:t * A_DV + (f + 1) * P],
                                     cv[:, 2 + f, t * P:(t + 1) * P], ident[:])
            pe.done(mm, "v_turned")
            act.wait("flipped")
            act.wait_last_lap("o")
            for j in range(4):
                m = act.done(A.activation(o[:, j // 2, (j % 2) * P:(j % 2 + 1) * P], bank[4][:, j * P:(j + 1) * P], ACT.Square,
                                          accum_out=small[:, 32 + j:33 + j]))
            pool.wait(m)
            m = rsqrt_col(36, 32, 4, 1.0)
            dve.wait(m)
            dve.wait_last_lap("qkt_read")
            for j in range(4):
                m = dve.done(V.tensor_scalar(qkn[:, j, :], bank[4][:, j * P:(j + 1) * P], small[:, 36 + j:37 + j],
                                             A_DK ** -0.5 if j < 2 else 1.0, ALU.mult, ALU.mult), "qkn")
            pe.wait("qkn")
            for j in range(4):
                mm = T.transpose(bank[6][:, j * P:(j + 1) * P], qkn[:, j, :], ident[:])
            m = pe.done(mm)
            act.wait(m)
            act.done(A.copy(qkt[:].rearrange("p a n -> p (a n)"), bank[6][:, :]), "qkt")
            m = dve.done(V.tensor_copy(gb[:], bcast(g_log[:, :, bass.ds(hd, 1)], [P, NT, P])))
            pe.wait(m)
            for t in range(NT):
                mm = T.matmul(bank[7][:, t * P:(t + 1) * P], gb[:, t, :], upper[:], start=True, stop=True)
            m = pe.done(mm)
            dve.wait(m)
            for t in range(NT):
                gc = g_cum[:, t, bass.ds(hd, 1)]
                gr = bank[7][:, t * P:(t + 1) * P]
                dve.done(V.tensor_scalar(up_dec[:, t, :], gr, gc, 0.0, ALU.subtract, ALU.min))
                dve.done(V.tensor_scalar(lo_dec[:, t, :], gr, gc, 0.0, ALU.subtract, ALU.max))
            m = dve.done(V.tensor_scalar(small[:, 44:45], bank[7][:, P - 1:P], g_cum[:, 0, bass.ds(hd, 1)], None, ALU.subtract))
            act.wait(m)
            act.done(A.activation(e_row[:], bank[7][:, P:S], ACT.Exp), "e_row")
            act.done(A.activation(small[:, 44:45], small[:, 44:45], ACT.Exp), "e_last")
            act.done(A.activation(up_dec[:], up_dec[:], ACT.Exp))
            m = act.done(A.activation(lo_dec[:], lo_dec[:], ACT.Exp, scale=-1.0))
            pool.wait(m)
            pool.done(G.tensor_tensor(lo_dec[:], lo_dec[:], bcast(lower[:].unsqueeze(1), [P, NT, P]), ALU.mult), "lo_dec")
            pool.done(G.tensor_tensor(up_dec[:], up_dec[:], bcast(upper[:].unsqueeze(1), [P, NT, P]), ALU.mult), "up_dec")
            pe.wait("qkt", "qkn")
            for t in range(NT):
                T.matmul(bank[4][:, t * P:(t + 1) * P], qkt[:, 2 + t, :], qkt[:, 2 + t, :], start=True, stop=True)
            for t in range(NT):
                mm = T.matmul(bank[4][:, (2 + t) * P:(3 + t) * P], qkt[:, 2 + t, :], qkt[:, t, :], start=True, stop=True)
            m = pe.done(mm)
            dve.wait(m, "lo_dec")
            for t in range(NT):
                m = dve.done(V.scalar_tensor_tensor(low[:, t, :], bank[4][:, t * P:(t + 1) * P],
                                                    beta[:, t, bass.ds(hd, 1)], lo_dec[:, t, :], ALU.mult, ALU.mult), "low")
            dve.wait("up_dec")
            dve.done(V.tensor_tensor(att[:], bank[4][:, 2 * P:4 * P].rearrange("p (a n) -> p a n", a=NT), up_dec[:],
                                     ALU.mult), "att")
            pe.wait("low")
            for t in range(NT):
                mm = T.transpose(bank[6][:, t * P:(t + 1) * P], low[:, t, :], ident[:])
            m = pe.done(mm)
            ids = bcast(ident[:].unsqueeze(1), [P, NT, P])
            dve.wait("low")
            dve.wait_last_lap("wt")
            m1 = dve.done(V.tensor_tensor(xt[:, 2:4, :], low[:], bcast(levels[:, 0:1, :], [P, NT, P]), ALU.mult))
            dve.wait(m)
            m2 = dve.done(V.tensor_tensor(xt[:, 0:2, :], bank[6][:, 0:S].rearrange("p (a n) -> p a n", a=NT),
                                          bcast(level0_t[:].unsqueeze(1), [P, NT, P]), ALU.mult))
            dve.wait(m1)
            dve.done(V.tensor_tensor(xt[:, 2:4, :], ids, xt[:, 2:4, :], ALU.subtract))
            dve.wait(m2)
            inv = dve.done(V.tensor_tensor(xt[:, 0:2, :], ids, xt[:, 0:2, :], ALU.subtract))
            zc = None
            pool.wait("low")
            for b in range(1, LEVELS):
                if b > 2:
                    pool.wait(f"z{b - 2}")
                else:
                    pool.wait_last_lap(f"z{LEVELS - 3 + b}")
                lb = pool.done(G.tensor_tensor(low_b[:, b % 2], low[:], bcast(levels[:, b:b + 1, :], [P, NT, P]), ALU.mult))
                pe.wait(lb, inv)
                for t in range(NT):
                    mm = T.matmul(bank[6][:, t * P:(t + 1) * P], low_b[:, b % 2, t, :], xt[:, t, :], start=True, stop=True)
                m = pe.done(mm, f"z{b}")
                act.wait(m)
                zc = act.done(A.copy(z[:].rearrange("p a n -> p (a n)"), bank[6][:, 0:S]))
                pe.wait(zc)
                for t in range(NT):
                    mm = T.matmul(bank[7][:, t * P:(t + 1) * P], xt[:, 2 + t, :], z[:, t, :], start=True, stop=True)
                w = 2
                if b < LEVELS - 1:
                    w = 4
                    for t in range(NT):
                        mm = T.matmul(bank[7][:, (2 + t) * P:(3 + t) * P], z[:, t, :], xt[:, 2 + t, :], start=True, stop=True)
                m = pe.done(mm)
                dve.wait(m)
                inv = dve.done(V.tensor_tensor(xt[:, 0:w, :], xt[:, 0:w, :],
                                               bank[7][:, 0:w * P].rearrange("p (a n) -> p a n", n=P), ALU.subtract))
            dve.wait("v_turned")
            for t in range(NT):
                m = dve.done(V.tensor_scalar(vbeta[:, t, :], bank[5][:, t * A_DV:(t + 1) * A_DV],
                                             beta[:, t, bass.ds(hd, 1)], None, ALU.mult), "vbeta")
            dve.done(V.tensor_scalar(kb[:], qkn[:, 3, :], beta[:, 1, bass.ds(hd, 1)], e_cum[:, 1, bass.ds(hd, 1)],
                                     ALU.mult, ALU.mult), "kb")
            dve.wait("e_last", "e_row", "qkt")
            dve.done(V.tensor_scalar(kdec[:], qkn[:, 2, :], small[:, 44:45], None, ALU.mult), "kdec")
            dve.done(V.tensor_tensor(qexp[:], qkt[:, 1, :], e_row[:], ALU.mult), "qkt_read")
            pe.wait(inv, "vbeta", "kb")
            m0 = pe.done(T.matmul(bank[5][:, 0:A_DV], xt[:, 0, :], vbeta[:, 0, :], start=True, stop=True))
            mw = pe.done(T.matmul(bank[6][:, 0:P], kb[:], xt[:, 1, :], start=True, stop=True), "wt")
            act.wait(m0)
            m0 = act.done(A.copy(vn[:, 0, :], bank[5][:, 0:A_DV]))
            act.wait(mw)
            mw = act.done(A.activation(nwt[:], bank[6][:, 0:P], ACT.Copy, scale=-1.0))
            pe.wait(m0, "kdec", "att")
            m = pe.done(T.matmul(bank[4][:, 0:A_DV], kdec[:], vn[:, 0, :], start=True, stop=True))
            act.wait(m)
            ms = act.done(A.copy(state[:], bank[4][:, 0:A_DV]))
            pe.wait(ms, mw)
            T.matmul(bank[7][:, 0:A_DV], xt[:, 1, :], vbeta[:, 1, :], start=True, stop=False)
            m = pe.done(T.matmul(bank[7][:, 0:A_DV], nwt[:], state[:], start=False, stop=True))
            act.wait(m)
            m = act.done(A.copy(vn[:, 1, :], bank[7][:, 0:A_DV]))
            pe.wait(m, "qkt_read")
            T.matmul(bank[5][:, 0:A_DV], att[:, 0, :], vn[:, 0, :], start=True, stop=True)
            T.matmul(bank[5][:, A_DV:], qexp[:], state[:], start=True, stop=False)
            m = pe.done(T.matmul(bank[5][:, A_DV:], att[:, 1, :], vn[:, 1, :], start=False, stop=True))
            act.wait(m)
            for t in range(NT):
                m = act.done(A.activation(vn[:, t, :], bank[5][:, t * A_DV:(t + 1) * A_DV], ACT.Square,
                                          accum_out=small[:, 40 + t:41 + t]))
            pool.wait(m)
            m = rsqrt_col(42, 40, NT, 1.0 / A_DV)
            dve.wait(m)
            dve.wait_last_lap("o_turned")
            for t in range(NT):
                m = dve.done(V.scalar_tensor_tensor(o[:, t, :], bank[5][:, t * A_DV:(t + 1) * A_DV], small[:, 42 + t:43 + t],
                                                    norm_a[:], ALU.mult, ALU.mult), "o")
            dve.wait("o", "zs")
            dve.done(V.tensor_tensor(o[:], o[:], zs[:], ALU.mult), "gated")
            pe.wait("gated", ms)
            for f in range(2):
                for t in range(NT):
                    mm = T.transpose(bank[4][:, f * S + t * P:f * S + (t + 1) * P], o[:, t, f * P:(f + 1) * P], ident[:])
            m = pe.done(mm, "o_turned")
            o3 = bank[4][:, :].rearrange("p (a n) -> p a n", n=S)
            hi = mid_hi[:, bass.ds(hd * 2, 2), :]
            act.wait(m)
            m = act.done(A.copy(hi, o3))
            dve.wait(m)
            dve.done(V.tensor_tensor(mid_lo[:, bass.ds(hd * 2, 2), :], o3, hi.bitcast(F32), ALU.subtract), "mid_lo")
        stage("delta", delta)
        scope.close()
        b3.close()

        def branch(name, n_lap_banks):
            def body(lap, feed, arrived):
                pe.wait("mid_lo", "v_ret", "zs", "conv1", "x")
                if lap == 0 and "mixed" in Lane.names:
                    pe.wait("mixed")
                square_lap(arrived, 2 * KD, 1, (mid_hi, mid_lo), [n_lap_banks[lap]])
                feed(4)
            stage(name, body)

        ret = ExitStack()
        ctx.enter_context(ret)
        sig = sb("sig", [P, 2, 512], scope=ret)
        halves = [(0, 1), (2, 3)]

        def gated(name, accumulate):
            def body(lap, feed, arrived):
                pe.wait("mid_lo")
                square_lap(arrived, KD, 2, (h_hi, h_lo), [(4, 5), (6, 7)])
                feed(2)
                for n in range(2):
                    A.wait_ge(unit_done, unit_mark(name, lap, 2 * n + 1))
                    for t in range(NT):
                        if Lane.names.get(f"sig{t}"):
                            act.wait(f"sig{t}")
                        m = act.done(A.activation(sig[:, t, :], bank[4 + 2 * n + t][:, :], ACT.Sigmoid))
                        dve.wait(m)
                        dst = wide[:, t, n * 512:(n + 1) * 512]
                        if accumulate:
                            m = dve.done(V.tensor_tensor(sig[:, t, :], sig[:, t, :], bank[halves[n][t]][:, :], ALU.mult))
                            dve.wait(m)
                            m = dve.done(V.tensor_tensor(dst, dst, sig[:, t, :], ALU.add), f"sig{t}")
                        else:
                            m = dve.done(V.tensor_tensor(dst, sig[:, t, :], bank[halves[n][t]][:, :], ALU.mult), f"sig{t}")
                Lane.names["mixed"] = m
            stage(name, body)

        branch("br_a", halves)
        gated("gate_a", False)

        retain = sb("retain", [P, B_HEADS, 384], scope=ret)
        cos_b, sin_b = sb("cos_b", [P, S], scope=ret), sb("sin_b", [P, S], scope=ret)
        norm_b = sb("norm_b", [P, B_HEADS * B_DV], scope=ret)
        phase_load([(retain[:].rearrange("p a n -> p (a n)"), a["retain"]), (cos_b[:], a["cos_b"]), (sin_b[:], a["sin_b"]),
                    (norm_b[:], a["norm_b"].partition_broadcast(P).rearrange("p a n -> p (a n)"))], everything())
        qk_rot = sb("r_qk", [P, 2, 2, S], scope=ret)
        sw = sb("r_sw", [P, 2, S], scope=ret)
        scr = sb("r_sc", [P, 384], scope=ret)
        gsl = sb("r_g", [P, NT, B_DV], scope=ret)
        ob = sb("r_o", [P, NT, B_DV], scope=ret)
        pe.wait("mixed")

        def retention(hd, feed, arrived):
            for s, free in enumerate(("rot0", "rot1", "gsl0", "gsl1")):
                arrived(s)
                pe.wait_last_lap(free)
                if s < 2:
                    mm = feature_major(s, s, 2, (h_hi, h_lo))
                else:
                    mm = token_major(s, s, (h_hi, h_lo))
                mm.then_inc(unit_done, 1)
            ready = lambda s: (unit_done, unit_mark("retention", hd, s))
            cb = bcast(cos_b[:].unsqueeze(1), [P, 2, S])
            for j in range(2):
                V.wait_ge(*ready(j))
                dve.wait_last_lap("scored")
                u = bank[j][:, :].rearrange("p (a n) -> p a n", n=S)
                m = dve.done(V.tensor_tensor(qk_rot[:, j], u, cb, ALU.mult))
                if j:
                    dve.wait("rot0")
                dve.done(V.tensor_tensor(sw[:, 0, :], u[:, 1, :], sin_b[:], ALU.mult))
                m = dve.done(V.tensor_tensor(sw[:, 1, :], u[:, 0, :], sin_b[:], ALU.mult))
                dve.wait(m)
                dve.done(V.tensor_tensor(qk_rot[:, j, 0, :], qk_rot[:, j, 0, :], sw[:, 0, :], ALU.subtract))
                dve.done(V.tensor_tensor(qk_rot[:, j, 1, :], qk_rot[:, j, 1, :], sw[:, 1, :], ALU.add), f"rot{j}")
                feed()
            for j in range(2):
                A.wait_ge(*ready(2 + j))
                act.wait_last_lap("ob_gated")
                act.done(A.activation(gsl[:, :, j * 256:(j + 1) * 256], bank[2 + j][:, :].rearrange("p (t n) -> p t n", t=NT),
                                      ACT.Silu), f"gsl{j}")
            feed(2)
            pe.wait("rot0", "rot1")
            pe.wait_last_lap("scr", "mid_lo")
            for c0, w, k0, q0 in ((0, S, 0, 0), (S, P, P, P)):
                for f in range(2):
                    mm = T.matmul(bank[4][:, c0:c0 + w], qk_rot[:, 1, f, k0:k0 + P], qk_rot[:, 0, f, q0:q0 + w],
                                  start=f == 0, stop=f == 1)
            m = pe.done(mm, "scored")
            dve.wait(m)
            dve.wait_last_lap("o_done")
            dve.done(V.tensor_tensor(scr[:], bank[4][:, 0:384],
                                     retain[:, bass.ds(hd, 1), :].rearrange("p a n -> p (a n)"), ALU.mult), "scr")
            pe.wait("scr")
            pe.wait_last_lap("ob")
            vv = [v_ret[:, t, bass.ds(hd * B_DV, B_DV)] for t in range(NT)]
            T.matmul(bank[5][:, :], scr[:, 0:P], vv[0], start=True, stop=True)
            T.matmul(bank[6][:, :], scr[:, P:S], vv[0], start=True, stop=False)
            m = pe.done(T.matmul(bank[6][:, :], scr[:, S:384], vv[1], start=False, stop=True), "o_done")
            act.wait(m)
            act.wait_last_lap("ob_turned")
            for t in range(NT):
                m = act.done(A.activation(ob[:, t, :], bank[5 + t][:, :], ACT.Square, accum_out=small[:, 40 + t:41 + t]))
            pool.wait(m)
            m = rsqrt_col(42, 40, NT, 1.0 / B_DV)
            dve.wait(m)
            for t in range(NT):
                dve.done(V.scalar_tensor_tensor(ob[:, t, :], bank[5 + t][:, :], small[:, 42 + t:43 + t],
                                                norm_b[:, bass.ds(hd * B_DV, B_DV)], ALU.mult, ALU.mult), "ob")
            dve.wait("ob", "gsl0", "gsl1")
            dve.done(V.tensor_tensor(ob[:], ob[:], gsl[:], ALU.mult), "ob_gated")
            pe.wait("ob_gated")
            for b, f0 in ((7, 0), (4, 2)):
                for f in range(f0, f0 + 2):
                    for t in range(NT):
                        mm = T.transpose(bank[b][:, (f - f0) * S + t * P:(f - f0) * S + (t + 1) * P],
                                         ob[:, t, f * P:(f + 1) * P], ident[:])
                m = pe.done(mm, "ob_turned")
                o3 = bank[b][:, :].rearrange("p (a n) -> p a n", n=S)
                hi = mid_hi[:, bass.ds(hd * 4 + f0, 2), :]
                act.wait(m)
                m = act.done(A.copy(hi, o3))
                dve.wait(m)
                dve.done(V.tensor_tensor(mid_lo[:, bass.ds(hd * 4 + f0, 2), :], o3, hi.bitcast(F32), ALU.subtract), "mid_lo")
        stage("retention", retention)
        pe.wait("gsl0", "gsl1", "rot1", "rot0")
        branch("br_b", halves)
        gated("gate_b", True)
        ret.close()
        b2.close()

        pe.wait("mixed")
        for b in range(4):
            for k in range(2 * b, 2 * b + 2):
                for t in range(NT):
                    c = (k % 2) * S + t * P
                    mm = T.transpose(bank[TR[b]][:, c:c + P], wide[:, t, k * P:(k + 1) * P], ident[:])
            m = pe.done(mm)
            o3 = bank[TR[b]][:, :].rearrange("p (a n) -> p a n", n=S)
            act.wait(m)
            m = act.done(A.copy(h_hi[:, 2 * b:2 * b + 2, :], o3))
            dve.wait(m)
            m = dve.done(V.tensor_tensor(h_lo[:, 2 * b:2 * b + 2, :], o3, h_hi[:, 2 * b:2 * b + 2, :].bitcast(F32), ALU.subtract))
        Lane.names["normed"] = m

        end = ExitStack()
        ctx.enter_context(end)
        junk = sb("junk", [P, NT, D], scope=end)
        act.wait(*everything())
        dve.wait(*everything())

        def add_normed(banks, ready, which):
            phase_load([(row[:], a["rows"][which:which + 1, :].partition_broadcast(P).rearrange("p a n -> p (a n)"))],
                       ("x",))
            for n in range(2):
                for t in range(NT):
                    A.wait_ge(*ready(n))
                    m = act.done(A.copy(wide[:, t, n * 512:(n + 1) * 512], bank[banks[n][t]][:, :]))
            m = statistics(wide, (m,), junk)
            dve.wait(m)
            for t in range(NT):
                m = dve.done(V.scalar_tensor_tensor(wide[:, t, :], wide[:, t, :], small[:, 2 + t:3 + t], row[:],
                                                    ALU.mult, ALU.mult))
                dve.wait(m)
                dve.done(V.tensor_tensor(x[:, t, :], x[:, t, :], wide[:, t, :], ALU.add), "x")

        def w_out(lap, feed, arrived):
            pe.wait("normed")
            square_lap(arrived, KD, 2, (h_hi, h_lo), halves)
            feed(4)
            add_normed(halves, lambda n: (unit_done, unit_mark("w_out", lap, 2 * n + 1)), 1)
        stage("w_out", w_out)
        if stop == "w_out":
            finish(x[:])
            return new_plan
        normed(x, ("x",), [(6, h_hi, h_lo)], ("x",))

        rl = sb("m_relu", [P, 2, 2 * S], scope=end)
        sq = sb("m_sq", [P, 2, 2 * S], scope=end)
        gm_hi, gm_lo = sb("gm_hi", [P, 4, S], F32R, scope=end), sb("gm_lo", [P, 4, S], F32R, scope=end)
        acc = [(4, 5), (6, 7)]

        def m_up(arrived):
            for s in range(2):
                arrived(s)
                pe.wait_last_lap(f"sq{s}")
                feature_major(s, s, 2, (h_hi, h_lo)).then_inc(unit_done, 1)

        def m_post(st, j, feed, down_value):
            for s in range(2):
                A.wait_ge(unit_done, unit_mark(st, j, s))
                act.wait_last_lap(f"sq{s}", "gm")
                m = act.done(A.activation(rl[:, s, :], bank[s][:, :], ACT.Relu))
                dve.wait(m)
                dve.done(V.scalar_tensor_tensor(sq[:, s, :], bank[s][:, :], 0.0, rl[:, s, :], ALU.max, ALU.mult), f"sq{s}")
                feed()
            if down_value is not None:
                A.wait_ge(unit_done, down_value)
            act.wait("sq0", "sq1")
            sqv = sq[:].rearrange("p a (b n) -> p (a b) n", n=S)
            m = act.done(A.copy(gm_hi[:], sqv))
            dve.wait(m)
            dve.done(V.tensor_tensor(gm_lo[:], sqv, gm_hi[:].bitcast(F32), ALU.subtract), "gm")

        def m_down(s0, arrived):
            for a2 in range(2):
                arrived(s0 + a2)
                wh = w_hi[:, s0 + a2, :].rearrange("p (k n) -> p k n", k=2)
                wl = w_lo[:, s0 + a2, :].rearrange("p (k n) -> p k n", k=2)
                for k in range(2):
                    for t in range(NT):
                        tk = slice(t * P, (t + 1) * P)
                        for n in range(2):
                            nn = slice(n * 512, (n + 1) * 512)
                            ob_ = bank[acc[t][n]][:, :]
                            kk = 2 * a2 + k
                            T.matmul(ob_, gm_hi[:, kk, tk], wh[:, k, nn], start=False, stop=False, skip_group_check=True)
                            T.matmul(ob_, gm_hi[:, kk, tk], wl[:, k, nn], start=False, stop=False, skip_group_check=True)
                            mm = T.matmul(ob_, gm_lo[:, kk, tk], wh[:, k, nn], start=False, stop=True, skip_group_check=True)
                mm.then_inc(unit_done, 1)

        def m_first(j, feed, arrived):
            m_up(arrived)
            pe.wait("normed")
            for t in range(NT):
                for n in range(2):
                    T.matmul(bank[acc[t][n]][:, :], zero_r[:, 0:P], zero_r[:], start=True, stop=True, skip_group_check=True)
            m_post("mlp_first", j, feed, None)
        stage("mlp_first", m_first)
        pe.wait("gm", "sq0", "sq1")

        def m_middle(j, feed, arrived):
            m_up(arrived)
            pe.wait_last_lap("gm")
            m_down(2, arrived)
            m_post("mlp", j, feed, unit_mark("mlp", j, 3))
        stage("mlp", m_middle)

        def m_last(j, feed, arrived):
            pe.wait("gm")
            m_down(0, arrived)
            add_normed([(4, 6), (5, 7)], lambda n: (unit_done, unit_mark("mlp_last", j, 1)), 2)
        stage("mlp_last", m_last)
        finish(x[:])
    return new_plan


class _Guess(dict):
    def __init__(self, lanes):
        super().__init__()
        self.lanes = lanes

    def __missing__(self, key):
        return self.lanes[0], 1


def arrays(i):
    def column(v):
        return v.reshape(KD, P).T
    out = {
        "x": i["x"][0], "positions": i["positions"], "stream": weight_stream(i),
        "gains": np.stack([column(v) for v in (
            i["attn_norm"][0], i["ffn_norm"][0], i["kv_norm"], i["attn_norm"][1], i["ffn_norm"][1],
            i["norm_mix_pre_2"][0], i["norm_mlp_pre_2"][0])], 1).reshape(P, -1),
        "rows": np.stack([i["final_norm"], i["norm_mix_post_2"][0], i["norm_mlp_post_2"][0]]),
        "norm_a": i["norm_a_2"], "norm_b": i["norm_b_2"],
        "sinks": i["sinks_b"], "a_log": i["a_log_2"], "dt_bias": i["dt_bias_2"],
        "w_ba": cols_unit(i["w_in_2"][0], (C_BA, 2 * A_HEADS)),
    }
    taps = np.concatenate([i["conv_w"], i["conv_b"][:, None, :]], 1)
    taps = taps.reshape(2, 4, 2, F_LAPS, 2, P)
    out["conv"] = taps.transpose(5, 0, 3, 2, 4, 1).reshape(P, -1)
    ca = i["conv_a_2"][0].reshape(4, 32, P)
    per_head = np.stack([ca[:, 0:8], ca[:, 8:16], ca[:, 16:32:2], ca[:, 17:32:2]], 2)
    out["conv_a"] = per_head.transpose(3, 1, 2, 0).reshape(P, -1)
    out.update(constants())
    return {k: np.ascontiguousarray(v) for k, v in out.items()}


def kernel(**inputs):
    import concourse.bacc as bacc
    from concourse.bass_utils import run_bass_kernel_spmd

    host = arrays({k: np.asarray(v) for k, v in inputs.items()})

    def build(plan):
        nc = bacc.Bacc("TRN2", target_bir_lowering=False, num_devices=1)
        dram = {n: nc.dram_tensor(n, v.shape, mybir.dt.from_np(v.dtype), kind="ExternalInput").ap()
                for n, v in host.items()}
        out = nc.dram_tensor("out", (S, D), F32, kind="ExternalOutput").ap()
        return nc, program(nc, dram, out, plan)

    _, plan = build({})
    nc, again = build(plan)
    assert plan == again
    r = run_bass_kernel_spmd(nc, [host], core_ids=[0])
    return r.results[0]["out"].reshape(1, S, D)
```

```python
from contextlib import ExitStack, contextmanager

import numpy as np

import concourse.bass as bass
from concourse import mybir

F32 = mybir.dt.float32
F32R = mybir.dt.float32r
I32 = mybir.dt.int32
ALU = mybir.AluOpType
ACT = mybir.ActivationFunctionType
AX = mybir.AxisListType
ENG = mybir.EngineType

P = 128
S = 256
NT = S // P
D = 1024
KD = D // P
EPS = 1e-6
NEG = -1e30
HEADS, HD, KV_HEADS, ROT = 16, 64, 4, 16
GROUPS = 4
GH = HEADS // GROUPS
F_TILES = 2816 // P
F_LAPS = F_TILES // 2
A_HEADS, A_DK, A_DV = 8, 128, 256
B_HEADS, B_DK, B_DV = 4, 256, 512
RET_CHUNK = 64
FF2 = 4096
M_LAPS = FF2 // (4 * P)
UNIT = 2048
SLOTS = 4
LEAD = 64
LEVELS = 7

C_QA, C_KA, C_VA, C_ZA, C_BA, C_QB, C_KB, C_VB, C_GB, C_GA2, C_GB2 = (
    0, 1024, 2048, 4096, 6144, 6160, 7184, 8208, 10256, 12304, 13328)


def constants():
    r = np.arange(P)
    row, col = r[:, None], r[None, :]
    f = np.float32
    out = {}
    out["ident"] = (row == col).astype(f)
    rot = np.zeros((P, P), f)
    for h in range(0, P, HD):
        for j in range(ROT // 2):
            rot[h + j + ROT // 2, h + j] = -1.0
            rot[h + j, h + j + ROT // 2] = 1.0
    out["rot"] = rot
    freq = np.zeros((P, 1), f)
    inv = np.power(f(500000.0), (-np.arange(0, ROT, 2).astype(f) / f(ROT))).astype(f)
    for h in range(0, P, HD):
        freq[h:h + ROT, 0] = np.concatenate([inv, inv])
    out["freq"] = freq
    causal = np.where(col <= row, 0.0, NEG).astype(f)
    band = np.where(col > row, 0.0, NEG).astype(f)
    out["mask_full"] = np.concatenate([causal, np.zeros((P, P), f), causal], 1)
    out["mask_window"] = np.concatenate([causal, band, causal], 1)
    out["upper"] = (row <= col).astype(f)
    out["lower_strict"] = (row > col).astype(f)
    lev = []
    for b in range(LEVELS):
        w = 1 << b
        lev.append(((row // (2 * w) == col // (2 * w)) & (row // w % 2 == 1) & (col // w % 2 == 0)).astype(f))
    out["levels"] = np.concatenate(lev, 1)
    out["level0_t"] = lev[0].T.copy()
    ret = []
    for h in range(B_HEADS):
        lg = np.log1p(-np.exp2(f(-5.0 - h))).astype(f)
        m, c = np.arange(S)[:, None], np.arange(S)[None, :]
        w = np.exp(lg * np.abs(c - m).astype(f)).astype(f) * (m // RET_CHUNK <= c // RET_CHUNK) * f(B_DK ** -0.5)
        ret.append(np.concatenate([w[0:P, :], w[P:S, P:S]], 1).astype(f))
    out["retain"] = np.concatenate(ret, 1)
    fb = np.power(f(10000.0), (-np.arange(0, B_DK, 2).astype(f) / f(B_DK))).astype(f)
    ang = (np.arange(S).astype(f)[None, :] * fb[:, None]).astype(f)
    out["cos_b"], out["sin_b"] = np.cos(ang).astype(f), np.sin(ang).astype(f)
    return {k: np.ascontiguousarray(v, f) for k, v in out.items()}


def cols_unit(w, *starts_and_widths):
    w = np.concatenate([w[:, a:a + n] for a, n in starts_and_widths], 1)
    return w.reshape(KD, P, -1).transpose(1, 0, 2).reshape(P, -1)


def rows_unit(w, k, kn, n, nn):
    return w[k * P:(k + kn) * P, n:n + nn].reshape(kn, P, nn).transpose(1, 0, 2).reshape(P, -1)


def square_units(w, k_blocks):
    return [rows_unit(w, 4 * k, 4, 512 * n, 512) for k, n in k_blocks]


BY_TILES = [(0, 0), (0, 1), (1, 0), (1, 1)]
BY_COLUMNS = [(0, 0), (1, 0), (0, 1), (1, 1)]
BR_A = [(0, 0), (1, 0), (2, 0), (0, 1), (1, 1), (2, 1), (3, 0), (3, 1)]
BR_B = [(k, n) for n in range(2) for k in range(4)]


def ffn_units(w_up, w_down):
    up = [[cols_unit(w_up, (256 * j, 256)), cols_unit(w_up, (F_TILES * P + 256 * j, 256))] for j in range(F_LAPS)]
    down = [[rows_unit(w_down, 2 * j, 2, 0, D)] for j in range(F_LAPS)]
    out = list(up[0])
    for j in range(1, F_LAPS):
        out += up[j] + down[j - 1]
    return out + down[-1]


def weight_stream(i):
    u = []
    for g in range(GROUPS):
        u += [cols_unit(i["w_qkv_a"][0], (part * D + 256 * g, 256)) for part in range(3)]
    u += square_units(i["w_o_a"][0], BY_TILES)
    u += ffn_units(i["w_up"][0], i["w_down"][0])
    for g in range(GROUPS):
        u.append(cols_unit(i["w_q_b"][0], (256 * g, 256)))
        kv = cols_unit(i["w_kv_b"], (HD * g, HD), (HD * g, HD), (KV_HEADS * HD + HD * g, HD))
        u.append(np.concatenate([kv, np.zeros((P, UNIT - kv.shape[1]), np.float32)], 1))
    u += square_units(i["w_o_b"][0], BY_TILES)
    u += ffn_units(i["w_up"][1], i["w_down"][1])
    w = i["w_in_2"][0]
    for h in range(A_HEADS):
        u += [cols_unit(w, (C_QA + P * h, P), (C_KA + P * h, P)), cols_unit(w, (C_VA + 256 * h, 256)),
              cols_unit(w, (C_VB + 256 * h, 256))]
        if h:
            u.append(cols_unit(w, (C_ZA + 256 * (h - 1), 256)))
    u += square_units(w[:, C_GA2:C_GA2 + D], BY_COLUMNS)
    u.append(cols_unit(w, (C_ZA + 256 * (A_HEADS - 1), 256)))
    u += square_units(i["w_br_a_2"][0], BR_A)
    for h in range(B_HEADS):
        u += [cols_unit(w, (C_QB + 256 * h, 256)), cols_unit(w, (C_KB + 256 * h, 256)),
              cols_unit(w, (C_GB + 512 * h, 256)), cols_unit(w, (C_GB + 512 * h + 256, 256))]
    u += square_units(w[:, C_GB2:C_GB2 + D], BY_COLUMNS)
    u += square_units(i["w_br_b_2"][0], BR_B)
    u += square_units(i["w_out_2"][0], BY_COLUMNS)
    up = [[cols_unit(i["w_up_2"][0], (512 * j, 256)), cols_unit(i["w_up_2"][0], (512 * j + 256, 256))]
          for j in range(M_LAPS)]
    down = [[rows_unit(i["w_down_2"][0], 4 * j + 2 * a, 2, 0, D) for a in range(2)] for j in range(M_LAPS)]
    u += up[0]
    for j in range(1, M_LAPS):
        u += up[j] + down[j - 1]
    u += down[-1]
    return np.stack(u)


STREAM = [("attn_a", GROUPS, 3), ("wo_a", 1, 4),
          ("ffn_a_first", 1, 2), ("ffn_a", F_LAPS - 1, 3), ("ffn_a_last", 1, 1),
          ("attn_b", GROUPS, 2), ("wo_b", 1, 4),
          ("ffn_b_first", 1, 2), ("ffn_b", F_LAPS - 1, 3), ("ffn_b_last", 1, 1),
          ("delta_first", 1, 3), ("delta", A_HEADS - 1, 4), ("delta_gate", 1, 4), ("delta_last", 1, 4),
          ("br_a", 1, 4), ("br_a_last", 1, 1),
          ("retention", B_HEADS, 4), ("gate_b", 1, 4), ("br_b", 2, 4), ("w_out", 1, 4),
          ("mlp_first", 1, 2), ("mlp", M_LAPS - 1, 4), ("mlp_last", 1, 2)]


class Mark:

    def __init__(self, lane, loop, offset):
        self.lane, self.loop, self.offset = lane, loop, offset


class Lane:

    def __init__(self, eng, sem):
        self.eng, self.sem = eng, sem
        self.start = 0
        self.k = 0

    def done(self, ins, name=None):
        ins.then_inc(self.sem, 1)
        self.k += 1
        m = Mark(self, Lane.loop, self.k if Lane.loop else self.start + self.k)
        if Lane.loop and Lane.loop.starts.get(self) is None:
            raise AssertionError
        if name:
            Lane.names[name] = m
            if Lane.loop:
                Lane.loop.seen[name] = (self, self.k)
        return m

    def wait(self, *marks):
        latest = {}
        for m in marks:
            if isinstance(m, str):
                m = Lane.names[m]
            if m is None or (m.lane is self and self.eng is Lane.pe_eng):
                continue
            key = (m.lane, m.loop is not None and m.loop is Lane.loop)
            if key not in latest or place(m) > place(latest[key]):
                latest[key] = m
        for m in latest.values():
            self.eng.wait_ge(m.lane.sem, value_of(m))

    def wait_last_lap(self, *names):
        if Lane.loop is None:
            self.wait(*[n for n in names if n in Lane.names])
            return
        latest = {}
        for n in names:
            Lane.loop.entry.append((self, n))
            lane, k = Lane.loop.plan_names[n]
            if lane is not self or self.eng is not Lane.pe_eng:
                latest[lane] = max(k, latest.get(lane, 0))
        for lane, k in latest.items():
            base = Lane.loop.starts[lane] + k - Lane.loop.per[lane]
            self.eng.wait_ge(lane.sem, Lane.loop.i * Lane.loop.per[lane] + base)


def place(m):
    return m.offset if m.loop is None or m.loop is Lane.loop else value_of(m)


def value_of(m):
    if m.loop is None:
        return m.offset
    lp = m.loop
    if lp is Lane.loop:
        return lp.i * lp.per[m.lane] + (lp.starts[m.lane] + m.offset)
    return (lp.n - 1) * lp.per[m.lane] + lp.starts[m.lane] + m.offset


class Loop:
    pass


Lane.loop = None
Lane.names = {}


def program(nc, a, out, plan, stop=None, debug=None):
    new_plan = {}
    with ExitStack() as ctx:
        def sb(name, shape, dt=F32, scope=ctx):
            name = f"sb_{name}"
            return scope.enter_context(nc.sbuf_tensor(name, shape, dt))

        def sem(name):
            return ctx.enter_context(nc.semaphore(name))

        pe, act, dve, pool = (Lane(e, sem(n)) for e, n in (
            (nc.tensor, "pe_done"), (nc.scalar, "act_done"), (nc.vector, "dve_done"), (nc.gpsimd, "pool_done")))
        LANES = (pe, act, dve, pool)
        for ln in LANES:
            ln.eng.sem_inc(ln.sem, LEAD)
            ln.start = LEAD
        Lane.pe_eng = nc.tensor
        Lane.loop, Lane.names = None, {}
        T, A, V, G = nc.tensor, nc.scalar, nc.vector, nc.gpsimd

        @contextmanager
        def laps(tag, n):
            lp = Loop()
            lp.n = n
            known = plan.get(tag, {"per": [1000] * 4, "names": {}})
            lp.per = dict(zip(LANES, known["per"]))
            lp.plan_names = {k: (LANES[x], y) for k, (x, y) in known["names"].items()}
            if not known["names"]:
                lp.plan_names = _Guess(LANES)
            lp.starts = {ln: ln.start + ln.k for ln in LANES}
            lp.seen, lp.entry = {}, []
            for x, name in known.get("entry", ()):
                if name in Lane.names:
                    LANES[x].wait(name)
            for ln in LANES:
                ln.start, ln.k = ln.start + ln.k, 0
            with nc.Fori(0, n, engines=[ENG.PE, ENG.Activation, ENG.DVE, ENG.Pool]) as i:
                lp.i = i
                Lane.loop = lp
                yield i
            Lane.loop = None
            new_plan[tag] = {"per": [ln.k for ln in LANES],
                             "entry": sorted({(LANES.index(x), y) for x, y in lp.entry}),
                             "names": {k: (LANES.index(x), y) for k, (x, y) in lp.seen.items()}}
            for ln in LANES:
                ln.start, ln.k = ln.start + n * ln.k, 0

        raw = sb("raw", [P, SLOTS, UNIT])
        w_hi = sb("w_hi", [P, SLOTS, UNIT], F32R)
        w_lo = sb("w_lo", [P, SLOTS, UNIT], F32R)
        raw_in = [sem(f"raw_in{r}") for r in range(SLOTS)]
        hi_done, lo_done = sem("hi_done"), sem("lo_done")
        unit_done = sem("unit_done")

        cut = {"attn_a": 2, "ffn_a": 5, "ffn_b": 10, "w_out": 19}.get(stop, 99)
        stream = STREAM[:cut]
        info, u0, before, uses = {}, 0, 0, [0] * SLOTS
        for name, n, r in stream:
            info[name] = (u0, n, r, before, list(uses))
            for s in range(r):
                uses[s] += n
            u0, before = u0 + n * r, r
        n_units = u0

        def raw_value(name, lap, s):
            return (lap + (info[name][4][s] + 1)) * 16

        def distance(name, first, s):
            _, _, r, before, _ = info[name]
            return r if not first else before if s < before else before + s

        for name, n, r in stream:
            u0, _, _, before, _ = info[name]

            def load(lap, s, first, u0=u0, r=r, name=name, before=before):
                if before or not first:
                    nc.sync.wait_ge(lo_done, lap * r + (u0 + s - distance(name, first, s) + 1))
                nc.sync.dma_start(raw[:, s, :], a["stream"][bass.ds(lap * r + (u0 + s), 1)]
                                  .rearrange("u p n -> (u p) n")).then_inc(raw_in[s], 16)
            for s in range(r):
                load(0, s, True)
            if n > 1:
                with nc.sync.Fori(1, n) as lap:
                    for s in range(r):
                        load(lap, s, False)

        order = [x[0] for x in stream]

        def split(name, lap, s, first):
            u0, _, r, before, _ = info[name]
            if before or not first:
                A.wait_ge(unit_done, lap * r + (u0 + s - distance(name, first, s) + 1))
            A.wait_ge(raw_in[s], raw_value(name, lap, s))
            A.copy(w_hi[:, s, :], raw[:, s, :]).then_inc(hi_done, 1)
            V.wait_ge(hi_done, lap * r + (u0 + s + 1))
            V.tensor_tensor(w_lo[:, s, :], raw[:, s, :], w_hi[:, s, :].bitcast(F32),
                            ALU.subtract).then_inc(lo_done, 1)

        class Feed:

            def __init__(self, name, lap, last):
                if last:
                    nxt = order.index(name) + 1
                    self.name = order[nxt] if nxt < len(order) else None
                    self.lap, self.first = 0, True
                else:
                    self.name, self.lap, self.first = name, lap + 1, False
                self.r = info[self.name][2] if self.name else 0
                self.s = 0

            def __call__(self, n=1):
                for _ in range(n):
                    if self.s < self.r:
                        split(self.name, self.lap, self.s, self.first)
                        self.s += 1

        def stage(name, body, peel=0):
            u0, n, r, _, _ = info[name]

            def run(lap, last):
                def arrived(s):
                    T.wait_ge(lo_done, lap * r + (u0 + s + 1))
                feed = Feed(name, lap, last)
                body(lap, feed, arrived)
                feed(SLOTS)
            for lap in range(peel):
                run(lap, False)
            if n - peel > 2:
                with laps(name, n - 1 - peel) as i:
                    run(i + peel if peel else i, False)
            else:
                for lap in range(peel, n - 1):
                    run(lap, False)
            run(n - 1, True)

        def weave(*parts):
            order = []
            for c, (steps, lo, hi) in enumerate(parts):
                for j, f in enumerate(steps):
                    order.append((lo + (hi - lo) * (j + 0.5) / len(steps), c, j, f))
            for *_, f in sorted(order, key=lambda x: x[:3]):
                f()

        bank = [ctx.enter_context(nc.psum_tensor(f"bank{b}", [P, 512], F32)) for b in range(8)]
        x = sb("x", [P, NT, D])
        h_hi = sb("h_hi", [P, KD, S], F32R)
        h_lo = sb("h_lo", [P, KD, S], F32R)
        mid_hi = sb("mid_hi", [P, 2 * KD, S], F32R)
        mid_lo = sb("mid_lo", [P, 2 * KD, S], F32R)
        wide = sb("wide", [P, NT, D])
        row = sb("row", [P, D])
        ident = sb("ident", [P, P])
        gains = sb("gains", [P, 7, KD])
        small = sb("small", [P, 64])
        POOL_CONST = {v: j for j, v in enumerate((-0.5, EPS, 256.0 / B_DV))}
        pool_const = sb("pool_const", [P, len(POOL_CONST), 4])
        boot, row_in, out_done = sem("boot"), sem("row_in"), sem("out_done")
        row_loads = [0]

        A.dma_start(x[:], a["x"].rearrange("(t p) d -> p t d", p=P)).then_inc(boot, 16)
        A.dma_start(ident[:], a["ident"]).then_inc(boot, 16)
        A.dma_start(gains[:], a["gains"].rearrange("p (a k) -> p a k", k=KD)).then_inc(boot, 16)
        for v, j in POOL_CONST.items():
            pool.wait(pool.done(G.memset(pool_const[:, j, :], v)))
        for ln in (act, dve, pe):
            ln.eng.wait_ge(boot, 48)

        phase_loads = [0]
        phase_in = sem("phase_in")

        def phase_load(pairs, after=()):
            act.wait(*after)
            for dst, src in pairs:
                A.dma_start(dst, src).then_inc(phase_in, 16)
                phase_loads[0] += 16
            v = phase_loads[0]
            for ln in (act, dve, pe, pool):
                ln.eng.wait_ge(phase_in, v)

        def bcast(ap, shape):
            return ap.to_broadcast(shape)

        def three(out_ap, l_hi, l_lo, r_hi, r_lo, start, stop, **kw):
            T.matmul(out_ap, l_hi, r_hi, start=start, stop=False, **kw)
            T.matmul(out_ap, l_hi, r_lo, start=False, stop=False, **kw)
            return T.matmul(out_ap, l_lo, r_hi, start=False, stop=stop, **kw)

        def used(ins, name=None):
            ins.then_inc(unit_done, 1)

        def parts_of(s, k, width):
            n = k * width
            return (w_hi[:, s, 0:n].rearrange("p (k n) -> p k n", k=k), w_lo[:, s, 0:n].rearrange("p (k n) -> p k n", k=k))

        def fresh_wait(fresh, k):
            if fresh and k % 2 == 0:
                pe.wait(fresh[k // 2])

        def feature_major(s, b, tiles, acts, before, width=256, fresh=None, ends=True):
            wh, wl = parts_of(s, KD, width)

            def step(j, k0):
                if j == k0 == 0:
                    before()
                for k in range(k0, k0 + 4):
                    if j == 0:
                        fresh_wait(fresh, k)
                    mm = three(bank[b][:, j * S:(j + 1) * S], wh[:, k, j * P:(j + 1) * P],
                               wl[:, k, j * P:(j + 1) * P], acts[0][:, k, :], acts[1][:, k, :], k == 0, k == KD - 1)
                if ends and (j, k0) == (tiles - 1, 4):
                    mm.then_inc(unit_done, 1)
            return [lambda j=j, k0=k0: step(j, k0) for j in range(tiles) for k0 in (0, 4)]

        def token_major(s, b, acts, before, c0=0, cols=256, width=256):
            wh, wl = parts_of(s, KD, width)

            def step(t, k0):
                if t == k0 == 0:
                    before()
                o, tk = bank[b][:, t * cols:(t + 1) * cols], slice(t * P, (t + 1) * P)
                for k in range(k0, k0 + 4):
                    mm = three(o, acts[0][:, k, tk], acts[1][:, k, tk], wh[:, k, c0:c0 + cols], wl[:, k, c0:c0 + cols],
                               k == 0, k == KD - 1)
                if (t, k0) == (NT - 1, 4):
                    mm.then_inc(unit_done, 1)
            return [lambda t=t, k0=k0: step(t, k0) for t in range(NT) for k0 in (0, 4)]

        def square_unit(s, block, kt, acts, banks, before, fresh=None):
            wh, wl = parts_of(s, 4, 512)

            def step(t, k0):
                if t == k0 == 0:
                    before()
                tk = slice(t * P, (t + 1) * P)
                for k in range(k0, k0 + 2):
                    kk = 4 * block + k
                    if t == 0:
                        fresh_wait(fresh, kk)
                    mm = three(bank[banks[t]][:, :], acts[0][:, kk, tk], acts[1][:, kk, tk], wh[:, k, :], wl[:, k, :],
                               kk == 0, kk == kt - 1)
                if (t, k0) == (NT - 1, 2):
                    mm.then_inc(unit_done, 1)
            return [lambda t=t, k0=k0: step(t, k0) for t in range(NT) for k0 in (0, 2)]

        def unit_mark(name_of_stage, lap, s):
            u0, _, r, _, _ = info[name_of_stage]
            return lap * r + (u0 + s + 1)

        def rsqrt_col(dst, src, n, halves=False, scale=None):
            d = small[:, dst:dst + n]
            s0 = small[:, src:src + n]
            if halves:
                pair = small[:, src:src + 2 * n].rearrange("p (t a) -> p t a", a=2)
                pool.wait(pool.done(G.tensor_tensor(d, pair[:, :, 0], pair[:, :, 1], ALU.add)))
                s0 = d
            if scale:
                pool.wait(pool.done(G.tensor_tensor(d, s0, pool_const[:, POOL_CONST[scale], 0:n], ALU.mult)))
                s0 = d
            pool.wait(pool.done(G.tensor_tensor(d, s0, pool_const[:, POOL_CONST[EPS], 0:n], ALU.add)))
            return pool.done(G.tensor_tensor(d, d, pool_const[:, POOL_CONST[-0.5], 0:n], ALU.pow))

        def zeros(scope):
            z = sb(f"zeros{len(zero_tiles)}", [P, 512], F32R, scope=scope)
            zero_tiles.append(z)
            pool.wait(*everything())
            pool.done(G.memset(z[:].bitcast(F32), 0.0), "zeros")
            return z
        zero_tiles = []

        TR = [4, 5, 6, 7]
        CHUNKS = [(0, 0), (1, 0), (0, 1), (1, 1)]

        def chunk(buf, t, n):
            return buf[:, t, n * 512:(n + 1) * 512]

        def mean_squares(src, marks, junk):
            for t, n in CHUNKS:
                act.wait(marks[t, n])
                m = act.done(A.activation(chunk(junk, t, n), chunk(src, t, n), ACT.Square, scale=D ** -0.5,
                                          accum_out=small[:, 2 * t + n:2 * t + n + 1]))
            pool.wait(m)
            return rsqrt_col(4, 0, NT, halves=True)

        def turned(marks, targets):
            ready = []
            for b in range(4):
                pe.wait(*marks[b // 2])
                for k in range(2 * b, 2 * b + 2):
                    for t in range(NT):
                        c = (k % 2) * S + t * P
                        mm = T.transpose(bank[TR[b]][:, c:c + P], wide[:, t, k * P:(k + 1) * P], ident[:])
                act.wait(pe.done(mm))
                for k in range(2 * b, 2 * b + 2):
                    for g, hi, lo in targets:
                        u = bank[TR[b]][:, (k % 2) * S:(k % 2 + 1) * S]
                        if g is None:
                            m = act.done(A.copy(hi[:, k, :], u))
                        else:
                            m = act.done(A.activation(hi[:, k, :], u, ACT.Copy, scale=gains[:, g, k:k + 1]))
                dve.wait(m)
                for k in range(2 * b, 2 * b + 2):
                    for g, hi, lo in targets:
                        u = bank[TR[b]][:, (k % 2) * S:(k % 2 + 1) * S]
                        if g is None:
                            m = dve.done(V.tensor_tensor(lo[:, k, :], u, hi[:, k, :].bitcast(F32), ALU.subtract))
                        else:
                            m = dve.done(V.scalar_tensor_tensor(lo[:, k, :], u, gains[:, g, k:k + 1],
                                                                hi[:, k, :].bitcast(F32), ALU.mult, ALU.subtract))
                ready.append(m)
            Lane.names["turned"] = m
            return ready

        def normed(src, marks, targets):
            m = mean_squares(src, marks, wide)
            act.wait(m)
            dve.wait(m)
            scaled = []
            for n in range(2):
                m0 = act.done(A.activation(chunk(wide, 0, n), chunk(src, 0, n), ACT.Copy, scale=small[:, 4:5]))
                m1 = dve.done(V.tensor_scalar(chunk(wide, 1, n), chunk(src, 1, n), small[:, 5:6], None, ALU.mult))
                scaled.append((m0, m1))
            return turned(scaled, targets)

        def add_residual(banks, wait_ready):
            marks = {}
            for t, n in CHUNKS:
                wait_ready(t, n)
                marks[t, n] = dve.done(V.tensor_tensor(chunk(x, t, n), bank[banks[n][t]][:, :], chunk(x, t, n), ALU.add))
            Lane.names["x"] = marks[1, 1]
            return marks

        def everything():
            return [Mark(ln, None, ln.start + ln.k) for ln in LANES]

        feed0 = Feed("attn_a", -1, False)
        feed0.name, feed0.lap, feed0.first, feed0.r = "attn_a", 0, True, info["attn_a"][2]
        feed0(SLOTS)

        b1 = ExitStack()
        ctx.enter_context(b1)
        cos_t, sin_t = sb("cos_t", [P, S], scope=b1), sb("sin_t", [P, S], scope=b1)
        rot = sb("rot", [P, P], scope=b1)
        freq = sb("freq", [P, 1], scope=b1)
        pos_i, pos_f = sb("pos_i", [P, S], I32, scope=b1), sb("pos_f", [P, S], scope=b1)
        turns = sb("turns", [P, S], scope=b1)
        masks = sb("masks", [P, 2, 384], scope=b1)
        sinks = sb("sinks", [P, HEADS], scope=b1)
        conv = sb("conv", [P, 2, F_LAPS, 4, 4], scope=b1)
        phase_load([(rot[:], a["rot"]), (freq[:], a["freq"]),
                    (pos_i[:], a["positions"].partition_broadcast(P).rearrange("p a n -> p (a n)")),
                    (masks[:, 0, :], a["mask_full"]), (masks[:, 1, :], a["mask_window"]),
                    (sinks[:], a["sinks"].partition_broadcast(P).rearrange("p a n -> p (a n)")),
                    (conv[:].rearrange("p a b c d -> p (a b c d)"), a["conv"])])

        two_pi = 6.283185307179586
        c1 = float(np.float32(int(two_pi * 128) / 128))
        c2 = float(np.float32(int((two_pi - c1) * 2 ** 20) / 2 ** 20))
        c3 = float(np.float32(two_pi - c1 - c2))
        magic = 1.5 * 2 ** 23

        def chain(ins):
            m = dve.done(ins)
            dve.wait(m)
            return m
        chain(V.tensor_copy(pos_f[:], pos_i[:]))
        chain(V.tensor_scalar(pos_f[:], pos_f[:], freq[:, 0:1], None, ALU.mult))
        for tab, shift in ((sin_t, 0.0), (cos_t, 0.25)):
            chain(V.tensor_scalar(turns[:], pos_f[:], 1.0 / two_pi, shift, ALU.mult, ALU.add))
            chain(V.tensor_scalar(turns[:], turns[:], magic, None, ALU.add))
            chain(V.tensor_scalar(turns[:], turns[:], magic, None, ALU.subtract))
            chain(V.scalar_tensor_tensor(tab[:], turns[:], -c1, pos_f[:], ALU.mult, ALU.add))
            chain(V.scalar_tensor_tensor(tab[:], turns[:], -c2, tab[:], ALU.mult, ALU.add))
            chain(V.scalar_tensor_tensor(tab[:], turns[:], -c3, tab[:], ALU.mult, ALU.add))
            if shift:
                chain(V.tensor_scalar(tab[:], tab[:], two_pi / 4, None, ALU.add))
            chain(V.tensor_scalar(tab[:], tab[:], float(np.float32(np.pi) - np.float32(3e-7)),
                                  -float(np.float32(np.pi) - np.float32(3e-7)), ALU.min, ALU.max))
            act.wait(Mark(dve, None, dve.start + dve.k))
            m = act.done(A.activation(tab[:], tab[:], ACT.Sin), "tables")
        dve.wait("tables")

        def attention_stage(name, out_name, mask_row, grouped, fresh):
            scope = ExitStack()
            qk_raw = sb(f"{name}_qk_raw", [P, 2, 512], scope=scope)
            qk_cos = sb(f"{name}_qk_cos", [P, 2, 512], scope=scope)
            qk = sb(f"{name}_qk", [P, 2, 512], scope=scope)
            v = sb(f"{name}_v", [P, NT, 256], scope=scope)
            sc = sb(f"{name}_sc", [P, 2, 384], scope=scope)
            pt = sb(f"{name}_pt", [P, 2, 384], scope=scope)
            kw = 1 if grouped else 2
            kv_acts = (mid_hi[:, KD:2 * KD], mid_lo[:, KD:2 * KD]) if grouped else (h_hi, h_lo)
            vw = NT * 64 if grouped else NT * 256
            vt = v[:].rearrange("p a n -> p (a n)")[:, 0:vw].rearrange("p (a n) -> p a n", a=NT)

            def rotate(j, tiles, ready):
                w = tiles * S
                A.wait_ge(*ready)
                act.wait_last_lap(f"rotmm{j}")
                r = act.done(A.copy(qk_raw[:, j, 0:w], bank[j][:, 0:w]))
                dve.wait(r)
                dve.wait_last_lap(f"rot{j}")
                c = dve.done(V.tensor_tensor(
                    qk_cos[:, j, 0:w].rearrange("p (a n) -> p a n", n=S),
                    bank[j][:, 0:w].rearrange("p (a n) -> p a n", n=S),
                    cos_t[:].unsqueeze(1).to_broadcast([P, tiles, S]), ALU.mult), f"rotcos{j}")
                pe.wait(r)
                if j == 0:
                    pe.wait_last_lap("rotsin1")
                else:
                    pe.wait("rotsin0")
                dve.wait(pe.done(T.matmul(bank[3][:, 0:w], rot[:], qk_raw[:, j, 0:w], start=True, stop=True), f"rotmm{j}"))
                if "scores_done" in Lane.names:
                    dve.wait("scores_done")
                m = dve.done(V.tensor_tensor(
                    qk[:, j, 0:w].rearrange("p (a n) -> p a n", n=S),
                    bank[3][:, 0:w].rearrange("p (a n) -> p a n", n=S),
                    sin_t[:].unsqueeze(1).to_broadcast([P, tiles, S]), ALU.mult), f"rotsin{j}")
                dve.wait(m, c)
                dve.done(V.tensor_tensor(qk[:, j, 0:w], qk[:, j, 0:w], qk_cos[:, j, 0:w], ALU.add), f"rot{j}")

            def scores(g, r):
                rows = slice(64 * (r % 2), 64 * (r % 2) + 64)
                q0 = (r // 2) * S
                k0 = 0 if grouped else q0
                if r == 0:
                    pe.wait_last_lap("rot0", "rot1")
                b = bank[4 + r % 2]
                if r >= 2:
                    pe.wait(f"masked{r - 2}")
                else:
                    pe.wait_last_lap(f"masked{r + 2}")
                T.matmul(b[:, 0:P], qk[rows, 0, q0:q0 + P], qk[rows, 1, k0:k0 + P], start=True, stop=True)
                mm = pe.done(T.matmul(b[:, P:384], qk[rows, 0, q0 + P:q0 + S], qk[rows, 1, k0:k0 + S],
                                      start=True, stop=True), "scores_done")
                y = sc[:, r % 2, :]
                dve.wait(mm)
                if r >= 2:
                    dve.wait(f"turned{r - 2}")
                else:
                    dve.wait_last_lap(f"turned{r + 2}")
                m = dve.done(V.scalar_tensor_tensor(y, b[:, 0:384], HD ** -0.5, masks[:, mask_row, :],
                                                    ALU.mult, ALU.add), f"masked{r}")
                dve.wait(m)
                c0 = 8 + 8 * (r % 2)
                dve.done(V.reduce_max(small[:, c0:c0 + 1], y[:, 0:P], AX.X))
                dve.wait(dve.done(V.reduce_max(small[:, c0 + 1:c0 + 2], y[:, P:384], AX.X)))
                neg = small[:, c0 + 2:c0 + 4]
                if grouped:
                    sink = sinks[:, bass.ds(g * GH + r, 1)]
                    m = dve.done(V.tensor_scalar(neg, small[:, c0:c0 + 2], sink, -1.0, ALU.max, ALU.mult))
                else:
                    m = dve.done(V.tensor_scalar(neg, small[:, c0:c0 + 2], -1.0, None, ALU.mult))
                act.wait(m)
                act.done(A.activation(y[:, 0:P], y[:, 0:P], ACT.Exp, bias=small[:, c0 + 2:c0 + 3],
                                      accum_out=small[:, c0 + 4:c0 + 5]))
                m = act.done(A.activation(y[:, P:384], y[:, P:384], ACT.Exp, bias=small[:, c0 + 3:c0 + 4],
                                          accum_out=small[:, c0 + 5:c0 + 6]), f"exp{r}")
                if grouped:
                    act.done(A.activation(small[:, c0 + 6:c0 + 8], neg, ACT.Exp, bias=sink), f"exp{r}")

            def normalize(r):
                y, c0 = sc[:, r % 2, :], 8 + 8 * (r % 2)
                dve.wait(f"exp{r}")
                if grouped:
                    dve.wait(dve.done(V.tensor_tensor(small[:, c0 + 4:c0 + 6], small[:, c0 + 4:c0 + 6],
                                                      small[:, c0 + 6:c0 + 8], ALU.add)))
                dve.wait(dve.done(V.reciprocal(small[:, c0 + 4:c0 + 6], small[:, c0 + 4:c0 + 6])))
                dve.done(V.tensor_scalar(y[:, 0:P], y[:, 0:P], small[:, c0 + 4:c0 + 5], None, ALU.mult))
                dve.done(V.tensor_scalar(y[:, P:384], y[:, P:384], small[:, c0 + 5:c0 + 6], None, ALU.mult),
                         f"probs{r}")

            def turn(r):
                y, z = sc[:, r % 2, :], pt[:, r % 2, :]
                pe.wait(f"probs{r}")
                if r:
                    pe.wait(f"pt{r - 1}")
                else:
                    pe.wait_last_lap(f"pt{GH - 1}")
                for c in range(3):
                    mm = T.transpose(bank[6][:, c * P:(c + 1) * P], y[:, c * P:(c + 1) * P], ident[:])
                act.wait(pe.done(mm, f"turned{r}"))
                if r >= 2:
                    act.wait(f"pv{r - 2}")
                else:
                    act.wait_last_lap(f"pv{r + 2}")
                act.done(A.copy(z, bank[6][:, 0:384]), f"pt{r}")

            def values(r):
                z = pt[:, r % 2, :]
                pe.wait(f"pt{r}")
                if r == 0:
                    pe.wait_last_lap("out_lo", "v_copy")
                d0 = 64 * (r % 2)
                c0 = 0 if grouped else 64 * r
                o = bank[7][d0:d0 + 64, (r // 2) * S:(r // 2 + 1) * S]
                T.matmul(o, vt[:, 0, c0:c0 + 64], z[:, 0:S], start=True, stop=False, skip_group_check=True)
                pe.done(T.matmul(o[:, P:S], vt[:, 1, c0:c0 + 64], z[:, S:384], start=False, stop=True,
                                 skip_group_check=True), f"pv{r}")

            def keep(g):
                o3 = bank[7][:, :].rearrange("p (a n) -> p a n", n=S)
                act.wait(f"pv{GH - 1}")
                hi = mid_hi[:, bass.ds(g * 2, 2), :]
                dve.wait(act.done(A.copy(hi, o3), "out_hi"))
                dve.done(V.tensor_tensor(mid_lo[:, bass.ds(g * 2, 2), :], o3, hi.bitcast(F32), ALU.subtract), "out_lo")

            def heads(g):
                s = [lambda: scores(g, 0), lambda: scores(g, 1)]
                for r in range(GH):
                    s += [lambda r=r: normalize(r), lambda r=r: turn(r)]
                    if r + 2 < GH:
                        s.append(lambda r=r: scores(g, r + 2))
                    s.append(lambda r=r: values(r))
                return s + [lambda: keep(g)]

            def body(g, feed, arrived):
                def begin(s, *free):
                    arrived(s)
                    pe.wait_last_lap(*free)
                later = not isinstance(g, int) or g > 0
                fr = None if later else fresh
                at = lambda s: (unit_done, unit_mark(name, g, s))
                units = feature_major(0, 0, 2, (h_hi, h_lo), lambda: begin(0, "rotcos0"), fresh=fr)
                if grouped:
                    units += [feed]
                    units += feature_major(1, 1, 1, kv_acts, lambda: begin(1, "rotcos1", "v_copy"), width=192, ends=False)
                    units += token_major(1, 2, kv_acts, lambda: None, c0=128, cols=64, width=192)
                    units += [lambda: rotate(0, 2, at(0)), feed, lambda: rotate(1, kw, at(1))]
                    v_ready = at(1)
                else:
                    units += [feed]
                    units += feature_major(1, 1, 2, (h_hi, h_lo), lambda: begin(1, "rotcos1"))
                    units += [feed, lambda: rotate(0, 2, at(0))]
                    tm = token_major(2, 2, (h_hi, h_lo), lambda: begin(2, "v_copy"))
                    units += tm[:2] + [lambda: rotate(1, kw, at(1))] + tm[2:]
                    v_ready = at(2)
                if later:
                    weave((units, 0, 1), (heads(g - 1), 0.1, 0.97))
                else:
                    weave((units, 0, 1))
                A.wait_ge(*v_ready)
                if "pv3" in Lane.names:
                    act.wait("pv3")
                act.done(A.copy(v[:].rearrange("p a n -> p (a n)")[:, 0:vw], bank[2][:, 0:vw]), "v_copy")
            stage(name, body, peel=1)

            marks = {}

            def project_out(lap, feed, arrived):
                banks = [(0, 1), (2, 3)]
                units = []
                for s, (block, n) in enumerate(BY_TILES):
                    def begin(s=s):
                        arrived(s)
                        if s == 0:
                            pe.wait("rotcos0", "rotcos1")
                        if s == 1:
                            pe.wait("v_copy", "rotsin0", "rotsin1")
                        if s == 2:
                            pe.wait("out_lo")
                    u = square_unit(s, block, KD, (mid_hi, mid_lo), banks[n], begin)
                    units.append(u + [feed])
                weave((units[0] + units[1], 0, 1), (heads(GROUPS - 1), 0.05, 0.99))
                weave((units[2] + units[3], 0, 1))
                marks.update(add_residual(banks, lambda t, n: V.wait_ge(unit_done, unit_mark(out_name, lap, 2 + n))))
            stage(out_name, project_out)
            scope.close()
            return marks

        def ffn(tag, layer, fresh):
            scope = ExitStack()
            cv = sb(f"{tag}_cv", [P, 4, S], scope=scope)
            sg = sb(f"{tag}_sg", [P, 2, S], scope=scope)
            gt_hi = sb(f"{tag}_gt_hi", [P, 2, S], F32R, scope=scope)
            gt_lo = sb(f"{tag}_gt_lo", [P, 2, S], F32R, scope=scope)
            acc = [(4, 5), (6, 7)]
            zero_r = zeros(scope)

            def up(arrived, fresh=None):
                steps = []
                for s in range(2):
                    def begin(s=s):
                        arrived(s)
                        pe.wait_last_lap(f"conv{s}")
                    steps += feature_major(s, s, 2, (h_hi, h_lo), begin, fresh=None if s else fresh)
                weave((steps, 0, 1))

            def post(j, jc, st, feed):
                cw = conv[:, layer, bass.ds(jc, 1), :, :].rearrange("p a b c -> p (a b) c")
                for s in range(2):
                    A.wait_ge(unit_done, unit_mark(st, j, s))
                    act.wait_last_lap(f"sg", "gprod")
                    for i in range(2):
                        y = 2 * s + i
                        c = act.done(A.activation(cv[:, y, :], bank[s][:, i * S:(i + 1) * S], ACT.Identity,
                                                  scale=cw[:, y, 2:3], bias=cw[:, y, 3:4]))
                    dve.wait(c)
                    for back in (1, 2):
                        for i in range(2):
                            y = 2 * s + i
                            m = dve.done(V.scalar_tensor_tensor(
                                cv[:, y, back:S], bank[s][:, i * S:(i + 1) * S - back], cw[:, y, 2 - back:3 - back],
                                cv[:, y, back:S], ALU.mult, ALU.add), f"conv{s}")
                        dve.wait(m)
                    if s == 0:
                        act.wait(m)
                        act.done(A.activation(sg[:], cv[:, 0:2, :], ACT.Silu), "sg")
                    feed()
                dve.wait("sg", m)
                m = dve.done(V.tensor_tensor(sg[:], sg[:], cv[:, 2:4, :], ALU.mult), "gprod")

            def split_g(feed):
                act.wait("gprod")
                A.wait_ge(unit_done, Lane.down_value)
                m = act.done(A.copy(gt_hi[:], sg[:]), "gt_hi")
                dve.wait(m)
                dve.done(V.tensor_tensor(gt_lo[:], sg[:], gt_hi[:].bitcast(F32), ALU.subtract), "gt")

            def down(s, arrived, marks=None):
                arrived(s)
                wh, wl = parts_of(s, 2, D)
                for k in range(2):
                    for t, n in CHUNKS:
                        tk, nn = slice(t * P, (t + 1) * P), slice(n * 512, (n + 1) * 512)
                        T.matmul(bank[acc[t][n]][:, :], gt_hi[:, k, tk], wh[:, k, nn], start=False, stop=False, skip_group_check=True)
                        T.matmul(bank[acc[t][n]][:, :], gt_hi[:, k, tk], wl[:, k, nn], start=False, stop=False, skip_group_check=True)
                        mm = T.matmul(bank[acc[t][n]][:, :], gt_lo[:, k, tk], wh[:, k, nn], start=False, stop=True, skip_group_check=True)
                        if marks is not None and k == 1 and (t, n) != CHUNKS[-1]:
                            marks[t, n] = pe.done(mm)
                mm.then_inc(unit_done, 1)

            def first(j, feed, arrived):
                up(arrived, fresh)
                pe.wait("turned", "zeros")
                for t in range(NT):
                    for n in range(2):
                        T.matmul(bank[acc[t][n]][:, :], zero_r[:, 0:P], zero_r[:], start=True, stop=True,
                                 skip_group_check=True)
                post(j, 0, f"{tag}_first", feed)
                Lane.down_value = 0
                split_g(feed)
            stage(f"{tag}_first", first)

            def middle(j, feed, arrived):
                up(arrived)
                pe.wait_last_lap("gt")
                down(2, arrived)
                post(j, j + 1, tag, feed)
                feed()
                Lane.down_value = unit_mark(tag, j, 2)
                split_g(feed)
            stage(tag, middle)
            marks = {}

            def last(j, feed, arrived):
                pe.wait("gt")
                done = {}
                down(0, arrived, done)
                feed(4)

                def ready(t, n):
                    if (t, n) in done:
                        dve.wait(done[t, n])
                    else:
                        V.wait_ge(unit_done, unit_mark(f"{tag}_last", j, 0))
                marks.update(add_residual([(4, 6), (5, 7)], ready))
            stage(f"{tag}_last", last)
            scope.close()
            return marks

        def finish(src):
            act.wait(*[Mark(ln, None, ln.start + ln.k) for ln in (act, dve, pool)])
            A.dma_start(out.rearrange("(t p) d -> p t d", p=P), src).then_inc(out_done, 16)
            A.wait_ge(out_done, 16)

        kv_hi, kv_lo = mid_hi[:, KD:2 * KD], mid_lo[:, KD:2 * KD]
        ready = normed(x, {c: None for c in CHUNKS}, [(0, h_hi, h_lo)])
        marks = attention_stage("attn_a", "wo_a", 0, False, ready)
        if stop == "attn_a":
            finish(x[:])
            return new_plan
        ready = normed(x, marks, [(1, h_hi, h_lo)])
        marks = ffn("ffn_a", 0, ready)
        if stop == "ffn_a":
            finish(x[:])
            return new_plan
        normed(x, marks, [(2, kv_hi, kv_lo), (3, h_hi, h_lo)])
        pe.wait("turned")
        marks = attention_stage("attn_b", "wo_b", 1, True, None)
        ready = normed(x, marks, [(4, h_hi, h_lo)])
        marks = ffn("ffn_b", 1, ready)
        phase_load([(row[:], a["rows"][0:1, :].partition_broadcast(P).rearrange("p a n -> p (a n)"))])
        m = mean_squares(x, marks, wide)
        dve.wait(m)
        marks = {}
        for t, n in CHUNKS:
            marks[t, n] = dve.done(V.scalar_tensor_tensor(chunk(x, t, n), chunk(x, t, n), small[:, 4 + t:5 + t],
                                                          row[:, n * 512:(n + 1) * 512], ALU.mult, ALU.mult), "x")
        if stop == "ffn_b":
            finish(x[:])
            return new_plan
        b1.close()

        b2 = ExitStack()
        ctx.enter_context(b2)
        v_ret = sb("v_ret", [P, NT, B_HEADS * B_DV], scope=b2)
        b3 = ExitStack()
        ctx.enter_context(b3)
        upper, lower = sb("upper", [P, P], scope=b3), sb("lower", [P, P], scope=b3)
        levels = sb("levels", [P, LEVELS, P], scope=b3)
        level0_t = sb("level0_t", [P, P], scope=b3)
        norm_a = sb("norm_a", [P, A_DV], scope=b3)
        conv_a = sb("conv_a", [P, A_HEADS, 4, 4], scope=b3)
        log_bias = sb("log_bias", [P, 2, A_HEADS], scope=b3)
        gate = sb("gate", [P, 6, NT, A_HEADS], scope=b3)
        ba = ExitStack()
        w_ba = sb("w_ba", [P, KD, 2 * A_HEADS], scope=ba)
        ba_hi, ba_lo = sb("ba_hi", [P, KD, 16], F32R, scope=ba), sb("ba_lo", [P, KD, 16], F32R, scope=ba)
        phase_load([(upper[:], a["upper"]), (lower[:], a["lower_strict"]),
                    (levels[:].rearrange("p a n -> p (a n)"), a["levels"]), (level0_t[:], a["level0_t"]),
                    (norm_a[:], a["norm_a"].partition_broadcast(P).rearrange("p a n -> p (a n)")),
                    (conv_a[:].rearrange("p a b c -> p (a b c)"), a["conv_a"]),
                    (w_ba[:].rearrange("p a b -> p (a b)"), a["w_ba"]),
                    (log_bias[:, 0, :], a["a_log"].partition_broadcast(P).rearrange("p a n -> p (a n)")),
                    (log_bias[:, 1, :], a["dt_bias"].partition_broadcast(P).rearrange("p a n -> p (a n)"))], everything())
        ready = normed(x, marks, [(5, h_hi, h_lo)])

        beta, g_log, g_cum, e_cum, t1, t2 = (gate[:, j] for j in range(6))
        chain(V.tensor_copy(ba_hi[:], w_ba[:]))
        m = chain(V.tensor_tensor(ba_lo[:], w_ba[:], ba_hi[:].bitcast(F32), ALU.subtract))
        pe.wait(m, "turned")
        ba_ps = bank[4][:, 0:NT * 16].rearrange("p (t n) -> p t n", t=NT)
        for t in range(NT):
            tk = slice(t * P, (t + 1) * P)
            for k in range(KD):
                mm = three(ba_ps[:, t, :], h_hi[:, k, tk], h_lo[:, k, tk], ba_hi[:, k, :], ba_lo[:, k, :],
                           k == 0, k == KD - 1)
        m = pe.done(mm)
        act.wait(m)
        m = act.done(A.activation(beta, ba_ps[:, :, 0:A_HEADS], ACT.Exp, scale=-1.0))
        dve.wait(m)
        chain(V.tensor_scalar(beta, beta, 1.0, None, ALU.add))
        chain(V.reciprocal(beta, beta))
        chain(V.tensor_tensor(g_log, ba_ps[:, :, A_HEADS:], log_bias[:, 1:2, :].to_broadcast([P, NT, A_HEADS]), ALU.add))
        m = chain(V.scalar_tensor_tensor(t1, g_log, -1.0, g_log, ALU.mult, ALU.max))
        act.wait(m)
        m = act.done(A.activation(t1, t1, ACT.Exp, scale=-1.0))
        act.wait(m)
        m = act.done(A.activation(t1, t1, ACT.Ln, bias=1.0))
        m = act.done(A.activation(log_bias[:, 0, :], log_bias[:, 0, :], ACT.Exp))
        dve.wait(m)
        chain(V.scalar_tensor_tensor(g_log, g_log, 0.0, t1, ALU.max, ALU.add))
        m = chain(V.scalar_tensor_tensor(g_log, g_log, -1.0, log_bias[:, 0:1, :].to_broadcast([P, NT, A_HEADS]),
                                         ALU.mult, ALU.mult))
        pe.wait(m)
        gsum = bank[5][:, 0:NT * A_HEADS].rearrange("p (t n) -> p t n", t=NT)
        for t in range(NT):
            mm = T.matmul(gsum[:, t, :], upper[:], g_log[:, t, :], start=True, stop=True)
        m = pe.done(mm)
        act.wait(m)
        m = act.done(A.activation(e_cum, gsum, ACT.Exp))
        m = act.done(A.copy(g_cum, gsum), "gates")
        for ln in (dve, pe):
            ln.wait("gates")
        ba.close()

        scope = ExitStack()
        wide_f = wide[:].rearrange("p a n -> p (a n)")
        cv = wide_f[:, 0:4 * S].rearrange("p (a n) -> p a n", a=4)
        qkn = wide_f[:, 1024:1536].rearrange("p (a n) -> p a n", a=4)
        qkt = wide_f[:, 1536:2048].rearrange("p (a n) -> p a n", a=4)
        vbeta = row[:, 0:512].rearrange("p (a n) -> p a n", a=NT)
        o = row[:, 512:1024].rearrange("p (a n) -> p a n", a=NT)
        zs = sb("d_z", [P, NT, A_DV], scope=scope)
        sq_junk = sb("d_sq", [P, 512], scope=scope)
        up_dec, lo_dec = sb("d_up_dec", [P, NT, P], scope=scope), sb("d_lo_dec", [P, NT, P], scope=scope)
        e_row = sb("d_e_row", [P, P], scope=scope)
        low = sb("d_low", [P, NT, P], scope=scope)
        low_b = sb("d_low_b", [P, 2, NT, P], scope=scope)
        att = sb("d_att", [P, NT, P], scope=scope)
        xt = sb("d_xt", [P, 4, P], scope=scope)
        z = sb("d_zm", [P, NT, P], scope=scope)
        kb, kdec, qexp, nwt = (sb(n, [P, P], scope=scope) for n in ("d_kb", "d_kdec", "d_qexp", "d_nwt"))
        vn = sb("d_vn", [P, NT, A_DV], scope=scope)
        state = sb("d_state", [P, A_DV], scope=scope)
        ids = ident[:].unsqueeze(1).to_broadcast([P, NT, P])
        two = lambda ap: ap.rearrange("p (a n) -> p a n", a=NT)

        def conv_post(hd, s, b, ready):
            cw = conv_a[:, bass.ds(hd, 1), :, :].rearrange("p a b c -> p (a b) c")
            A.wait_ge(*ready)
            if "flipped" in Lane.names:
                act.wait("flipped", "v_turned")
            for i in range(2):
                y = 2 * s + i
                c = act.done(A.activation(cv[:, y, :], bank[b][:, i * S:(i + 1) * S], ACT.Copy, scale=cw[:, y, 3:4]))
            dve.wait(c)
            for back in (1, 2, 3):
                for i in range(2):
                    y = 2 * s + i
                    m = dve.done(V.scalar_tensor_tensor(
                        cv[:, y, back:S], bank[b][:, i * S:(i + 1) * S - back], cw[:, y, 3 - back:4 - back],
                        cv[:, y, back:S], ALU.mult, ALU.add), f"conv{s}")
                if back < 3:
                    dve.wait(m)

        def inverse_steps(hd):
            h1 = bass.ds(hd, 1)

            def flip_qk():
                pe.wait_last_lap("silu", "att")
                for j in range(4):
                    mm = T.transpose(bank[4][:, j * P:(j + 1) * P], cv[:, j // 2, (j % 2) * P:(j % 2 + 1) * P], ident[:])
                pe.done(mm, "flipped")

            def flip_v():
                for t in range(NT):
                    for f in range(2):
                        mm = T.transpose(bank[5][:, t * A_DV + f * P:t * A_DV + (f + 1) * P],
                                         cv[:, 2 + f, t * P:(t + 1) * P], ident[:])
                pe.done(mm, "v_turned")

            def norms():
                act.wait("flipped")
                act.wait_last_lap("sq_o")
                for j in range(4):
                    m = act.done(A.activation(sq_junk[:, j * P:(j + 1) * P], bank[4][:, j * P:(j + 1) * P], ACT.Square,
                                              accum_out=small[:, 32 + j:33 + j]), "sq_qk")
                pool.wait(m)
                rsqrt_col(36, 32, 4)
                Lane.names["r_qk"] = Mark(pool, Lane.loop, pool.k if Lane.loop else pool.start + pool.k)

            def row_decay():
                dve.wait_last_lap("row_g")
                m = dve.done(V.tensor_copy(small[:, 46:48], g_log[:, :, h1].rearrange("p t a -> p (t a)")))
                pe.wait(m)
                pe.wait_last_lap("inv")
                for t in range(NT):
                    mm = T.matmul(bank[7][:, t * P:(t + 1) * P], small[:, 46 + t:47 + t].to_broadcast([P, P]), upper[:],
                                  start=True, stop=True)
                dve.wait(pe.done(mm, "row_g"))
                dve.wait_last_lap("e_last")
                for t in range(NT):
                    gc = g_cum[:, t, h1]
                    gr = bank[7][:, t * P:(t + 1) * P]
                    dve.done(V.tensor_scalar(up_dec[:, t, :], gr, gc, 0.0, ALU.subtract, ALU.min))
                    dve.done(V.tensor_scalar(lo_dec[:, t, :], gr, gc, 0.0, ALU.subtract, ALU.max))
                m = dve.done(V.tensor_scalar(small[:, 44:45], bank[7][:, P - 1:P], g_cum[:, 0, h1], None, ALU.subtract))
                act.wait(m)
                m = act.done(A.activation(lo_dec[:], lo_dec[:], ACT.Exp, scale=-1.0))
                pool.wait(m)
                pool.done(G.tensor_tensor(lo_dec[:], lo_dec[:], lower[:].unsqueeze(1).to_broadcast([P, NT, P]), ALU.mult), "lo_dec")
                m = act.done(A.activation(up_dec[:], up_dec[:], ACT.Exp))
                pool.wait(m)
                pool.done(G.tensor_tensor(up_dec[:], up_dec[:], upper[:].unsqueeze(1).to_broadcast([P, NT, P]), ALU.mult), "up_dec")
                act.wait_last_lap("qexp")
                act.done(A.activation(e_row[:], bank[7][:, P:S], ACT.Exp), "e_row")
                act.done(A.activation(small[:, 44:45], small[:, 44:45], ACT.Exp), "e_last")

            def scale_qk():
                dve.wait("r_qk")
                for j in range(4):
                    m = dve.done(V.tensor_scalar(qkn[:, j, :], bank[4][:, j * P:(j + 1) * P], small[:, 36 + j:37 + j],
                                                 A_DK ** -0.5 if j < 2 else 1.0, ALU.mult, ALU.mult), "qkn")

            def back_qk():
                pe.wait("qkn")
                for j in range(4):
                    mm = T.transpose(bank[6][:, j * P:(j + 1) * P], qkn[:, j, :], ident[:])
                act.wait(pe.done(mm))
                act.done(A.copy(qkt.rearrange("p a n -> p (a n)"), bank[6][:, :]), "qkt")

            def products():
                pe.wait("qkt")
                for t in range(NT):
                    T.matmul(bank[4][:, t * P:(t + 1) * P], qkt[:, 2 + t, :], qkt[:, 2 + t, :], start=True, stop=True)
                for t in range(NT):
                    mm = T.matmul(bank[4][:, (2 + t) * P:(3 + t) * P], qkt[:, 2 + t, :], qkt[:, t, :], start=True, stop=True)
                dve.wait(pe.done(mm, "qk_products"), "lo_dec")
                for t in range(NT):
                    m = dve.done(V.scalar_tensor_tensor(low[:, t, :], bank[4][:, t * P:(t + 1) * P],
                                                        beta[:, t, h1], lo_dec[:, t, :], ALU.mult, ALU.mult), "low")

            def start_inverse():
                pe.wait("low")
                for t in range(NT):
                    mm = T.transpose(bank[6][:, t * P:(t + 1) * P], low[:, t, :], ident[:])
                m = pe.done(mm)
                dve.wait("low")
                dve.wait_last_lap("v1")
                m1 = dve.done(V.tensor_tensor(xt[:, 2:4, :], low[:], levels[:, 0:1, :].to_broadcast([P, NT, P]), ALU.mult))
                dve.wait(m)
                m2 = dve.done(V.tensor_tensor(xt[:, 0:2, :], two(bank[6][:, 0:S]),
                                              level0_t[:].unsqueeze(1).to_broadcast([P, NT, P]), ALU.mult))
                dve.wait(m1)
                dve.done(V.tensor_tensor(xt[:, 2:4, :], ids, xt[:, 2:4, :], ALU.subtract))
                dve.wait(m2)
                dve.done(V.tensor_tensor(xt[:, 0:2, :], ids, xt[:, 0:2, :], ALU.subtract), "inv")
                blocks(1)
                blocks(2)

            def blocks(b):
                pool.wait("low")
                if b > 2:
                    pool.wait(f"z{b - 2}")
                else:
                    pool.wait_last_lap(f"z{LEVELS - 3 + b}")
                pool.done(G.tensor_tensor(low_b[:, b % 2], low[:], levels[:, b:b + 1, :].to_broadcast([P, NT, P]), ALU.mult),
                          f"blocks{b}")

            def level_a(b):
                pe.wait(f"blocks{b}", "inv")
                for t in range(NT):
                    mm = T.matmul(bank[6][:, t * P:(t + 1) * P], low_b[:, b % 2, t, :], xt[:, t, :], start=True, stop=True)
                m = pe.done(mm, f"z{b}")
                if b + 2 < LEVELS:
                    blocks(b + 2)
                act.wait(m)
                if b > 1:
                    act.wait("zx")
                act.done(A.copy(z[:].rearrange("p a n -> p (a n)"), bank[6][:, 0:S]), "z")

            def level_b(b):
                pe.wait("z")
                for t in range(NT):
                    mm = T.matmul(bank[7][:, t * P:(t + 1) * P], xt[:, 2 + t, :], z[:, t, :], start=True, stop=True)
                w = 2
                if b < LEVELS - 1:
                    w = 4
                    for t in range(NT):
                        mm = T.matmul(bank[7][:, (2 + t) * P:(3 + t) * P], z[:, t, :], xt[:, 2 + t, :], start=True, stop=True)
                dve.wait(pe.done(mm, "zx"))
                dve.done(V.tensor_tensor(xt[:, 0:w, :], xt[:, 0:w, :],
                                         bank[7][:, 0:w * P].rearrange("p (a n) -> p a n", n=P), ALU.subtract), "inv")

            def sides():
                dve.wait("v_turned", "up_dec")
                dve.wait_last_lap("outputs")
                for t in range(NT):
                    dve.done(V.tensor_scalar(vbeta[:, t, :], bank[5][:, t * A_DV:(t + 1) * A_DV],
                                             beta[:, t, h1], None, ALU.mult), "vbeta")
                dve.done(V.tensor_tensor(att[:], two(bank[4][:, 2 * P:4 * P]), up_dec[:], ALU.mult), "att")
                dve.done(V.tensor_scalar(kb[:], qkn[:, 3, :], beta[:, 1, h1], e_cum[:, 1, h1], ALU.mult, ALU.mult), "kb")
                dve.wait("e_last", "e_row", "qkt")
                dve.done(V.tensor_scalar(kdec[:], qkn[:, 2, :], small[:, 44:45], None, ALU.mult), "kdec")
                dve.done(V.tensor_tensor(qexp[:], qkt[:, 1, :], e_row[:], ALU.mult), "qexp")

            steps = [flip_qk, flip_v, norms, row_decay, scale_qk, back_qk, products, start_inverse]
            for b in range(1, LEVELS):
                steps += [lambda b=b: level_a(b), lambda b=b: level_b(b)]
                if b == 2:
                    steps.append(sides)
            return steps

        def output_steps(hd):
            b3_ = bank[3]

            def first_values():
                pe.wait_last_lap("inv", "vbeta", "kb", "mid_lo")
                T.matmul(b3_[:, 0:A_DV], xt[:, 0, :], vbeta[:, 0, :], start=True, stop=True)
                m = pe.done(T.matmul(b3_[:, A_DV:A_DV + P], kb[:], xt[:, 1, :], start=True, stop=True))
                act.wait(m)
                act.wait_last_lap("o_read")
                act.done(A.copy(vn[:, 0, :], b3_[:, 0:A_DV]), "v0")
                act.done(A.activation(nwt[:], b3_[:, A_DV:A_DV + P], ACT.Copy, scale=-1.0), "nwt")

            def first_state():
                pe.wait("nwt")
                pe.wait_last_lap("kdec")
                m = pe.done(T.matmul(b3_[:, 0:A_DV], kdec[:], vn[:, 0, :], start=True, stop=True))
                act.wait(m)
                act.done(A.copy(state[:], b3_[:, 0:A_DV]), "state")

            def second_values():
                pe.wait("state")
                T.matmul(b3_[:, 0:A_DV], xt[:, 1, :], vbeta[:, 1, :], start=True, stop=False)
                m = pe.done(T.matmul(b3_[:, 0:A_DV], nwt[:], state[:], start=False, stop=True), "v1")
                act.wait(m)
                act.done(A.copy(vn[:, 1, :], b3_[:, 0:A_DV]), "vn")

            def outputs():
                pe.wait("vn")
                pe.wait_last_lap("att", "qexp")
                T.matmul(b3_[:, 0:A_DV], att[:, 0, :], vn[:, 0, :], start=True, stop=True)
                T.matmul(b3_[:, A_DV:], qexp[:], state[:], start=True, stop=False)
                m = pe.done(T.matmul(b3_[:, A_DV:], att[:, 1, :], vn[:, 1, :], start=False, stop=True), "outputs")
                act.wait(m)
                if "sq_qk" in Lane.names:
                    act.wait("sq_qk")
                for t in range(NT):
                    m = act.done(A.activation(sq_junk[:, t * A_DV:(t + 1) * A_DV], b3_[:, t * A_DV:(t + 1) * A_DV],
                                              ACT.Square, scale=A_DV ** -0.5, accum_out=small[:, 40 + t:41 + t]), "sq_o")
                pool.wait(m)
                m = rsqrt_col(42, 40, NT)
                dve.wait(m)
                for t in range(NT):
                    m = dve.done(V.scalar_tensor_tensor(o[:, t, :], b3_[:, t * A_DV:(t + 1) * A_DV], small[:, 42 + t:43 + t],
                                                        norm_a[:], ALU.mult, ALU.mult), "o_read")
                dve.wait(m)
                dve.wait_last_lap("zs")
                dve.done(V.tensor_tensor(o, o, zs[:], ALU.mult), "gated")

            def store():
                pe.wait("gated")
                for f in range(2):
                    for t in range(NT):
                        mm = T.transpose(b3_[:, f * S + t * P:f * S + (t + 1) * P], o[:, t, f * P:(f + 1) * P], ident[:])
                m = pe.done(mm, "o_turned")
                o3 = two(b3_[:, :])
                hi = mid_hi[:, bass.ds(hd * 2, 2), :]
                act.wait(m)
                dve.wait(act.done(A.copy(hi, o3)))
                dve.done(V.tensor_tensor(mid_lo[:, bass.ds(hd * 2, 2), :], o3, hi.bitcast(F32), ALU.subtract), "mid_lo")

            return [first_values, first_state, second_values, outputs, store]

        def delta_units(name, hd, feed, arrived, fresh=None):
            at = lambda s: (unit_done, unit_mark(name, hd, s))

            def begin(s, *free):
                arrived(s)
                pe.wait_last_lap(*free)

            def keep_v():
                A.wait_ge(*at(2))
                act.done(A.copy(v_ret[:, :, bass.ds(head * 256, 256)], two(bank[0][:, :])), "v_ret")
            head = hd if name == "delta_first" else hd + 1
            u = feature_major(0, 0, 2, (h_hi, h_lo), lambda: begin(0, "v_ret"), fresh=fresh)
            u += [lambda: conv_post(head, 0, 0, at(0)), feed]
            u += feature_major(1, 1, 2, (h_hi, h_lo), lambda: begin(1, "conv1"))
            u += [lambda: conv_post(head, 1, 1, at(1)), feed]

            def vb_begin():
                arrived(2)
                pe.wait("conv0")
            u += token_major(2, 0, (h_hi, h_lo), vb_begin)
            u += [keep_v, feed]
            return u

        def delta_end(z_ready=None):
            act.wait("conv0", "conv1")
            act.done(A.activation(cv, cv, ACT.Silu), "silu")
            if z_ready:
                silu_z(z_ready)

        def silu_z(z_ready):
            A.wait_ge(*z_ready)
            if "gated" in Lane.names:
                act.wait("gated")
            act.done(A.activation(zs[:].rearrange("p a n -> p (a n)"), bank[2][:, :], ACT.Silu), "zs")

        def z_unit(s, arrived, *free):
            def begin():
                arrived(s)
                pe.wait_last_lap("zs", *free)
            return token_major(s, 2, (h_hi, h_lo), begin)

        def delta_first(lap, feed, arrived):
            weave((delta_units("delta_first", 0, feed, arrived, ready), 0, 1))
            delta_end()
        stage("delta_first", delta_first)

        def delta(lap, feed, arrived):
            units = delta_units("delta", lap, feed, arrived) + z_unit(3, arrived) + [feed]
            if isinstance(lap, int) and lap == 0:
                weave((units, 0, 1), (inverse_steps(lap), 0.02, 0.95))
            else:
                weave((units, 0, 1), (inverse_steps(lap), 0.02, 0.95), (output_steps(lap - 1), 0.03, 0.6))
            delta_end((unit_done, unit_mark("delta", lap, 3)))
        stage("delta", delta, peel=2)
        LAST = A_HEADS - 1

        def delta_gate(lap, feed, arrived):
            units = []

            def keep(n, banks):
                A.wait_ge(unit_done, unit_mark("delta_gate", lap, 2 * n + 1))
                act.wait("kb", "kdec", "qexp", "qk_products")
                for t in (1, 0):
                    act.done(A.activation(chunk(wide, t, n), bank[banks[t]][:, :], ACT.Sigmoid), f"sg{t}")
            for s, (block, n) in enumerate(BY_COLUMNS):
                banks = ((0, 1), (2, 1))[n]

                def begin(s=s):
                    arrived(s)
                    if s == 0:
                        pe.wait("v_ret", "conv1")
                    if s == 2:
                        pe.wait("zs")
                u = square_unit(s, block, KD, (h_hi, h_lo), banks, begin)
                if s == 2:
                    u = u[:2] + [lambda: keep(0, (0, 1)), lambda: pe.wait("sg1")] + u[2:]
                units += u + [feed]
            weave((units, 0, 1), (inverse_steps(LAST), 0.02, 0.85), (output_steps(LAST - 1), 0.03, 0.6))
            keep(1, (2, 1))
        stage("delta_gate", delta_gate)

        br_banks = [(4, 5), (6, 7)]

        def br_a_unit(s, at, arrived, last=False):
            block, n = BR_A[at]

            def begin():
                arrived(s)
                if at == 0:
                    pe.wait("att", "vbeta")
                if at == 3:
                    pe.wait("inv", "e_row", "e_last", "z")
                if block == 3:
                    pe.wait("mid_lo")
            return square_unit(s, block, 2 * KD, (mid_hi, mid_lo), br_banks[n], begin)

        def delta_last(lap, feed, arrived):
            units = z_unit(0, arrived, "sg0", "sg1") + [lambda: silu_z((unit_done, unit_mark("delta_last", lap, 0))), feed]
            for j in range(3):
                units += br_a_unit(1 + j, j, arrived) + [feed]
            weave((units, 0, 1), (output_steps(LAST), 0.02, 0.9))
        stage("delta_last", delta_last)

        def br_a(lap, feed, arrived):
            for s in range(4):
                weave((br_a_unit(s, 3 + s, arrived) + [feed], 0, 1))
        stage("br_a", br_a)

        def br_a_last(lap, feed, arrived):
            weave((br_a_unit(0, 7, arrived) + [feed], 0, 1))
            feed(4)
            for n in range(2):
                V.wait_ge(unit_done, unit_mark("br_a", 0, 3) if n == 0 else unit_mark("br_a_last", 0, 0))
                if n == 0:
                    dve.wait("sg0", "sg1", *everything())
                for t in range(NT):
                    dve.done(V.tensor_tensor(chunk(wide, t, n), chunk(wide, t, n), bank[br_banks[n][t]][:, :], ALU.mult),
                             "mixed")
        stage("br_a_last", br_a_last)
        scope.close()
        b3.close()

        ret = ExitStack()
        ctx.enter_context(ret)
        retain = sb("retain", [P, B_HEADS, 384], scope=ret)
        cos_b, sin_b = sb("cos_b", [P, S], scope=ret), sb("sin_b", [P, S], scope=ret)
        norm_b = sb("norm_b", [P, B_DV], scope=ret)
        qk_rot = sb("r_qk", [P, 2, 2, S], scope=ret)
        sw = row[:, 0:512].rearrange("p (a n) -> p a n", a=2)
        scr = row[:, 512:896]
        gsl = sb("r_g", [P, NT, B_DV], scope=ret)
        ob = sb("r_o", [P, NT, B_DV], scope=ret)
        norm_in = sem("norm_in")
        phase_load([(retain[:].rearrange("p a n -> p (a n)"), a["retain"]), (cos_b[:], a["cos_b"]), (sin_b[:], a["sin_b"])],
                   everything())
        dve.wait(*everything())

        def rotary_b(j, ready):
            V.wait_ge(*ready)
            if "scored" in Lane.names:
                dve.wait("scored")
            u = two(bank[j][:, :])
            dve.done(V.tensor_tensor(qk_rot[:, j], u, cos_b[:].unsqueeze(1).to_broadcast([P, 2, S]), ALU.mult))
            if j:
                dve.wait("rot0")
            else:
                dve.wait_last_lap("rot1")
            dve.done(V.tensor_tensor(sw[:, 0, :], u[:, 1, :], sin_b[:], ALU.mult))
            dve.wait(dve.done(V.tensor_tensor(sw[:, 1, :], u[:, 0, :], sin_b[:], ALU.mult)))
            dve.done(V.tensor_tensor(qk_rot[:, j, 0, :], qk_rot[:, j, 0, :], sw[:, 0, :], ALU.subtract))
            dve.done(V.tensor_tensor(qk_rot[:, j, 1, :], qk_rot[:, j, 1, :], sw[:, 1, :], ALU.add), f"rot{j}")

        def retention_steps(hd, norm_value):
            def score():
                pe.wait_last_lap("rot0", "rot1", "scr", "mid_lo")
                for c0, w, k0, q0 in ((0, S, 0, 0), (S, P, P, P)):
                    for f in range(2):
                        mm = T.matmul(bank[4][:, c0:c0 + w], qk_rot[:, 1, f, k0:k0 + P], qk_rot[:, 0, f, q0:q0 + w],
                                      start=f == 0, stop=f == 1)
                dve.wait(pe.done(mm, "scored"))
                dve.wait_last_lap("o_done")
                dve.done(V.tensor_tensor(scr, bank[4][:, 0:384],
                                         retain[:, bass.ds(hd, 1), :].rearrange("p a n -> p (a n)"), ALU.mult), "scr")

            def output(t):
                pe.wait("scr")
                pe.wait_last_lap("ob")
                vv = [v_ret[:, j, bass.ds(hd * B_DV, B_DV)] for j in range(NT)]
                if t == 0:
                    mm = T.matmul(bank[5][:, :], scr[:, 0:P], vv[0], start=True, stop=True)
                else:
                    T.matmul(bank[6][:, :], scr[:, P:S], vv[0], start=True, stop=False)
                    mm = T.matmul(bank[6][:, :], scr[:, S:384], vv[1], start=False, stop=True)
                act.wait(pe.done(mm, "o_done"))
                act.wait_last_lap("ob_turned")
                act.done(A.activation(ob[:, t, :], bank[5 + t][:, :], ACT.Square, scale=1 / 16,
                                      accum_out=small[:, 40 + t:41 + t]), "ob_sq")

            def scale():
                pool.wait("ob_sq")
                dve.wait(rsqrt_col(42, 40, NT, scale=256.0 / B_DV))
                V.wait_ge(norm_in, norm_value)
                for t in range(NT):
                    dve.done(V.scalar_tensor_tensor(ob[:, t, :], bank[5 + t][:, :], small[:, 42 + t:43 + t],
                                                    norm_b[:], ALU.mult, ALU.mult), "ob")
                dve.wait("ob")
                dve.wait_last_lap("gsl0", "gsl1")
                dve.done(V.tensor_tensor(ob[:], ob[:], gsl[:], ALU.mult), "ob_gated")

            def store(b, f0):
                pe.wait("ob_gated")
                for f in range(f0, f0 + 2):
                    for t in range(NT):
                        mm = T.transpose(bank[b][:, (f - f0) * S + t * P:(f - f0) * S + (t + 1) * P],
                                         ob[:, t, f * P:(f + 1) * P], ident[:])
                act.wait(pe.done(mm, "ob_turned"))
                o3 = two(bank[b][:, :])
                hi = mid_hi[:, bass.ds(hd * 4 + f0, 2), :]
                dve.wait(act.done(A.copy(hi, o3)))
                dve.done(V.tensor_tensor(mid_lo[:, bass.ds(hd * 4 + f0, 2), :], o3, hi.bitcast(F32), ALU.subtract), "mid_lo")
            return [score, lambda: output(0), lambda: output(1), scale, lambda: store(7, 0), lambda: store(4, 2)]

        def load_norm_b(hd):
            if "ob" in Lane.names:
                act.wait("ob")
            A.dma_start(norm_b[:], a["norm_b"][0:1, bass.ds(hd * B_DV, B_DV)].partition_broadcast(P)
                        .rearrange("p a n -> p (a n)")).then_inc(norm_in, 16)

        def retention(hd, feed, arrived):
            at = lambda s: (unit_done, unit_mark("retention", hd, s))
            later = not isinstance(hd, int) or hd > 0

            def begin(s, *free):
                arrived(s)
                pe.wait_last_lap(*free)
            units = feature_major(0, 0, 2, (h_hi, h_lo), lambda: begin(0, "rot0")) + [feed]
            units += feature_major(1, 1, 2, (h_hi, h_lo), lambda: begin(1, "rot1"))
            units += [lambda: rotary_b(0, at(0)), feed]
            g0 = token_major(2, 2, (h_hi, h_lo), lambda: begin(2, "gsl0"))
            units += g0[:2] + [lambda: rotary_b(1, at(1))] + g0[2:] + [feed]
            units += token_major(3, 3, (h_hi, h_lo), lambda: begin(3, "gsl1"))
            if later:
                weave((units, 0, 1), (retention_steps(hd - 1, hd * 16), 0.05, 0.8))
            else:
                weave((units, 0, 1))
            load_norm_b(hd)
            for j in range(2):
                A.wait_ge(*at(2 + j))
                if "ob_gated" in Lane.names:
                    act.wait("ob_gated")
                act.done(A.activation(gsl[:, :, j * 256:(j + 1) * 256], two(bank[2 + j][:, :]), ACT.Silu), f"gsl{j}")
        stage("retention", retention, peel=1)

        sig = v_ret[:].rearrange("p t n -> p (t n)")[:, 0:NT * D].rearrange("p (t n) -> p t n", t=NT)

        def gate_b(lap, feed, arrived):
            units = []
            for s, (block, n) in enumerate(BY_COLUMNS):
                def begin(s=s, n=n):
                    arrived(s)
                    if s == 0:
                        pe.wait("rot0", "rot1")
                    if s == 2:
                        pe.wait("gsl0", "gsl1")
                units += square_unit(s, block, KD, (h_hi, h_lo), [(0, 1), (2, 3)][n], begin) + [feed]
            weave((units, 0, 1), (retention_steps(B_HEADS - 1, B_HEADS * 16), 0.05, 0.8))
            for n in range(2):
                A.wait_ge(unit_done, unit_mark("gate_b", lap, 2 * n + 1))
                act.wait("o_done")
                for t in range(NT):
                    act.done(A.activation(chunk(sig, t, n), bank[2 * n + t][:, :], ACT.Sigmoid), f"sig{n}")
        stage("gate_b", gate_b)

        def br_b(lap, feed, arrived):
            for s in range(4):
                def begin(s=s):
                    arrived(s)
                    if s == 0 and lap == 0:
                        pe.wait("scr", "mid_lo")
                    if s == 0 and lap == 1:
                        pe.wait("ob")
                weave((square_unit(s, s, 2 * KD, (mid_hi, mid_lo), br_banks[lap], begin) + [feed], 0, 1))
            V.wait_ge(unit_done, unit_mark("br_b", lap, 3))
            dve.wait(f"sig{lap}")
            mixed = []
            for t in range(NT):
                mixed.append(dve.done(V.tensor_tensor(chunk(sig, t, lap), chunk(sig, t, lap), bank[br_banks[lap][t]][:, :], ALU.mult)))
            for t in range(NT):
                dve.wait(mixed[t])
                mixed[t] = dve.done(V.tensor_tensor(chunk(wide, t, lap), chunk(wide, t, lap), chunk(sig, t, lap), ALU.add))
            mix_marks.append(tuple(mixed))
        mix_marks = []
        stage("br_b", br_b)
        ret.close()
        b2.close()

        act.wait(*everything())
        pe.wait(*mix_marks[1])
        ready = turned(mix_marks, [(None, h_hi, h_lo)])

        end = ExitStack()
        ctx.enter_context(end)
        junk = sb("junk", [P, NT, D], scope=end)

        def add_normed(banks, wait_ready, which):
            phase_load([(row[:], a["rows"][which:which + 1, :].partition_broadcast(P).rearrange("p a n -> p (a n)"))],
                       everything()[1:3])
            marks = {}
            for t, n in CHUNKS:
                wait_ready(act, t, n)
                marks[t, n] = act.done(A.copy(chunk(wide, t, n), bank[banks[n][t]][:, :]))
            m = mean_squares(wide, marks, junk)
            dve.wait(m)
            for t, n in CHUNKS:
                m = dve.done(V.scalar_tensor_tensor(chunk(wide, t, n), chunk(wide, t, n), small[:, 4 + t:5 + t],
                                                    row[:, n * 512:(n + 1) * 512], ALU.mult, ALU.mult))
                dve.wait(m)
                marks[t, n] = dve.done(V.tensor_tensor(chunk(x, t, n), chunk(x, t, n), chunk(wide, t, n), ALU.add), "x")
            return marks
        marks = {}

        def w_out(lap, feed, arrived):
            for s, (block, n) in enumerate(BY_COLUMNS):
                weave((square_unit(s, block, KD, (h_hi, h_lo), [(0, 1), (2, 3)][n], lambda s=s: arrived(s),
                                   fresh=ready if n == 0 else None) + [feed], 0, 1))
            feed(4)
            marks.update(add_normed([(0, 1), (2, 3)],
                                    lambda ln, t, n: ln.eng.wait_ge(unit_done, unit_mark("w_out", lap, 2 * n + 1)), 1))
        stage("w_out", w_out)
        if stop == "w_out":
            finish(x[:])
            return new_plan
        ready = normed(x, marks, [(6, h_hi, h_lo)])

        rl = sb("m_relu", [P, 2, 2 * S], scope=end)
        sq = sb("m_sq", [P, 2, 2 * S], scope=end)
        gm_hi, gm_lo = sb("gm_hi", [P, 4, S], F32R, scope=end), sb("gm_lo", [P, 4, S], F32R, scope=end)
        acc = [(4, 5), (6, 7)]
        zero_r = zeros(end)

        def m_up(arrived, fresh=None):
            steps = []
            for s in range(2):
                def begin(s=s):
                    arrived(s)
                    pe.wait_last_lap(f"sq{s}")
                steps += feature_major(s, s, 2, (h_hi, h_lo), begin, fresh=None if s else fresh)
            weave((steps, 0, 1))

        def m_post(st, j, feed, down_value):
            for s in range(2):
                A.wait_ge(unit_done, unit_mark(st, j, s))
                act.wait_last_lap(f"sq{s}", "gm")
                m = act.done(A.activation(rl[:, s, :], bank[s][:, :], ACT.Relu))
                dve.wait(m)
                dve.done(V.scalar_tensor_tensor(sq[:, s, :], bank[s][:, :], 0.0, rl[:, s, :], ALU.max, ALU.mult), f"sq{s}")
                feed()
            if down_value is not None:
                feed()
                A.wait_ge(unit_done, down_value)
            act.wait("sq0", "sq1")
            sqv = sq[:].rearrange("p a (b n) -> p (a b) n", n=S)
            m = act.done(A.copy(gm_hi[:], sqv))
            dve.wait(m)
            dve.done(V.tensor_tensor(gm_lo[:], sqv, gm_hi[:].bitcast(F32), ALU.subtract), "gm")

        def m_down(s0, arrived, marks=None):
            for a2 in range(2):
                arrived(s0 + a2)
                wh, wl = parts_of(s0 + a2, 2, D)
                for k in range(2):
                    for t, n in CHUNKS:
                        kk, tk, nn = 2 * a2 + k, slice(t * P, (t + 1) * P), slice(n * 512, (n + 1) * 512)
                        dst = bank[acc[t][n]][:, :]
                        T.matmul(dst, gm_hi[:, kk, tk], wh[:, k, nn], start=False, stop=False, skip_group_check=True)
                        T.matmul(dst, gm_hi[:, kk, tk], wl[:, k, nn], start=False, stop=False, skip_group_check=True)
                        mm = T.matmul(dst, gm_lo[:, kk, tk], wh[:, k, nn], start=False, stop=True, skip_group_check=True)
                        if marks is not None and kk == 3 and (t, n) != CHUNKS[-1]:
                            marks[t, n] = pe.done(mm)
                mm.then_inc(unit_done, 1)

        def m_first(j, feed, arrived):
            m_up(arrived, ready)
            pe.wait("turned", "zeros")
            for t in range(NT):
                for n in range(2):
                    T.matmul(bank[acc[t][n]][:, :], zero_r[:, 0:P], zero_r[:], start=True, stop=True, skip_group_check=True)
            m_post("mlp_first", j, feed, None)
        stage("mlp_first", m_first)

        def m_middle(j, feed, arrived):
            m_up(arrived)
            pe.wait_last_lap("gm")
            m_down(2, arrived)
            m_post("mlp", j, feed, unit_mark("mlp", j, 3))
        stage("mlp", m_middle)

        def m_last(j, feed, arrived):
            pe.wait("gm")
            done = {}
            m_down(0, arrived, done)

            def wait_ready(ln, t, n):
                if (t, n) in done:
                    ln.wait(done[t, n])
                else:
                    ln.eng.wait_ge(unit_done, unit_mark("mlp_last", j, 1))
            add_normed([(4, 6), (5, 7)], wait_ready, 2)
        stage("mlp_last", m_last)
        finish(x[:])
    return new_plan


class _Guess(dict):
    def __init__(self, lanes):
        super().__init__()
        self.lanes = lanes

    def __missing__(self, key):
        return self.lanes[0], 1


def arrays(i):
    def column(v):
        return v.reshape(KD, P).T
    out = {
        "x": i["x"][0], "positions": i["positions"], "stream": weight_stream(i),
        "gains": np.stack([column(v) for v in (
            i["attn_norm"][0], i["ffn_norm"][0], i["kv_norm"], i["attn_norm"][1], i["ffn_norm"][1],
            i["norm_mix_pre_2"][0], i["norm_mlp_pre_2"][0])], 1).reshape(P, -1),
        "rows": np.stack([i["final_norm"], i["norm_mix_post_2"][0], i["norm_mlp_post_2"][0]]),
        "norm_a": i["norm_a_2"], "norm_b": i["norm_b_2"],
        "sinks": i["sinks_b"], "a_log": i["a_log_2"], "dt_bias": i["dt_bias_2"],
        "w_ba": cols_unit(i["w_in_2"][0], (C_BA, 2 * A_HEADS)),
    }
    taps = np.concatenate([i["conv_w"], i["conv_b"][:, None, :]], 1)
    taps = taps.reshape(2, 4, 2, F_LAPS, 2, P)
    out["conv"] = taps.transpose(5, 0, 3, 2, 4, 1).reshape(P, -1)
    ca = i["conv_a_2"][0].reshape(4, 32, P)
    per_head = np.stack([ca[:, 0:8], ca[:, 8:16], ca[:, 16:32:2], ca[:, 17:32:2]], 2)
    out["conv_a"] = per_head.transpose(3, 1, 2, 0).reshape(P, -1)
    out.update(constants())
    return {k: np.ascontiguousarray(v) for k, v in out.items()}


def kernel(**inputs):
    import concourse.bacc as bacc
    from concourse.bass_utils import run_bass_kernel_spmd

    host = arrays({k: np.asarray(v) for k, v in inputs.items()})

    def build(plan):
        nc = bacc.Bacc("TRN2", target_bir_lowering=False, num_devices=1)
        dram = {n: nc.dram_tensor(n, v.shape, mybir.dt.from_np(v.dtype), kind="ExternalInput").ap()
                for n, v in host.items()}
        out = nc.dram_tensor("out", (S, D), F32, kind="ExternalOutput").ap()
        return nc, program(nc, dram, out, plan)

    _, plan = build({})
    nc, again = build(plan)
    assert plan == again
    r = run_bass_kernel_spmd(nc, [host], core_ids=[0])
    return r.results[0]["out"].reshape(1, S, D)
```

```python
from contextlib import ExitStack, contextmanager

import numpy as np

import concourse.bass as bass
from concourse import mybir

F32 = mybir.dt.float32
F32R = mybir.dt.float32r
I32 = mybir.dt.int32
ALU = mybir.AluOpType
ACT = mybir.ActivationFunctionType
AX = mybir.AxisListType
ENG = mybir.EngineType

P = 128
S = 256
NT = S // P
D = 1024
KD = D // P
EPS = 1e-6
NEG = -1e30
HEADS, HD, KV_HEADS, ROT = 16, 64, 4, 16
GROUPS = 4
GH = HEADS // GROUPS
F_TILES = 2816 // P
F_LAPS = F_TILES // 2
A_HEADS, A_DK, A_DV = 8, 128, 256
B_HEADS, B_DK, B_DV = 4, 256, 512
RET_CHUNK = 64
FF2 = 4096
M_LAPS = FF2 // (4 * P)
UNIT = 2048
SLOTS = 4
LEAD = 64
LEVELS = 7

C_QA, C_KA, C_VA, C_ZA, C_BA, C_QB, C_KB, C_VB, C_GB, C_GA2, C_GB2 = (
    0, 1024, 2048, 4096, 6144, 6160, 7184, 8208, 10256, 12304, 13328)


def constants():
    r = np.arange(P)
    row, col = r[:, None], r[None, :]
    f = np.float32
    out = {}
    out["ident"] = (row == col).astype(f)
    rot = np.zeros((P, P), f)
    for h in range(0, P, HD):
        for j in range(ROT // 2):
            rot[h + j + ROT // 2, h + j] = -1.0
            rot[h + j, h + j + ROT // 2] = 1.0
    out["rot"] = rot
    freq = np.zeros((P, 1), f)
    inv = np.power(f(500000.0), (-np.arange(0, ROT, 2).astype(f) / f(ROT))).astype(f)
    for h in range(0, P, HD):
        freq[h:h + ROT, 0] = np.concatenate([inv, inv])
    out["freq"] = freq
    causal = np.where(col <= row, 0.0, NEG).astype(f)
    band = np.where(col > row, 0.0, NEG).astype(f)
    out["mask_full"] = np.concatenate([causal, np.zeros((P, P), f), causal], 1)
    out["mask_window"] = np.concatenate([causal, band, causal], 1)
    out["upper"] = (row <= col).astype(f)
    out["lower_strict"] = (row > col).astype(f)
    lev = []
    for b in range(LEVELS):
        w = 1 << b
        lev.append(((row // (2 * w) == col // (2 * w)) & (row // w % 2 == 1) & (col // w % 2 == 0)).astype(f))
    out["levels"] = np.concatenate(lev, 1)
    out["level0_t"] = lev[0].T.copy()
    ret = []
    for h in range(B_HEADS):
        lg = np.log1p(-np.exp2(f(-5.0 - h))).astype(f)
        m, c = np.arange(S)[:, None], np.arange(S)[None, :]
        w = np.exp(lg * np.abs(c - m).astype(f)).astype(f) * (m // RET_CHUNK <= c // RET_CHUNK) * f(B_DK ** -0.5)
        ret.append(np.concatenate([w[0:P, :], w[P:S, P:S]], 1).astype(f))
    out["retain"] = np.concatenate(ret, 1)
    fb = np.power(f(10000.0), (-np.arange(0, B_DK, 2).astype(f) / f(B_DK))).astype(f)
    ang = (np.arange(S).astype(f)[None, :] * fb[:, None]).astype(f)
    out["cos_b"], out["sin_b"] = np.cos(ang).astype(f), np.sin(ang).astype(f)
    return {k: np.ascontiguousarray(v, f) for k, v in out.items()}


def cols_unit(w, *starts_and_widths):
    w = np.concatenate([w[:, a:a + n] for a, n in starts_and_widths], 1)
    return w.reshape(KD, P, -1).transpose(1, 0, 2).reshape(P, -1)


def rows_unit(w, k, kn, n, nn):
    return w[k * P:(k + kn) * P, n:n + nn].reshape(kn, P, nn).transpose(1, 0, 2).reshape(P, -1)


def square_units(w, k_blocks):
    return [rows_unit(w, 4 * k, 4, 512 * n, 512) for k, n in k_blocks]


BY_COLUMNS = [(0, 0), (1, 0), (0, 1), (1, 1)]
BR_A = [(0, 0), (1, 0), (2, 0), (0, 1), (1, 1), (2, 1), (3, 0), (3, 1)]
BR_B = [(k, n) for n in range(2) for k in range(4)]


def output_units(w):
    return square_units(w, [(0, 0), (0, 1)]) + [rows_unit(w, k, 2, 0, D) for k in (4, 6)]


def ffn_units(w_up, w_down):
    up = [[cols_unit(w_up, (256 * j, 256)), cols_unit(w_up, (F_TILES * P + 256 * j, 256))] for j in range(F_LAPS)]
    down = [[rows_unit(w_down, 2 * j, 2, 0, D)] for j in range(F_LAPS)]
    out = list(up[0])
    for j in range(1, F_LAPS):
        out += up[j] + down[j - 1]
    return out + down[-1]


def weight_stream(i):
    u = []
    for g in range(GROUPS):
        u += [cols_unit(i["w_qkv_a"][0], (part * D + 256 * g, 256)) for part in range(3)]
    u += output_units(i["w_o_a"][0])
    u += ffn_units(i["w_up"][0], i["w_down"][0])
    for g in range(GROUPS):
        u.append(cols_unit(i["w_q_b"][0], (256 * g, 256)))
        kv = [i["w_kv_b"][:, c:c + HD] for c in (HD * g, HD * g, (KV_HEADS + g) * HD)]
        u.append(cols_unit(np.concatenate(kv + [np.zeros((D, HD), np.float32)], 1), (0, 256)))
    u += output_units(i["w_o_b"][0])
    u += ffn_units(i["w_up"][1], i["w_down"][1])
    w = i["w_in_2"][0]
    for h in range(A_HEADS):
        u += [cols_unit(w, (C_QA + P * h, P), (C_KA + P * h, P)), cols_unit(w, (C_VA + 256 * h, 256)),
              cols_unit(w, (C_VB + 256 * h, 256))]
        if h:
            u.append(cols_unit(w, (C_ZA + 256 * (h - 1), 256)))
    u += square_units(w[:, C_GA2:C_GA2 + D], BY_COLUMNS)
    u.append(cols_unit(w, (C_ZA + 256 * (A_HEADS - 1), 256)))
    u += square_units(i["w_br_a_2"][0], BR_A)
    for h in range(B_HEADS):
        u += [cols_unit(w, (C_QB + 256 * h, 256)), cols_unit(w, (C_KB + 256 * h, 256)),
              cols_unit(w, (C_GB + 512 * h, 256)), cols_unit(w, (C_GB + 512 * h + 256, 256))]
    u += square_units(w[:, C_GB2:C_GB2 + D], BY_COLUMNS)
    u += square_units(i["w_br_b_2"][0], BR_B)
    u += square_units(i["w_out_2"][0], BY_COLUMNS)
    up = [[cols_unit(i["w_up_2"][0], (512 * j, 256)), cols_unit(i["w_up_2"][0], (512 * j + 256, 256))]
          for j in range(M_LAPS)]
    down = [[rows_unit(i["w_down_2"][0], 4 * j + 2 * a, 2, 0, D) for a in range(2)] for j in range(M_LAPS)]
    u += up[0]
    for j in range(1, M_LAPS):
        u += up[j] + down[j - 1]
    u += down[-1]
    return np.stack(u)


STREAM = [("attn_a", GROUPS, 3), ("wo_a", 1, 4),
          ("ffn_a_first", 1, 2), ("ffn_a", F_LAPS - 1, 3), ("ffn_a_last", 1, 1),
          ("attn_b", GROUPS, 2), ("wo_b", 1, 4),
          ("ffn_b_first", 1, 2), ("ffn_b", F_LAPS - 1, 3), ("ffn_b_last", 1, 1),
          ("delta_first", 1, 3), ("delta", A_HEADS - 1, 4), ("delta_gate", 1, 4), ("delta_last", 1, 4),
          ("br_a", 1, 4), ("br_a_last", 1, 1),
          ("retention", B_HEADS, 4), ("gate_b", 1, 4), ("br_b", 2, 4), ("w_out", 1, 4),
          ("mlp_first", 1, 2), ("mlp", M_LAPS - 1, 4), ("mlp_last", 1, 2)]

LATE = {"attn_a": 1, "attn_b": 1, "ffn_a_first": 1, "ffn_b_first": 1, "mlp_first": 1,
        "delta_first": 2, "delta": 1, "delta_gate": 1, "retention": 1,
        "wo_a": 2, "wo_b": 2, "delta_last": 1, "gate_b": 1, "w_out": 3}


PLACES = {
    "a_heads": (0.089, 0.143, 0.155, 0.237, 0.291, 0.36, 0.392, 0.445, 0.525, 0.565, 0.665, 0.674, 0.729, 0.772,
        0.857, 0.919, 1),
    "a_rot_q": (0.43, 0.578),
    "a_rot_k": (0.706, 0.848),
    "a_feed": (0.047, 0.417, 0.88),
    "b_heads": (0.066, 0.108, 0.164, 0.204, 0.26, 0.316, 0.373, 0.402, 0.433, 0.551, 0.561, 0.621, 0.707, 0.75,
        0.807, 0.875, 1.037),
    "b_rot_q": (0.563, 0.848),
    "b_rot_k": (0.878, 1.084, 1.138),
    "b_feed": (0.164, 0.745, 1.323),
    "a_out_heads": (0.175, 0.229, 0.23, 0.299, 0.353, 0.413, 0.429, 0.485, 0.549, 0.567, 0.707, 0.736, 0.736,
        0.756, 0.773, 0.822, 0.961),
    "a_out_feed": (-0.207, 0.152, 0.482),
    "b_out_heads": (0.055, 0.111, 0.163, 0.215, 0.273, 0.274, 0.313, 0.416, 0.523, 0.584, 0.758, 0.759, 0.76,
        0.77, 0.832, 0.883, 0.884),
    "b_out_feed": (0.253, 0.372, 0.922),
    "d_conv_qk": (0.217, 0.272, 0.356, 0.36, 0.397),
    "d_conv_v": (0.567, 0.655, 0.733, 0.764, 0.765),
    "d_inverse": (0.027, 0.073, 0.073, 0.163, 0.164, 0.254, 0.299, 0.344, 0.389, 0.435, 0.471, 0.525, 0.571,
        0.624, 0.661, 0.706, 0.751, 0.839, 0.884, 0.929, 0.974),
    "d_outputs": (0.017, 0.092, 0.222, 0.379, 0.513),
    "first_gates": (0.293, 0.504, 0.854),
    "first_conv_qk": (0.408, 0.491, 0.634, 0.634, 0.641),
    "first_conv_v": (0.752, 0.785, 0.827, 0.869, 0.911),
    "first_feed": (-1.15, -0.041, 0.291, 0.609, 0.759),
    "d_keep": (0.716,),
    "d_feed": (0.103, 0.375, 0.604, 0.844),
    "g_inverse": (0.02, 0.85),
    "g_outputs": (0.03, 0.6),
    "g_feed": (0.08, 0.3, 0.55, 0.8),
    "l_outputs": (0.02, 0.9),
    "l_feed": (0.08, 0.35, 0.6, 0.85),
    "r_rot0": (0.27, 0.32),
    "r_rot1": (0.52, 0.58),
    "r_steps": (0.03, 0.8),
    "r_feed": (0.08, 0.38, 0.62, 0.86),
    "rg_steps": (0.05, 0.8),
    "rg_feed": (0.08, 0.3, 0.55, 0.8),
}


def places(key, n):
    p = PLACES[key]
    if len(p) == n:
        return list(p)
    lo, hi = p
    return [lo + (hi - lo) * (j + 0.5) / n for j in range(n)]


class Mark:

    def __init__(self, lane, loop, offset):
        self.lane, self.loop, self.offset = lane, loop, offset


class Lane:

    def __init__(self, eng, sem):
        self.eng, self.sem = eng, sem
        self.start = 0
        self.k = 0

    def done(self, ins, name=None):
        ins.then_inc(self.sem, 1)
        self.k += 1
        m = Mark(self, Lane.loop, self.k if Lane.loop else self.start + self.k)
        if name:
            Lane.names[name] = m
            if Lane.loop:
                Lane.loop.seen[name] = (self, self.k)
        return m

    def wait(self, *marks):
        latest = {}
        for m in marks:
            if isinstance(m, str):
                m = Lane.names[m]
            if m is None or (m.lane is self and self.eng is Lane.pe_eng):
                continue
            key = (m.lane, m.loop is not None and m.loop is Lane.loop)
            if key not in latest or place(m) > place(latest[key]):
                latest[key] = m
        for m in latest.values():
            self.eng.wait_ge(m.lane.sem, value_of(m))

    def wait_last_lap(self, *names):
        if Lane.loop is None:
            self.wait(*[n for n in names if n in Lane.names])
            return
        latest = {}
        for n in names:
            Lane.loop.entry.append((self, n))
            lane, k = Lane.loop.plan_names[n]
            if lane is not self or self.eng is not Lane.pe_eng:
                latest[lane] = max(k, latest.get(lane, 0))
        for lane, k in latest.items():
            base = Lane.loop.starts[lane] + k - Lane.loop.per[lane]
            self.eng.wait_ge(lane.sem, Lane.loop.i * Lane.loop.per[lane] + base)


def place(m):
    return m.offset if m.loop is None or m.loop is Lane.loop else value_of(m)


def value_of(m):
    if m.loop is None:
        return m.offset
    lp = m.loop
    if lp is Lane.loop:
        return lp.i * lp.per[m.lane] + (lp.starts[m.lane] + m.offset)
    return (lp.n - 1) * lp.per[m.lane] + lp.starts[m.lane] + m.offset


class Loop:
    pass


Lane.loop = None
Lane.names = {}


def program(nc, a, out, plan):
    new_plan = {}
    with ExitStack() as ctx:
        def sb(name, shape, dt=F32, scope=ctx):
            name = f"sb_{name}"
            return scope.enter_context(nc.sbuf_tensor(name, shape, dt))

        def sem(name):
            return ctx.enter_context(nc.semaphore(name))

        pe, act, dve, pool = (Lane(e, sem(n)) for e, n in (
            (nc.tensor, "pe_done"), (nc.scalar, "act_done"), (nc.vector, "dve_done"), (nc.gpsimd, "pool_done")))
        LANES = (pe, act, dve, pool)
        for ln in LANES:
            ln.eng.sem_inc(ln.sem, LEAD)
            ln.start = LEAD
        Lane.pe_eng = nc.tensor
        Lane.loop, Lane.names = None, {}
        T, A, V, G = nc.tensor, nc.scalar, nc.vector, nc.gpsimd

        @contextmanager
        def laps(tag, n):
            lp = Loop()
            lp.n = n
            known = plan.get(tag, {"per": [1000] * 4, "names": {}})
            lp.per = dict(zip(LANES, known["per"]))
            lp.plan_names = {k: (LANES[x], y) for k, (x, y) in known["names"].items()}
            if not known["names"]:
                lp.plan_names = FirstPass(LANES)
            lp.starts = {ln: ln.start + ln.k for ln in LANES}
            lp.seen, lp.entry = {}, []
            for x, name in known.get("entry", ()):
                if name in Lane.names:
                    m, (lane, k) = Lane.names[name], lp.plan_names[name]
                    if m.lane is not lane or value_of(m) > lp.starts[lane] + k - lp.per[lane]:
                        LANES[x].wait(m)
            for ln in LANES:
                ln.start, ln.k = ln.start + ln.k, 0
            with nc.Fori(0, n, engines=[ENG.PE, ENG.Activation, ENG.DVE, ENG.Pool]) as i:
                lp.i = i
                Lane.loop = lp
                yield i
            Lane.loop = None
            new_plan[tag] = {"per": [ln.k for ln in LANES],
                             "entry": sorted({(LANES.index(x), y) for x, y in lp.entry}),
                             "names": {k: (LANES.index(x), y) for k, (x, y) in lp.seen.items()}}
            for ln in LANES:
                ln.start, ln.k = ln.start + n * ln.k, 0

        raw = sb("raw", [P, SLOTS, UNIT])
        w_hi = sb("w_hi", [P, SLOTS, UNIT], F32R)
        w_lo = sb("w_lo", [P, SLOTS, UNIT], F32R)
        raw_in = [sem(f"raw_in{r}") for r in range(SLOTS)]
        hi_done, lo_done = sem("hi_done"), sem("lo_done")
        unit_done = sem("unit_done")

        x = sb("x", [P, NT, D])
        x_in = [sem(f"x_in{t}") for t in range(NT)]
        ident = sb("ident", [P, P])
        gains = sb("gains", [P, 7, KD])
        ident_in = sem("ident_in")

        class Stage:
            pass

        info, number, slot, uses, last_unit = {}, 0, 0, [0] * SLOTS, [None] * SLOTS
        for name, n, r in STREAM:
            st = info[name] = Stage()
            st.first, st.laps, st.units = number, n, r
            st.slots = [(slot + s) % SLOTS for s in range(r)]
            st.uses = [uses[b] for b in st.slots]
            st.before = [last_unit[b] for b in st.slots]
            for s, b in enumerate(st.slots):
                uses[b] += n
                last_unit[b] = number + (n - 1) * r + s
            number, slot = number + n * r, (slot + r) % SLOTS
        slots_now = [None]

        def wait_last_unit(eng, semaphore, name, lap, s, first):
            st = info[name]
            if not first:
                eng.wait_ge(semaphore, lap * st.units + (st.first + s - st.units + 1))
            elif st.before[s] is not None:
                eng.wait_ge(semaphore, st.before[s] + 1)

        for t in range(NT):
            nc.sync.dma_start(x[:, t, :], a["x"][t * P:(t + 1) * P, :]).then_inc(x_in[t], 16)
        nc.sync.dma_start(ident[:], a["ident"]).then_inc(ident_in, 16)
        nc.sync.dma_start(gains[:], a["gains"].rearrange("p (a k) -> p a k", k=KD)).then_inc(ident_in, 16)
        for name, n, r in STREAM:
            st = info[name]

            def load(lap, s, first, st=st, name=name):
                wait_last_unit(nc.sync, lo_done, name, lap, s, first)
                nc.sync.dma_start(raw[:, st.slots[s], :], a["stream"][bass.ds(lap * st.units + (st.first + s), 1)]
                                  .rearrange("u p n -> (u p) n")).then_inc(raw_in[st.slots[s]], 16)
            for s in range(r):
                load(0, s, True)
            if n > 1:
                with nc.sync.Fori(1, n) as lap:
                    for s in range(r):
                        load(lap, s, False)

        order = [x[0] for x in STREAM]

        HALF = UNIT // 2

        def split_hi(name, lap, s, first, half):
            st = info[name]
            b, c = st.slots[s], slice(half * HALF, (half + 1) * HALF)
            if half == 0:
                wait_last_unit(A, unit_done, name, lap, s, first)
                A.wait_ge(raw_in[b], (lap + (st.uses[s] + 1)) * 16)
            A.copy(w_hi[:, b, c], raw[:, b, c]).then_inc(hi_done, 1)

        def split_lo(name, lap, s, half):
            st = info[name]
            b, c = st.slots[s], slice(half * HALF, (half + 1) * HALF)
            V.wait_ge(hi_done, lap * (2 * st.units) + (2 * (st.first + s) + half + 1))
            ins = V.tensor_tensor(w_lo[:, b, c], raw[:, b, c], w_hi[:, b, c].bitcast(F32), ALU.subtract)
            if half:
                ins.then_inc(lo_done, 1)

        class Feed:

            def __init__(self, name, lap, last):
                def job(name, lap, s, first):
                    hi = [lambda h=h: split_hi(name, lap, s, first, h) for h in range(2)]
                    return hi, [lambda h=h: split_lo(name, lap, s, h) for h in range(2)]

                self.jobs = []
                if name is not None:
                    r = info[name].units
                    first = isinstance(lap, int) and lap == 0
                    self.jobs += [job(name, lap, s, first) for s in range(r - LATE.get(name, 0), r)]
                if last:
                    nxt = order.index(name) + 1 if name is not None else 0
                    name, lap = (order[nxt] if nxt < len(order) else None), 0
                else:
                    lap = lap + 1
                if name is not None:
                    r = info[name].units
                    self.jobs += [job(name, lap, s, last) for s in range(r - LATE.get(name, 0))]

            def __call__(self, n=1):
                for _ in range(n):
                    if self.jobs:
                        hi, lo = self.jobs.pop(0)
                        for f in hi + lo:
                            f()

            def at(self, key):
                out = []
                for p in PLACES[key]:
                    if self.jobs:
                        hi, lo = self.jobs.pop(0)
                        out += [(hi, p, p + 0.06), (lo, p + 0.05, p + 0.13)]
                return out

        def stage(name, body, peel=0):
            st = info[name]
            n = st.laps
            slots_now[0] = st.slots

            def run(lap, last):
                def arrived(s):
                    T.wait_ge(lo_done, lap * st.units + (st.first + s + 1))
                feed = Feed(name, lap, last)
                body(lap, feed, arrived)
                feed(2 * SLOTS)
            for lap in range(peel):
                run(lap, False)
            if n - peel > 2:
                with laps(name, n - 1 - peel) as i:
                    run(i + peel if peel else i, False)
            else:
                for lap in range(peel, n - 1):
                    run(lap, False)
            run(n - 1, True)

        def weave(*parts):
            order = []
            for c, part in enumerate(parts):
                steps = part[0]
                if isinstance(part[1], str):
                    at = places(part[1], len(steps))
                else:
                    at = [part[1] + (part[2] - part[1]) * (j + 0.5) / len(steps) for j in range(len(steps))]
                order += [(p, c, j, f) for j, (p, f) in enumerate(zip(at, steps))]
            for *_, f in sorted(order, key=lambda x: x[:3]):
                f()

        bank = [ctx.enter_context(nc.psum_tensor(f"bank{b}", [P, 512], F32)) for b in range(8)]
        h_hi = sb("h_hi", [P, KD, S], F32R)
        h_lo = sb("h_lo", [P, KD, S], F32R)
        mid_hi = sb("mid_hi", [P, 2 * KD, S], F32R)
        mid_lo = sb("mid_lo", [P, 2 * KD, S], F32R)
        wide = sb("wide", [P, NT, D])
        row = sb("row", [P, D])
        small = sb("small", [P, 64])
        POOL_CONST = {v: j for j, v in enumerate((-0.5, EPS, 256.0 / B_DV))}
        pool_const = sb("pool_const", [P, len(POOL_CONST), 4])
        tables_in, out_done = sem("tables_in"), sem("out_done")
        for v, j in POOL_CONST.items():
            pool.wait(pool.done(G.memset(pool_const[:, j, :], v)))

        phase_loads = [0]
        phase_in = sem("phase_in")

        def phase_load(pairs, after=()):
            act.wait(*after)
            for dst, src in pairs:
                A.dma_start(dst, src).then_inc(phase_in, 16)
                phase_loads[0] += 16
            return phase_loads[0]

        def phase_ready(value, *lanes):
            for ln in lanes:
                ln.eng.wait_ge(phase_in, value)

        def row_of(which):
            return [(row[:], a["rows"][which:which + 1, :].partition_broadcast(P).rearrange("p a n -> p (a n)"))]

        def three(out_ap, l_hi, l_lo, r_hi, r_lo, start, stop, **kw):
            T.matmul(out_ap, l_hi, r_hi, start=start, stop=False, **kw)
            T.matmul(out_ap, l_hi, r_lo, start=False, stop=False, **kw)
            return T.matmul(out_ap, l_lo, r_hi, start=False, stop=stop, **kw)

        def parts_of(s, k, width):
            n, s = k * width, slots_now[0][s]
            return (w_hi[:, s, 0:n].rearrange("p (k n) -> p k n", k=k), w_lo[:, s, 0:n].rearrange("p (k n) -> p k n", k=k))

        def fresh_wait(fresh, k):
            if fresh and k % 2 == 0:
                pe.wait(fresh[k // 2])

        def feature_major(s, b, tiles, acts, before, width=256, fresh=None, ends=True):
            wh, wl = parts_of(s, KD, width)

            def step(j, k0):
                if j == k0 == 0:
                    before()
                for k in range(k0, k0 + 4):
                    if j == 0:
                        fresh_wait(fresh, k)
                    mm = three(bank[b][:, j * S:(j + 1) * S], wh[:, k, j * P:(j + 1) * P],
                               wl[:, k, j * P:(j + 1) * P], acts[0][:, k, :], acts[1][:, k, :], k == 0, k == KD - 1)
                if ends and (j, k0) == (tiles - 1, 4):
                    mm.then_inc(unit_done, 1)
            return [lambda j=j, k0=k0: step(j, k0) for j in range(tiles) for k0 in (0, 4)]

        def token_major(s, b, acts, before, c0=0, cols=256, width=256):
            wh, wl = parts_of(s, KD, width)

            def step(t, k0):
                if t == k0 == 0:
                    before()
                o, tk = bank[b][:, t * cols:(t + 1) * cols], slice(t * P, (t + 1) * P)
                for k in range(k0, k0 + 4):
                    mm = three(o, acts[0][:, k, tk], acts[1][:, k, tk], wh[:, k, c0:c0 + cols], wl[:, k, c0:c0 + cols],
                               k == 0, k == KD - 1)
                if (t, k0) == (NT - 1, 4):
                    mm.then_inc(unit_done, 1)
            return [lambda t=t, k0=k0: step(t, k0) for t in range(NT) for k0 in (0, 4)]

        def square_unit(s, block, kt, acts, banks, before, fresh=None):
            wh, wl = parts_of(s, 4, 512)

            def step(t, k0):
                if t == k0 == 0:
                    before()
                tk = slice(t * P, (t + 1) * P)
                for k in range(k0, k0 + 2):
                    kk = 4 * block + k
                    if t == 0:
                        fresh_wait(fresh, kk)
                    mm = three(bank[banks[t]][:, :], acts[0][:, kk, tk], acts[1][:, kk, tk], wh[:, k, :], wl[:, k, :],
                               kk == 0, kk == kt - 1)
                if (t, k0) == (NT - 1, 2):
                    mm.then_inc(unit_done, 1)
            return [lambda t=t, k0=k0: step(t, k0) for t in range(NT) for k0 in (0, 2)]

        def unit_mark(name_of_stage, lap, s):
            st = info[name_of_stage]
            return lap * st.units + (st.first + s + 1)

        def rsqrt_col(dst, src, n, halves=False, scale=None):
            d = small[:, dst:dst + n]
            s0 = small[:, src:src + n]
            if halves:
                pair = small[:, src:src + 2 * n].rearrange("p (t a) -> p t a", a=2)
                pool.wait(pool.done(G.tensor_tensor(d, pair[:, :, 0], pair[:, :, 1], ALU.add)))
                s0 = d
            if scale:
                pool.wait(pool.done(G.tensor_tensor(d, s0, pool_const[:, POOL_CONST[scale], 0:n], ALU.mult)))
                s0 = d
            pool.wait(pool.done(G.tensor_tensor(d, s0, pool_const[:, POOL_CONST[EPS], 0:n], ALU.add)))
            return pool.done(G.tensor_tensor(d, d, pool_const[:, POOL_CONST[-0.5], 0:n], ALU.pow))

        def zeros(scope):
            z = sb(f"zeros{len(zero_tiles)}", [P, 512], F32R, scope=scope)
            zero_tiles.append(z)
            pool.wait(*everything())
            pool.done(G.memset(z[:].bitcast(F32), 0.0), "zeros")
            return z
        zero_tiles = []

        TR = [4, 5, 6, 7]
        CHUNKS = [(0, 0), (1, 0), (0, 1), (1, 1)]

        def chunk(buf, t, n):
            return buf[:, t, n * 512:(n + 1) * 512]

        def mean_squares(src, marks, junk, loads=None):
            for t, n in sorted(CHUNKS) if loads else CHUNKS:
                act.wait(marks[t, n])
                if loads:
                    A.wait_ge(loads[t], 16)
                m = act.done(A.activation(chunk(junk, t, n), chunk(src, t, n), ACT.Square, scale=D ** -0.5,
                                          accum_out=small[:, 2 * t + n:2 * t + n + 1]))
            pool.wait(m)
            return rsqrt_col(4, 0, NT, halves=True)

        def turned(marks, targets, pairs=range(4)):
            ready = []
            for b in pairs:
                pe.wait(*marks[b // 2])
                for k in range(2 * b, 2 * b + 2):
                    for t in range(NT):
                        c = (k % 2) * S + t * P
                        mm = T.transpose(bank[TR[b]][:, c:c + P], wide[:, t, k * P:(k + 1) * P], ident[:])
                act.wait(pe.done(mm))
                for k in range(2 * b, 2 * b + 2):
                    for g, hi, lo in targets:
                        u = bank[TR[b]][:, (k % 2) * S:(k % 2 + 1) * S]
                        if g is None:
                            m = act.done(A.copy(hi[:, k, :], u))
                        else:
                            m = act.done(A.activation(hi[:, k, :], u, ACT.Copy, scale=gains[:, g, k:k + 1]))
                dve.wait(m)
                for k in range(2 * b, 2 * b + 2):
                    for g, hi, lo in targets:
                        u = bank[TR[b]][:, (k % 2) * S:(k % 2 + 1) * S]
                        if g is None:
                            m = dve.done(V.tensor_tensor(lo[:, k, :], u, hi[:, k, :].bitcast(F32), ALU.subtract))
                        else:
                            m = dve.done(V.scalar_tensor_tensor(lo[:, k, :], u, gains[:, g, k:k + 1],
                                                                hi[:, k, :].bitcast(F32), ALU.mult, ALU.subtract))
                ready.append(m)
            Lane.names["turned"] = m
            return ready

        def normed(src, m, targets, between=None):
            act.wait(m)
            dve.wait(m)
            scaled = []
            for n in range(2):
                m0 = act.done(A.activation(chunk(wide, 0, n), chunk(src, 0, n), ACT.Copy, scale=small[:, 4:5]))
                m1 = dve.done(V.tensor_scalar(chunk(wide, 1, n), chunk(src, 1, n), small[:, 5:6], None, ALU.mult))
                scaled.append((m0, m1))
            if between:
                between()
            return turned(scaled, targets)

        def add_residual(banks, wait_ready):
            marks = {}
            for t, n in CHUNKS:
                wait_ready(t, n)
                marks[t, n] = dve.done(V.tensor_tensor(chunk(x, t, n), bank[banks[n][t]][:, :], chunk(x, t, n), ALU.add))
            Lane.names["x"] = marks[1, 1]
            return marks

        def everything():
            return [Mark(ln, None, ln.start + ln.k) for ln in LANES]

        b1 = ExitStack()
        ctx.enter_context(b1)
        cos_t, sin_t = sb("cos_t", [P, S], scope=b1), sb("sin_t", [P, S], scope=b1)
        rot = sb("rot", [P, P], scope=b1)
        freq = sb("freq", [P, 1], scope=b1)
        pos_i, pos_f = sb("pos_i", [P, S], I32, scope=b1), sb("pos_f", [P, S], scope=b1)
        turns = sb("turns", [P, S], scope=b1)
        masks = sb("masks", [P, 2, 384], scope=b1)
        sinks = sb("sinks", [P, HEADS], scope=b1)
        conv = sb("conv", [P, 2, F_LAPS, 4, 4], scope=b1)
        A.dma_start(freq[:], a["freq"]).then_inc(tables_in, 16)
        A.dma_start(pos_i[:], a["positions"].partition_broadcast(P).rearrange("p a n -> p (a n)")).then_inc(tables_in, 16)

        two_pi = 6.283185307179586
        c1 = float(np.float32(int(two_pi * 128) / 128))
        c2 = float(np.float32(int((two_pi - c1) * 2 ** 20) / 2 ** 20))
        c3 = float(np.float32(two_pi - c1 - c2))
        magic = 1.5 * 2 ** 23

        def chain(ins):
            m = dve.done(ins)
            dve.wait(m)
            return m
        V.wait_ge(tables_in, 32)
        chain(V.tensor_copy(pos_f[:], pos_i[:]))
        chain(V.tensor_scalar(pos_f[:], pos_f[:], freq[:, 0:1], None, ALU.mult))

        def angles(tab, shift):
            chain(V.tensor_scalar(turns[:], pos_f[:], 1.0 / two_pi, shift, ALU.mult, ALU.add))
            chain(V.tensor_scalar(turns[:], turns[:], magic, None, ALU.add))
            chain(V.tensor_scalar(turns[:], turns[:], magic, None, ALU.subtract))
            chain(V.scalar_tensor_tensor(tab[:], turns[:], -c1, pos_f[:], ALU.mult, ALU.add))
            chain(V.scalar_tensor_tensor(tab[:], turns[:], -c2, tab[:], ALU.mult, ALU.add))
            chain(V.scalar_tensor_tensor(tab[:], turns[:], -c3, tab[:], ALU.mult, ALU.add))
            if shift:
                chain(V.tensor_scalar(tab[:], tab[:], two_pi / 4, None, ALU.add))
            chain(V.tensor_scalar(tab[:], tab[:], float(np.float32(np.pi) - np.float32(3e-7)),
                                  -float(np.float32(np.pi) - np.float32(3e-7)), ALU.min, ALU.max))
            Lane.names["angles"] = Mark(dve, None, dve.start + dve.k)
        angles(sin_t, 0.0)

        m = mean_squares(x, {c: None for c in CHUNKS}, wide, x_in)
        for t in range(NT):
            V.wait_ge(x_in[t], 16)
        feed0 = Feed(None, -1, True)

        def between():
            for ln in (pe, act, dve):
                ln.eng.wait_ge(ident_in, 32)
            feed0()
        ready = normed(x, m, [(0, h_hi, h_lo)], between)
        feed0()
        in_b1 = phase_load([(rot[:], a["rot"]),
                            (masks[:, 0, :], a["mask_full"]), (masks[:, 1, :], a["mask_window"]),
                            (sinks[:], a["sinks"].partition_broadcast(P).rearrange("p a n -> p (a n)")),
                            (conv[:].rearrange("p a b c d -> p (a b c d)"), a["conv"])] + row_of(0))
        angles(cos_t, 0.25)
        act.wait("angles")
        for tab in (sin_t, cos_t):
            act.done(A.activation(tab[:], tab[:], ACT.Sin), "tables")
        feed0(SLOTS)
        dve.wait("tables")

        def attention_stage(name, out_name, mask_row, grouped, fresh):
            scope = ExitStack()
            qk_raw = sb(f"{name}_qk_raw", [P, 2, 512], scope=scope)
            qk_cos = sb(f"{name}_qk_cos", [P, 2, 512], scope=scope)
            qk = sb(f"{name}_qk", [P, 2, 512], scope=scope)
            v = sb(f"{name}_v", [P, NT, 256], scope=scope)
            sc = sb(f"{name}_sc", [P, 2, 384], scope=scope)
            pt = sb(f"{name}_pt", [P, 2, 384], scope=scope)
            kw = 1 if grouped else 2
            kv_acts = (mid_hi[:, KD:2 * KD], mid_lo[:, KD:2 * KD]) if grouped else (h_hi, h_lo)
            vw = NT * 64 if grouped else NT * 256
            vt = v[:].rearrange("p a n -> p (a n)")[:, 0:vw].rearrange("p (a n) -> p a n", a=NT)

            def rotate(j, tiles, ready):
                w = tiles * S
                wide_copy = 512 if grouped else w

                def first():
                    A.wait_ge(*ready)
                    act.wait_last_lap(f"rotmm{j}", *(["v_turned"] if grouped and j else []))
                    dve.wait(act.done(A.copy(qk_raw[:, j, 0:wide_copy], bank[j][:, 0:wide_copy]), f"raw{j}"))
                    dve.wait_last_lap(f"rot{j}")
                    dve.done(V.tensor_tensor(
                        qk_cos[:, j, 0:w].rearrange("p (a n) -> p a n", n=S),
                        bank[j][:, 0:w].rearrange("p (a n) -> p a n", n=S),
                        cos_t[:].unsqueeze(1).to_broadcast([P, tiles, S]), ALU.mult), f"rotcos{j}")

                def second():
                    pe.wait(f"raw{j}")
                    if "rotmm0" not in Lane.names:
                        phase_ready(in_b1, pe)
                    if j == 0:
                        pe.wait_last_lap("rotsin1")
                    else:
                        pe.wait("rotsin0")
                    dve.wait(pe.done(T.matmul(bank[3][:, 0:w], rot[:], qk_raw[:, j, 0:w], start=True, stop=True), f"rotmm{j}"))
                    if "scores_done" in Lane.names:
                        dve.wait("scores_done")
                    m = dve.done(V.tensor_tensor(
                        qk[:, j, 0:w].rearrange("p (a n) -> p a n", n=S),
                        bank[3][:, 0:w].rearrange("p (a n) -> p a n", n=S),
                        sin_t[:].unsqueeze(1).to_broadcast([P, tiles, S]), ALU.mult), f"rotsin{j}")
                    dve.wait(m, f"rotcos{j}")
                    dve.done(V.tensor_tensor(qk[:, j, 0:w], qk[:, j, 0:w], qk_cos[:, j, 0:w], ALU.add), f"rot{j}")
                return [first, second]

            def turn_v():
                pe.wait("raw1")
                pe.wait_last_lap("v_copy")
                for t in range(NT):
                    mm = T.transpose(bank[2][:, t * P:(t + 1) * P], qk_raw[:, 1, S + t * P:S + (t + 1) * P], ident[:])
                pe.done(mm, "v_turned")

            def scores(g, r):
                rows = slice(64 * (r % 2), 64 * (r % 2) + 64)
                q0 = (r // 2) * S
                k0 = 0 if grouped else q0
                if r == 0:
                    pe.wait_last_lap("rot0", "rot1")
                b = bank[4 + r % 2]
                if r >= 2:
                    pe.wait(f"masked{r - 2}")
                else:
                    pe.wait_last_lap(f"masked{r + 2}")
                T.matmul(b[:, 0:P], qk[rows, 0, q0:q0 + P], qk[rows, 1, k0:k0 + P], start=True, stop=True)
                mm = pe.done(T.matmul(b[:, P:384], qk[rows, 0, q0 + P:q0 + S], qk[rows, 1, k0:k0 + S],
                                      start=True, stop=True), "scores_done")
                y = sc[:, r % 2, :]
                dve.wait(mm)
                if r >= 2:
                    dve.wait(f"turned{r - 2}")
                else:
                    dve.wait_last_lap(f"turned{r + 2}")
                m = dve.done(V.scalar_tensor_tensor(y, b[:, 0:384], HD ** -0.5, masks[:, mask_row, :],
                                                    ALU.mult, ALU.add), f"masked{r}")
                dve.wait(m)
                c0 = 8 + 8 * (r % 2)
                dve.done(V.reduce_max(small[:, c0:c0 + 1], y[:, 0:P], AX.X))
                dve.wait(dve.done(V.reduce_max(small[:, c0 + 1:c0 + 2], y[:, P:384], AX.X)))
                neg = small[:, c0 + 2:c0 + 4]
                if grouped:
                    sink = sinks[:, bass.ds(g * GH + r, 1)]
                    m = dve.done(V.tensor_scalar(neg, small[:, c0:c0 + 2], sink, -1.0, ALU.max, ALU.mult))
                else:
                    m = dve.done(V.tensor_scalar(neg, small[:, c0:c0 + 2], -1.0, None, ALU.mult))
                act.wait(m)
                act.done(A.activation(y[:, 0:P], y[:, 0:P], ACT.Exp, bias=small[:, c0 + 2:c0 + 3],
                                      accum_out=small[:, c0 + 4:c0 + 5]))
                m = act.done(A.activation(y[:, P:384], y[:, P:384], ACT.Exp, bias=small[:, c0 + 3:c0 + 4],
                                          accum_out=small[:, c0 + 5:c0 + 6]), f"exp{r}")
                if grouped:
                    act.done(A.activation(small[:, c0 + 6:c0 + 8], neg, ACT.Exp, bias=sink), f"exp{r}")

            def normalize(r):
                y, c0 = sc[:, r % 2, :], 8 + 8 * (r % 2)
                dve.wait(f"exp{r}")
                if grouped:
                    dve.wait(dve.done(V.tensor_tensor(small[:, c0 + 4:c0 + 6], small[:, c0 + 4:c0 + 6],
                                                      small[:, c0 + 6:c0 + 8], ALU.add)))
                dve.wait(dve.done(V.reciprocal(small[:, c0 + 4:c0 + 6], small[:, c0 + 4:c0 + 6])))
                dve.done(V.tensor_scalar(y[:, 0:P], y[:, 0:P], small[:, c0 + 4:c0 + 5], None, ALU.mult))
                dve.done(V.tensor_scalar(y[:, P:384], y[:, P:384], small[:, c0 + 5:c0 + 6], None, ALU.mult),
                         f"probs{r}")

            def turn(r):
                y, z = sc[:, r % 2, :], pt[:, r % 2, :]
                pe.wait(f"probs{r}")
                if r:
                    pe.wait(f"pt{r - 1}")
                else:
                    pe.wait_last_lap(f"pt{GH - 1}")
                for c in range(3):
                    mm = T.transpose(bank[6][:, c * P:(c + 1) * P], y[:, c * P:(c + 1) * P], ident[:])
                act.wait(pe.done(mm, f"turned{r}"))
                if r >= 2:
                    act.wait(f"pv{r - 2}")
                else:
                    act.wait_last_lap(f"pv{r + 2}")
                act.done(A.copy(z, bank[6][:, 0:384]), f"pt{r}")

            def values(r):
                z = pt[:, r % 2, :]
                pe.wait(f"pt{r}")
                if r == 0:
                    pe.wait_last_lap("out_lo", "v_copy")
                d0 = 64 * (r % 2)
                c0 = 0 if grouped else 64 * r
                o = bank[7][d0:d0 + 64, (r // 2) * S:(r // 2 + 1) * S]
                T.matmul(o, vt[:, 0, c0:c0 + 64], z[:, 0:S], start=True, stop=False, skip_group_check=True)
                pe.done(T.matmul(o[:, P:S], vt[:, 1, c0:c0 + 64], z[:, S:384], start=False, stop=True,
                                 skip_group_check=True), f"pv{r}")

            def keep(g):
                o3 = bank[7][:, :].rearrange("p (a n) -> p a n", n=S)
                act.wait(f"pv{GH - 1}")
                hi = mid_hi[:, bass.ds(g * 2, 2), :]
                dve.wait(act.done(A.copy(hi, o3), "out_hi"))
                dve.done(V.tensor_tensor(mid_lo[:, bass.ds(g * 2, 2), :], o3, hi.bitcast(F32), ALU.subtract), "out_lo")

            def heads(g):
                s = [lambda: scores(g, 0), lambda: scores(g, 1)]
                for r in range(GH):
                    s += [lambda r=r: normalize(r), lambda r=r: turn(r)]
                    if r + 2 < GH:
                        s.append(lambda r=r: scores(g, r + 2))
                    s.append(lambda r=r: values(r))
                return s + [lambda: keep(g)]

            def body(g, feed, arrived):
                def begin(s, *free):
                    arrived(s)
                    pe.wait_last_lap(*free)
                later = not isinstance(g, int) or g > 0
                fr = None if later else fresh
                at = lambda s: (unit_done, unit_mark(name, g, s))
                q = feature_major(0, 0, 2, (h_hi, h_lo), lambda: begin(0, "rotcos0"), fresh=fr)
                rot_q, rot_k = rotate(0, 2, at(0)), rotate(1, kw, at(1))
                if grouped:
                    k = feature_major(1, 1, 2, kv_acts, lambda: begin(1, "rotcos1"))
                    units = q + k
                    more = [(rot_q, "b_rot_q"), (rot_k + [turn_v], "b_rot_k")]
                    feeds = feed.at("b_feed")
                else:
                    k = feature_major(1, 1, 2, (h_hi, h_lo), lambda: begin(1, "rotcos1"))
                    units = q + k + token_major(2, 2, (h_hi, h_lo), lambda: begin(2, "v_copy"))
                    more = [(rot_q, "a_rot_q"), (rot_k, "a_rot_k")]
                    feeds = feed.at("a_feed")
                if later:
                    weave((units, 0, 1), (heads(g - 1), "b_heads" if grouped else "a_heads"), *more, *feeds)
                else:
                    weave((units, 0, 1), *more, *feeds)
                    phase_ready(in_b1, act, dve)
                if grouped:
                    act.wait("v_turned")
                else:
                    A.wait_ge(*at(2))
                if "pv3" in Lane.names:
                    act.wait("pv3")
                if grouped:
                    act.done(A.copy(vt, bank[2][:, 0:NT * P].rearrange("p (a n) -> p a n", a=NT)[:, :, 0:HD]), "v_copy")
                else:
                    act.done(A.copy(v[:].rearrange("p a n -> p (a n)"), bank[2][:, :]), "v_copy")
            stage(name, body, peel=1)

            marks = {}

            def project_out(lap, feed, arrived):
                banks = [(0, 1), (2, 3)]
                units = []
                for s in range(2):
                    def begin(s=s):
                        arrived(s)
                        if s == 0:
                            pe.wait("rotcos0", "rotcos1")
                        if s == 1:
                            pe.wait("v_copy", "rotsin0", "rotsin1")
                    units += square_unit(s, 0, KD, (mid_hi, mid_lo), banks[s], begin)
                done = {}

                def two_tiles(s, k0):
                    wh, wl = parts_of(s, 2, D)

                    def step(t, n):
                        tk, nn = slice(t * P, (t + 1) * P), slice(n * 512, (n + 1) * 512)
                        if (t, n) == CHUNKS[0]:
                            arrived(s)
                        for k in range(2):
                            mm = three(bank[banks[n][t]][:, :], mid_hi[:, k0 + k, tk], mid_lo[:, k0 + k, tk],
                                       wh[:, k, nn], wl[:, k, nn], False, k0 + k == KD - 1)
                        if (t, n) == CHUNKS[-1]:
                            mm.then_inc(unit_done, 1)
                        elif s == 3:
                            done[t, n] = pe.done(mm)
                    return [lambda t=t, n=n: step(t, n) for t, n in CHUNKS]
                weave((units + two_tiles(2, 4), 0, 1), (heads(GROUPS - 1), f"{out_name[-1]}_out_heads"),
                      *feed.at(f"{out_name[-1]}_out_feed"))
                pe.wait("out_lo")
                weave((two_tiles(3, 6), 0, 1))

                def ready(t, n):
                    if (t, n) in done:
                        dve.wait(done[t, n])
                    else:
                        V.wait_ge(unit_done, unit_mark(out_name, lap, 3))
                marks.update(add_residual(banks, ready))
            stage(out_name, project_out)
            scope.close()
            return marks

        def ffn(tag, layer, fresh):
            scope = ExitStack()
            cv = sb(f"{tag}_cv", [P, 4, S], scope=scope)
            sg = sb(f"{tag}_sg", [P, 2, S], scope=scope)
            parts, last_parts = ([sb(f"{tag}_{p}_{b}", [P, 2, S], F32R, scope=scope) for p in ("hi", "lo")]
                                 for b in ("all", "last"))
            acc = [(4, 5), (6, 7)]
            zero_r = zeros(scope)

            def up(arrived, fresh=None, b0=0, free="conv"):
                steps = []
                for s in range(2):
                    def begin(s=s):
                        arrived(s)
                        if free:
                            pe.wait_last_lap(f"{free}{s}")
                    steps += feature_major(s, b0 + s, 2, (h_hi, h_lo), begin, fresh=None if s else fresh)
                weave((steps, 0, 1))

            def post(j, jc, st, feed, b0=0):
                cw = conv[:, layer, bass.ds(jc, 1), :, :].rearrange("p a b c -> p (a b) c")
                for s in range(2):
                    A.wait_ge(unit_done, unit_mark(st, j, s))
                    act.wait_last_lap(f"sg", "gprod")
                    for i in range(2):
                        y = 2 * s + i
                        c = act.done(A.activation(cv[:, y, :], bank[b0 + s][:, i * S:(i + 1) * S], ACT.Identity,
                                                  scale=cw[:, y, 2:3], bias=cw[:, y, 3:4]))
                    dve.wait(c)
                    for back in (1, 2):
                        for i in range(2):
                            y = 2 * s + i
                            m = dve.done(V.scalar_tensor_tensor(
                                cv[:, y, back:S], bank[b0 + s][:, i * S:(i + 1) * S - back], cw[:, y, 2 - back:3 - back],
                                cv[:, y, back:S], ALU.mult, ALU.add), f"conv{s}" if b0 == 0 else None)
                        dve.wait(m)
                    if s == 0:
                        act.wait(m)
                        act.done(A.activation(sg[:], cv[:, 0:2, :], ACT.Silu), "sg")
                    feed()
                dve.wait("sg", m)
                m = dve.done(V.tensor_tensor(sg[:], sg[:], cv[:, 2:4, :], ALU.mult), "gprod")

            def split_g(g, free=None):
                act.wait("gprod")
                if free is not None:
                    A.wait_ge(unit_done, free)
                dve.wait(act.done(A.copy(g[0][:], sg[:])))
                dve.done(V.tensor_tensor(g[1][:], sg[:], g[0][:].bitcast(F32), ALU.subtract), "gt")

            def down(s, g, arrived, marks=None):
                arrived(s)
                wh, wl = parts_of(s, 2, D)
                for k in range(2):
                    for t, n in CHUNKS:
                        tk, nn = slice(t * P, (t + 1) * P), slice(n * 512, (n + 1) * 512)
                        mm = three(bank[acc[t][n]][:, :], g[0][:, k, tk], g[1][:, k, tk], wh[:, k, nn], wl[:, k, nn],
                                   False, True, skip_group_check=True)
                        if marks is not None and k == 1 and (t, n) != CHUNKS[-1]:
                            marks[t, n] = pe.done(mm)
                mm.then_inc(unit_done, 1)

            def first(j, feed, arrived):
                feed(3)
                up(arrived, fresh, 2, None)
                pe.wait("turned", "zeros")
                for t in range(NT):
                    for n in range(2):
                        T.matmul(bank[acc[t][n]][:, :], zero_r[:, 0:P], zero_r[:], start=True, stop=True,
                                 skip_group_check=True)
                post(j, 0, f"{tag}_first", feed, 2)
                split_g(parts)
            stage(f"{tag}_first", first)

            def middle(j, feed, arrived):
                up(arrived)
                pe.wait_last_lap("gt")
                down(2, parts, arrived)
                post(j, j + 1, tag, feed)
                if isinstance(j, int) and j == info[tag].laps - 1:
                    split_g(last_parts)
                    return
                feed()
                split_g(parts, unit_mark(tag, j, 2))
            stage(tag, middle, peel=1)
            marks = {}

            def last(j, feed, arrived):
                pe.wait("gt")
                done = {}
                down(0, last_parts, arrived, done)
                feed(4)

                def ready(t, n):
                    if (t, n) in done:
                        dve.wait(done[t, n])
                    else:
                        V.wait_ge(unit_done, unit_mark(f"{tag}_last", j, 0))
                marks.update(add_residual([(4, 6), (5, 7)], ready))
            stage(f"{tag}_last", last)
            scope.close()
            return marks

        kv_hi, kv_lo = mid_hi[:, KD:2 * KD], mid_lo[:, KD:2 * KD]
        marks = attention_stage("attn_a", "wo_a", 0, False, ready)
        ready = normed(x, mean_squares(x, marks, wide), [(1, h_hi, h_lo)])
        marks = ffn("ffn_a", 0, ready)
        ready = normed(x, mean_squares(x, marks, wide), [(2, kv_hi, kv_lo), (3, h_hi, h_lo)])
        marks = attention_stage("attn_b", "wo_b", 1, True, ready)
        ready = normed(x, mean_squares(x, marks, wide), [(4, h_hi, h_lo)])
        marks = ffn("ffn_b", 1, ready)
        ffn_over = everything()
        b1.close()

        b2 = ExitStack()
        ctx.enter_context(b2)
        v_ret = sb("v_ret", [P, NT, B_HEADS * B_DV], scope=b2)
        b3 = ExitStack()
        ctx.enter_context(b3)
        upper, lower = sb("upper", [P, P], scope=b3), sb("lower", [P, P], scope=b3)
        levels = sb("levels", [P, LEVELS, P], scope=b3)
        level0_t = sb("level0_t", [P, P], scope=b3)
        norm_a = sb("norm_a", [P, A_DV], scope=b3)
        conv_a = sb("conv_a", [P, A_HEADS, 4, 4], scope=b3)
        log_bias = sb("log_bias", [P, 2, A_HEADS], scope=b3)
        gate = sb("gate", [P, 5, NT, A_HEADS], scope=b3)
        scope = ExitStack()
        sq_junk = sb("d_sq", [P, 512], scope=scope)
        w_ba = sq_junk[:, 0:P].rearrange("p (k n) -> p k n", k=KD)
        ba_hi, ba_lo = (sb(n, [P, KD, 2 * A_HEADS], F32R, scope=scope)[:] for n in ("ba_hi", "ba_lo"))
        m = mean_squares(x, marks, wide)
        in_b3 = phase_load([(upper[:], a["upper"]), (lower[:], a["lower_strict"]),
                    (levels[:].rearrange("p a n -> p (a n)"), a["levels"]), (level0_t[:], a["level0_t"]),
                    (norm_a[:], a["norm_a"].partition_broadcast(P).rearrange("p a n -> p (a n)")),
                    (conv_a[:].rearrange("p a b c -> p (a b c)"), a["conv_a"]),
                    (sq_junk[:, 0:P], a["w_ba"]),
                    (log_bias[:, 0, :], a["a_log"].partition_broadcast(P).rearrange("p a n -> p (a n)")),
                    (log_bias[:, 1, :], a["dt_bias"].partition_broadcast(P).rearrange("p a n -> p (a n)"))], ffn_over)
        dve.wait(m)
        marks = {}
        for t, n in CHUNKS:
            marks[t, n] = dve.done(V.scalar_tensor_tensor(chunk(x, t, n), chunk(x, t, n), small[:, 4 + t:5 + t],
                                                          row[:, n * 512:(n + 1) * 512], ALU.mult, ALU.mult), "x")

        ready = normed(x, mean_squares(x, marks, wide), [(5, h_hi, h_lo)])
        phase_ready(in_b3, act, dve, pe, pool)

        gate_t = row[0:2 * A_HEADS, 0:S]
        beta, g_log, g_cum, e_cum, t1 = (gate[:, j] for j in range(5))

        def gates_project():
            chain(V.tensor_copy(ba_hi, w_ba))
            m = chain(V.tensor_tensor(ba_lo, w_ba, ba_hi.bitcast(F32), ALU.subtract))
            pe.wait(m, "turned")
            n = 2 * A_HEADS
            for k in range(KD):
                mm = three(bank[5][0:n, 0:S], ba_hi[:, k, :], ba_lo[:, k, :], h_hi[:, k, :], h_lo[:, k, :], k == 0, k == KD - 1)
            act.wait(pe.done(mm))
            act.done(A.copy(gate_t, bank[5][0:n, 0:S]), "gate_t")

        def gates():
            n = 2 * A_HEADS
            pe.wait("gate_t")
            ba_ps = bank[4][:, 0:NT * n].rearrange("p (t n) -> p t n", t=NT)
            for t in range(NT):
                mm = T.matmul(ba_ps[:, t, :], gate_t[:, t * P:(t + 1) * P], ident[0:n, 0:n], start=True, stop=True)
            act.wait(pe.done(mm))
            m = act.done(A.activation(beta, ba_ps[:, :, 0:A_HEADS], ACT.Exp, scale=-1.0))
            dve.wait(m)
            chain(V.tensor_scalar(beta, beta, 1.0, None, ALU.add))
            chain(V.reciprocal(beta, beta))
            chain(V.tensor_tensor(g_log, ba_ps[:, :, A_HEADS:], log_bias[:, 1:2, :].to_broadcast([P, NT, A_HEADS]), ALU.add))
            m = chain(V.scalar_tensor_tensor(t1, g_log, -1.0, g_log, ALU.mult, ALU.max))
            act.wait(m)
            m = act.done(A.activation(t1, t1, ACT.Exp, scale=-1.0))
            act.done(A.activation(log_bias[:, 0, :], log_bias[:, 0, :], ACT.Exp))
            act.wait(m)
            dve.wait(act.done(A.activation(t1, t1, ACT.Ln, bias=1.0)))
            chain(V.scalar_tensor_tensor(g_log, g_log, 0.0, t1, ALU.max, ALU.add))
            chain(V.scalar_tensor_tensor(g_log, g_log, -1.0, log_bias[:, 0:1, :].to_broadcast([P, NT, A_HEADS]),
                                         ALU.mult, ALU.mult))
            Lane.names["g_log"] = Mark(dve, None, dve.start + dve.k)

        def gates_sum():
            pe.wait("g_log")
            gsum = bank[5][:, 0:NT * A_HEADS].rearrange("p (t n) -> p t n", t=NT)
            for t in range(NT):
                mm = T.matmul(gsum[:, t, :], upper[:], g_log[:, t, :], start=True, stop=True)
            act.wait(pe.done(mm))
            act.done(A.activation(e_cum, gsum, ACT.Exp))
            act.done(A.copy(g_cum, gsum), "gates")
            dve.wait("gates")

        wide_f = wide[:].rearrange("p a n -> p (a n)")
        cv = wide_f[:, 0:4 * S].rearrange("p (a n) -> p a n", a=4)
        qkn = wide_f[:, 1024:1536].rearrange("p (a n) -> p a n", a=4)
        qkt = wide_f[:, 1536:2048].rearrange("p (a n) -> p a n", a=4)
        vbeta = row[:, 0:512].rearrange("p (a n) -> p a n", a=NT)
        o = row[:, 512:1024].rearrange("p (a n) -> p a n", a=NT)
        zs = sb("d_z", [P, NT, A_DV], scope=scope)
        up_dec, lo_dec = sb("d_up_dec", [P, NT, P], scope=scope), sb("d_lo_dec", [P, NT, P], scope=scope)
        e_row = sb("d_e_row", [P, P], scope=scope)
        low = sb("d_low", [P, NT, P], scope=scope)
        low_b = sb("d_low_b", [P, 2, NT, P], scope=scope)
        att = sb("d_att", [P, NT, P], scope=scope)
        xt = sb("d_xt", [P, 4, P], scope=scope)
        z = sb("d_zm", [P, NT, P], scope=scope)
        kb, kdec, qexp, nwt = (sb(n, [P, P], scope=scope) for n in ("d_kb", "d_kdec", "d_qexp", "d_nwt"))
        vn = sb("d_vn", [P, NT, A_DV], scope=scope)
        state = sb("d_state", [P, A_DV], scope=scope)
        ids = ident[:].unsqueeze(1).to_broadcast([P, NT, P])
        two = lambda ap: ap.rearrange("p (a n) -> p a n", a=NT)

        def conv_post(hd, s, b, ready):
            cw = conv_a[:, bass.ds(hd, 1), :, :].rearrange("p a b c -> p (a b) c")

            def newest():
                A.wait_ge(*ready)
                if "flipped" in Lane.names:
                    act.wait(("flipped", "v_turned")[s])
                for i in range(2):
                    y = 2 * s + i
                    act.done(A.activation(cv[:, y, :], bank[b][:, i * S:(i + 1) * S], ACT.Copy, scale=cw[:, y, 3:4]), f"tap{s}")

            def older(back):
                dve.wait(f"tap{s}" if back == 1 else f"conv{s}")
                for i in range(2):
                    y = 2 * s + i
                    dve.done(V.scalar_tensor_tensor(
                        cv[:, y, back:S], bank[b][:, i * S:(i + 1) * S - back], cw[:, y, 3 - back:4 - back],
                        cv[:, y, back:S], ALU.mult, ALU.add), f"conv{s}")

            def silu():
                act.wait(f"conv{s}")
                act.done(A.activation(cv[:, 2 * s:2 * s + 2, :], cv[:, 2 * s:2 * s + 2, :], ACT.Silu), f"silu{s}")
            return [newest] + [lambda back=back: older(back) for back in (1, 2, 3)] + [silu]

        def inverse_steps(hd):
            h1 = bass.ds(hd, 1)

            def flip_qk():
                pe.wait_last_lap("silu0", "att")
                for j in range(4):
                    mm = T.transpose(bank[4][:, j * P:(j + 1) * P], cv[:, j // 2, (j % 2) * P:(j % 2 + 1) * P], ident[:])
                pe.done(mm, "flipped")

            def flip_v():
                pe.wait_last_lap("silu1")
                for t in range(NT):
                    for f in range(2):
                        mm = T.transpose(bank[5][:, t * A_DV + f * P:t * A_DV + (f + 1) * P],
                                         cv[:, 2 + f, t * P:(t + 1) * P], ident[:])
                pe.done(mm, "v_turned")

            def norms():
                act.wait("flipped")
                act.wait_last_lap("sq_o")
                for j in range(4):
                    m = act.done(A.activation(sq_junk[:, j * P:(j + 1) * P], bank[4][:, j * P:(j + 1) * P], ACT.Square,
                                              accum_out=small[:, 32 + j:33 + j]), "sq_qk")
                pool.wait(m)
                rsqrt_col(36, 32, 4)
                Lane.names["r_qk"] = Mark(pool, Lane.loop, pool.k if Lane.loop else pool.start + pool.k)

            def row_decay():
                dve.wait_last_lap("row_g")
                m = dve.done(V.tensor_copy(small[:, 46:48], g_log[:, :, h1].rearrange("p t a -> p (t a)")))
                pe.wait(m)
                pe.wait_last_lap("inv")
                for t in range(NT):
                    mm = T.matmul(bank[7][:, t * P:(t + 1) * P], small[:, 46 + t:47 + t].to_broadcast([P, P]), upper[:],
                                  start=True, stop=True)
                dve.wait(pe.done(mm, "row_g"))
                dve.wait_last_lap("e_last")
                for t in range(NT):
                    gc = g_cum[:, t, h1]
                    gr = bank[7][:, t * P:(t + 1) * P]
                    dve.done(V.tensor_scalar(up_dec[:, t, :], gr, gc, 0.0, ALU.subtract, ALU.min))
                    dve.done(V.tensor_scalar(lo_dec[:, t, :], gr, gc, 0.0, ALU.subtract, ALU.max))
                m = dve.done(V.tensor_scalar(small[:, 44:45], bank[7][:, P - 1:P], g_cum[:, 0, h1], None, ALU.subtract))
                act.wait(m)
                m = act.done(A.activation(lo_dec[:], lo_dec[:], ACT.Exp, scale=-1.0))
                pool.wait(m)
                pool.done(G.tensor_tensor(lo_dec[:], lo_dec[:], lower[:].unsqueeze(1).to_broadcast([P, NT, P]), ALU.mult), "lo_dec")
                m = act.done(A.activation(up_dec[:], up_dec[:], ACT.Exp))
                pool.wait(m)
                pool.done(G.tensor_tensor(up_dec[:], up_dec[:], upper[:].unsqueeze(1).to_broadcast([P, NT, P]), ALU.mult), "up_dec")
                act.wait_last_lap("qexp")
                act.done(A.activation(e_row[:], bank[7][:, P:S], ACT.Exp), "e_row")
                act.done(A.activation(small[:, 44:45], small[:, 44:45], ACT.Exp), "e_last")

            def scale_qk():
                dve.wait("r_qk")
                for j in range(4):
                    m = dve.done(V.tensor_scalar(qkn[:, j, :], bank[4][:, j * P:(j + 1) * P], small[:, 36 + j:37 + j],
                                                 A_DK ** -0.5 if j < 2 else 1.0, ALU.mult, ALU.mult), "qkn")

            def back_qk():
                pe.wait("qkn")
                for j in range(4):
                    mm = T.transpose(bank[6][:, j * P:(j + 1) * P], qkn[:, j, :], ident[:])
                act.wait(pe.done(mm))
                act.done(A.copy(qkt.rearrange("p a n -> p (a n)"), bank[6][:, :]), "qkt")

            def products():
                pe.wait("qkt")
                for t in range(NT):
                    T.matmul(bank[4][:, t * P:(t + 1) * P], qkt[:, 2 + t, :], qkt[:, 2 + t, :], start=True, stop=True)
                for t in range(NT):
                    mm = T.matmul(bank[4][:, (2 + t) * P:(3 + t) * P], qkt[:, 2 + t, :], qkt[:, t, :], start=True, stop=True)
                dve.wait(pe.done(mm, "qk_products"), "lo_dec")
                for t in range(NT):
                    m = dve.done(V.scalar_tensor_tensor(low[:, t, :], bank[4][:, t * P:(t + 1) * P],
                                                        beta[:, t, h1], lo_dec[:, t, :], ALU.mult, ALU.mult), "low")

            def start_inverse():
                pe.wait("low")
                for t in range(NT):
                    mm = T.transpose(bank[6][:, t * P:(t + 1) * P], low[:, t, :], ident[:])
                m = pe.done(mm)
                dve.wait("low")
                dve.wait_last_lap("v1")
                m1 = dve.done(V.tensor_tensor(xt[:, 2:4, :], low[:], levels[:, 0:1, :].to_broadcast([P, NT, P]), ALU.mult))
                dve.wait(m)
                m2 = dve.done(V.tensor_tensor(xt[:, 0:2, :], two(bank[6][:, 0:S]),
                                              level0_t[:].unsqueeze(1).to_broadcast([P, NT, P]), ALU.mult))
                dve.wait(m1)
                dve.done(V.tensor_tensor(xt[:, 2:4, :], ids, xt[:, 2:4, :], ALU.subtract))
                dve.wait(m2)
                dve.done(V.tensor_tensor(xt[:, 0:2, :], ids, xt[:, 0:2, :], ALU.subtract), "inv")
                blocks(1)
                blocks(2)

            def blocks(b):
                pool.wait("low")
                if b > 2:
                    pool.wait(f"z{b - 2}")
                else:
                    pool.wait_last_lap(f"z{LEVELS - 3 + b}")
                pool.done(G.tensor_tensor(low_b[:, b % 2], low[:], levels[:, b:b + 1, :].to_broadcast([P, NT, P]), ALU.mult),
                          f"blocks{b}")

            def level_a(b):
                pe.wait(f"blocks{b}", "inv")
                for t in range(NT):
                    mm = T.matmul(bank[6][:, t * P:(t + 1) * P], low_b[:, b % 2, t, :], xt[:, t, :], start=True, stop=True)
                m = pe.done(mm, f"z{b}")
                if b + 2 < LEVELS:
                    blocks(b + 2)
                act.wait(m)
                if b > 1:
                    act.wait("zx")
                act.done(A.copy(z[:].rearrange("p a n -> p (a n)"), bank[6][:, 0:S]), "z")

            def level_b(b):
                pe.wait("z")
                for t in range(NT):
                    mm = T.matmul(bank[7][:, t * P:(t + 1) * P], xt[:, 2 + t, :], z[:, t, :], start=True, stop=True)
                w = 2
                if b < LEVELS - 1:
                    w = 4
                    for t in range(NT):
                        mm = T.matmul(bank[7][:, (2 + t) * P:(3 + t) * P], z[:, t, :], xt[:, 2 + t, :], start=True, stop=True)
                dve.wait(pe.done(mm, "zx"))
                dve.done(V.tensor_tensor(xt[:, 0:w, :], xt[:, 0:w, :],
                                         bank[7][:, 0:w * P].rearrange("p (a n) -> p a n", n=P), ALU.subtract), "inv")

            def sides():
                dve.wait("v_turned", "up_dec")
                dve.wait_last_lap("outputs")
                for t in range(NT):
                    dve.done(V.tensor_scalar(vbeta[:, t, :], bank[5][:, t * A_DV:(t + 1) * A_DV],
                                             beta[:, t, h1], None, ALU.mult), "vbeta")
                dve.done(V.tensor_tensor(att[:], two(bank[4][:, 2 * P:4 * P]), up_dec[:], ALU.mult), "att")
                dve.done(V.tensor_scalar(kb[:], qkn[:, 3, :], beta[:, 1, h1], e_cum[:, 1, h1], ALU.mult, ALU.mult), "kb")
                dve.wait("e_last", "e_row", "qkt")
                dve.done(V.tensor_scalar(kdec[:], qkn[:, 2, :], small[:, 44:45], None, ALU.mult), "kdec")
                dve.done(V.tensor_tensor(qexp[:], qkt[:, 1, :], e_row[:], ALU.mult), "qexp")

            steps = [row_decay, flip_qk, norms, flip_v, scale_qk, back_qk, products, start_inverse]
            for b in range(1, LEVELS):
                steps += [lambda b=b: level_a(b), lambda b=b: level_b(b)]
                if b == 2:
                    steps.append(sides)
            return steps

        def output_steps(hd):
            b3_ = bank[3]

            def first_values():
                pe.wait_last_lap("inv", "vbeta", "kb", "mid_lo")
                T.matmul(b3_[:, 0:A_DV], xt[:, 0, :], vbeta[:, 0, :], start=True, stop=True)
                m = pe.done(T.matmul(b3_[:, A_DV:A_DV + P], kb[:], xt[:, 1, :], start=True, stop=True))
                act.wait(m)
                act.wait_last_lap("o_read")
                act.done(A.copy(vn[:, 0, :], b3_[:, 0:A_DV]), "v0")
                act.done(A.activation(nwt[:], b3_[:, A_DV:A_DV + P], ACT.Copy, scale=-1.0), "nwt")

            def first_state():
                pe.wait("nwt")
                pe.wait_last_lap("kdec")
                m = pe.done(T.matmul(b3_[:, 0:A_DV], kdec[:], vn[:, 0, :], start=True, stop=True))
                act.wait(m)
                act.done(A.copy(state[:], b3_[:, 0:A_DV]), "state")

            def second_values():
                pe.wait("state")
                T.matmul(b3_[:, 0:A_DV], xt[:, 1, :], vbeta[:, 1, :], start=True, stop=False)
                m = pe.done(T.matmul(b3_[:, 0:A_DV], nwt[:], state[:], start=False, stop=True), "v1")
                act.wait(m)
                act.done(A.copy(vn[:, 1, :], b3_[:, 0:A_DV]), "vn")

            def outputs():
                pe.wait("vn")
                pe.wait_last_lap("att", "qexp")
                T.matmul(b3_[:, 0:A_DV], att[:, 0, :], vn[:, 0, :], start=True, stop=True)
                T.matmul(b3_[:, A_DV:], qexp[:], state[:], start=True, stop=False)
                m = pe.done(T.matmul(b3_[:, A_DV:], att[:, 1, :], vn[:, 1, :], start=False, stop=True), "outputs")
                act.wait(m)
                if "sq_qk" in Lane.names:
                    act.wait("sq_qk")
                for t in range(NT):
                    m = act.done(A.activation(sq_junk[:, t * A_DV:(t + 1) * A_DV], b3_[:, t * A_DV:(t + 1) * A_DV],
                                              ACT.Square, scale=A_DV ** -0.5, accum_out=small[:, 40 + t:41 + t]), "sq_o")
                pool.wait(m)
                m = rsqrt_col(42, 40, NT)
                dve.wait(m)
                for t in range(NT):
                    m = dve.done(V.scalar_tensor_tensor(o[:, t, :], b3_[:, t * A_DV:(t + 1) * A_DV], small[:, 42 + t:43 + t],
                                                        norm_a[:], ALU.mult, ALU.mult), "o_read")
                dve.wait(m)
                dve.wait_last_lap("zs")
                dve.done(V.tensor_tensor(o, o, zs[:], ALU.mult), "gated")

            def store():
                pe.wait("gated")
                for f in range(2):
                    for t in range(NT):
                        mm = T.transpose(b3_[:, f * S + t * P:f * S + (t + 1) * P], o[:, t, f * P:(f + 1) * P], ident[:])
                m = pe.done(mm, "o_turned")
                o3 = two(b3_[:, :])
                hi = mid_hi[:, bass.ds(hd * 2, 2), :]
                act.wait(m)
                dve.wait(act.done(A.copy(hi, o3)))
                dve.done(V.tensor_tensor(mid_lo[:, bass.ds(hd * 2, 2), :], o3, hi.bitcast(F32), ALU.subtract), "mid_lo")

            return [first_values, first_state, second_values, outputs, store]

        def delta_units(name, hd, feed, arrived, fresh=None):
            at = lambda s: (unit_done, unit_mark(name, hd, s))

            def begin(s, *free):
                arrived(s)
                pe.wait_last_lap(*free)

            def keep_v():
                A.wait_ge(*at(2))
                act.done(A.copy(v_ret[:, :, bass.ds(head * 256, 256)], two(bank[0][:, :])), "v_ret")
            head = hd if name == "delta_first" else hd + 1
            u = feature_major(0, 0, 2, (h_hi, h_lo), lambda: begin(0, "v_ret"), fresh=fresh)
            u += feature_major(1, 1, 2, (h_hi, h_lo), lambda: begin(1, "conv1"))

            def vb_begin():
                arrived(2)
                pe.wait("conv0")
            u += token_major(2, 0, (h_hi, h_lo), vb_begin)
            return u, conv_post(head, 0, 0, at(0)), conv_post(head, 1, 1, at(1)), [keep_v]

        def silu_z(z_ready):
            A.wait_ge(*z_ready)
            if "gated" in Lane.names:
                act.wait("gated")
            act.done(A.activation(zs[:].rearrange("p a n -> p (a n)"), bank[2][:, :], ACT.Silu), "zs")

        def z_unit(s, arrived, *free):
            def begin():
                arrived(s)
                pe.wait_last_lap("zs", *free)
            return token_major(s, 2, (h_hi, h_lo), begin)

        def delta_first(lap, feed, arrived):
            u, conv_qk, conv_v, keep = delta_units("delta_first", 0, feed, arrived, ready)
            weave((u, 0, 1), ([gates_project, gates, gates_sum], "first_gates"), (conv_qk, "first_conv_qk"),
                  (conv_v, "first_conv_v"), (keep, 1, 1.1), *feed.at("first_feed"))
        stage("delta_first", delta_first)

        def delta(lap, feed, arrived):
            u, conv_qk, conv_v, keep = delta_units("delta", lap, feed, arrived)
            units = u + z_unit(3, arrived)
            z_end = [lambda: silu_z((unit_done, unit_mark("delta", lap, 3)))]
            parts = [(units, 0, 1), (conv_qk, "d_conv_qk"), (conv_v, "d_conv_v"), (keep, "d_keep"), (z_end, 1.01, 1.02)]
            parts += feed.at("d_feed")
            parts += [(inverse_steps(lap), "d_inverse")]
            if not (isinstance(lap, int) and lap == 0):
                parts += [(output_steps(lap - 1), "d_outputs")]
            weave(*parts)
        stage("delta", delta, peel=2)
        LAST = A_HEADS - 1

        def delta_gate(lap, feed, arrived):
            units = []

            def keep(n, banks):
                A.wait_ge(unit_done, unit_mark("delta_gate", lap, 2 * n + 1))
                act.wait("kb", "kdec", "qexp", "qk_products")
                for t in (1, 0):
                    act.done(A.activation(chunk(wide, t, n), bank[banks[t]][:, :], ACT.Sigmoid), f"sg{t}")
            for s, (block, n) in enumerate(BY_COLUMNS):
                banks = ((0, 1), (2, 1))[n]

                def begin(s=s):
                    arrived(s)
                    if s == 0:
                        pe.wait("v_ret", "conv1")
                    if s == 2:
                        pe.wait("zs")
                u = square_unit(s, block, KD, (h_hi, h_lo), banks, begin)
                if s == 2:
                    u = u[:2] + [lambda: keep(0, (0, 1)), lambda: pe.wait("sg1")] + u[2:]
                units += u
            weave((units, 0, 1), (inverse_steps(LAST), "g_inverse"), (output_steps(LAST - 1), "g_outputs"),
                  *feed.at("g_feed"))
            keep(1, (2, 1))
        stage("delta_gate", delta_gate)

        br_banks = [(4, 5), (6, 7)]

        def br_a_unit(s, at, arrived, last=False):
            block, n = BR_A[at]

            def begin():
                arrived(s)
                if at == 0:
                    pe.wait("att", "vbeta")
                if at == 3:
                    pe.wait("inv", "e_row", "e_last", "z")
                if block == 3:
                    pe.wait("mid_lo")
            return square_unit(s, block, 2 * KD, (mid_hi, mid_lo), br_banks[n], begin)

        def delta_last(lap, feed, arrived):
            units = z_unit(0, arrived, "sg0", "sg1")
            for j in range(3):
                units += br_a_unit(1 + j, j, arrived)
            weave((units, 0, 1), ([lambda: silu_z((unit_done, unit_mark("delta_last", lap, 0)))], 0.27, 0.3),
                  (output_steps(LAST), "l_outputs"), *feed.at("l_feed"))
        stage("delta_last", delta_last)
        scope.close()
        b3.close()
        ret = ExitStack()
        retain = sb("retain", [P, B_HEADS, 384], scope=ret)
        cos_b, sin_b = sb("cos_b", [P, S], scope=ret), sb("sin_b", [P, S], scope=ret)
        norm_b = sb("norm_b", [P, B_DV], scope=ret)
        in_ret = phase_load([(retain[:].rearrange("p a n -> p (a n)"), a["retain"]), (cos_b[:], a["cos_b"]), (sin_b[:], a["sin_b"])],
                            everything())

        def br_a(lap, feed, arrived):
            for s in range(4):
                weave((br_a_unit(s, 3 + s, arrived) + [feed], 0, 1))
        stage("br_a", br_a)

        def br_a_last(lap, feed, arrived):
            weave((br_a_unit(0, 7, arrived) + [feed], 0, 1))
            feed(4)
            for n in range(2):
                V.wait_ge(unit_done, unit_mark("br_a", 0, 3) if n == 0 else unit_mark("br_a_last", 0, 0))
                if n == 0:
                    dve.wait("sg0", "sg1", *everything())
                for t in range(NT):
                    dve.done(V.tensor_tensor(chunk(wide, t, n), chunk(wide, t, n), bank[br_banks[n][t]][:, :], ALU.mult),
                             "mixed")
        stage("br_a_last", br_a_last)

        ctx.enter_context(ret)
        qk_rot = sb("r_qk", [P, 2, 2, S], scope=ret)
        sw = row[:, 0:512].rearrange("p (a n) -> p a n", a=2)
        scr = row[:, 512:896]
        gsl = sb("r_g", [P, NT, B_DV], scope=ret)
        ob = sb("r_o", [P, NT, B_DV], scope=ret)
        norm_in = sem("norm_in")
        dve.wait(*everything())
        phase_ready(in_ret, dve)

        def rotary_b(j, ready):
            V.wait_ge(*ready)
            if "scored" in Lane.names:
                dve.wait("scored")
            u = two(bank[j][:, :])
            dve.done(V.tensor_tensor(qk_rot[:, j], u, cos_b[:].unsqueeze(1).to_broadcast([P, 2, S]), ALU.mult))
            if j:
                dve.wait("rot0")
            else:
                dve.wait_last_lap("rot1")
            dve.done(V.tensor_tensor(sw[:, 0, :], u[:, 1, :], sin_b[:], ALU.mult))
            dve.wait(dve.done(V.tensor_tensor(sw[:, 1, :], u[:, 0, :], sin_b[:], ALU.mult)))
            dve.done(V.tensor_tensor(qk_rot[:, j, 0, :], qk_rot[:, j, 0, :], sw[:, 0, :], ALU.subtract))
            dve.done(V.tensor_tensor(qk_rot[:, j, 1, :], qk_rot[:, j, 1, :], sw[:, 1, :], ALU.add), f"rot{j}")

        def retention_steps(hd, norm_value):
            def score():
                pe.wait_last_lap("rot0", "rot1", "scr", "mid_lo")
                for c0, w, k0, q0 in ((0, S, 0, 0), (S, P, P, P)):
                    for f in range(2):
                        mm = T.matmul(bank[4][:, c0:c0 + w], qk_rot[:, 1, f, k0:k0 + P], qk_rot[:, 0, f, q0:q0 + w],
                                      start=f == 0, stop=f == 1)
                dve.wait(pe.done(mm, "scored"))
                dve.wait_last_lap("o_done")
                dve.done(V.tensor_tensor(scr, bank[4][:, 0:384],
                                         retain[:, bass.ds(hd, 1), :].rearrange("p a n -> p (a n)"), ALU.mult), "scr")

            def output(t):
                pe.wait("scr")
                pe.wait_last_lap("ob")
                vv = [v_ret[:, j, bass.ds(hd * B_DV, B_DV)] for j in range(NT)]
                if t == 0:
                    mm = T.matmul(bank[5][:, :], scr[:, 0:P], vv[0], start=True, stop=True)
                else:
                    T.matmul(bank[6][:, :], scr[:, P:S], vv[0], start=True, stop=False)
                    mm = T.matmul(bank[6][:, :], scr[:, S:384], vv[1], start=False, stop=True)
                act.wait(pe.done(mm, "o_done"))
                act.wait_last_lap("ob_turned")
                act.done(A.activation(ob[:, t, :], bank[5 + t][:, :], ACT.Square, scale=1 / 16,
                                      accum_out=small[:, 40 + t:41 + t]), "ob_sq")

            def scale():
                pool.wait("ob_sq")
                dve.wait(rsqrt_col(42, 40, NT, scale=256.0 / B_DV))
                V.wait_ge(norm_in, norm_value)
                for t in range(NT):
                    dve.done(V.scalar_tensor_tensor(ob[:, t, :], bank[5 + t][:, :], small[:, 42 + t:43 + t],
                                                    norm_b[:], ALU.mult, ALU.mult), "ob")
                dve.wait("ob")
                dve.wait_last_lap("gsl0", "gsl1")
                dve.done(V.tensor_tensor(ob[:], ob[:], gsl[:], ALU.mult), "ob_gated")

            def store(b, f0):
                pe.wait("ob_gated")
                for f in range(f0, f0 + 2):
                    for t in range(NT):
                        mm = T.transpose(bank[b][:, (f - f0) * S + t * P:(f - f0) * S + (t + 1) * P],
                                         ob[:, t, f * P:(f + 1) * P], ident[:])
                act.wait(pe.done(mm, "ob_turned"))
                o3 = two(bank[b][:, :])
                hi = mid_hi[:, bass.ds(hd * 4 + f0, 2), :]
                dve.wait(act.done(A.copy(hi, o3)))
                dve.done(V.tensor_tensor(mid_lo[:, bass.ds(hd * 4 + f0, 2), :], o3, hi.bitcast(F32), ALU.subtract), "mid_lo")
            return [score, lambda: output(0), lambda: output(1), scale, lambda: store(7, 0), lambda: store(4, 2)]

        def load_norm_b(hd):
            if "ob" in Lane.names:
                act.wait("ob")
            A.dma_start(norm_b[:], a["norm_b"][0:1, bass.ds(hd * B_DV, B_DV)].partition_broadcast(P)
                        .rearrange("p a n -> p (a n)")).then_inc(norm_in, 16)

        def retention(hd, feed, arrived):
            at = lambda s: (unit_done, unit_mark("retention", hd, s))
            later = not isinstance(hd, int) or hd > 0

            def begin(s, *free):
                arrived(s)
                pe.wait_last_lap(*free)
            units = feature_major(0, 0, 2, (h_hi, h_lo), lambda: begin(0, "rot0"))
            units += feature_major(1, 1, 2, (h_hi, h_lo), lambda: begin(1, "rot1"))
            units += token_major(2, 2, (h_hi, h_lo), lambda: begin(2, "gsl0"))
            units += token_major(3, 3, (h_hi, h_lo), lambda: begin(3, "gsl1"))
            parts = [(units, 0, 1), ([lambda: rotary_b(0, at(0))], "r_rot0"), ([lambda: rotary_b(1, at(1))], "r_rot1")]
            if later:
                parts.append((retention_steps(hd - 1, hd * 16), "r_steps"))
            weave(*parts, *feed.at("r_feed"))
            load_norm_b(hd)
            for j in range(2):
                A.wait_ge(*at(2 + j))
                if "ob_gated" in Lane.names:
                    act.wait("ob_gated")
                act.done(A.activation(gsl[:, :, j * 256:(j + 1) * 256], two(bank[2 + j][:, :]), ACT.Silu), f"gsl{j}")
        stage("retention", retention, peel=1)

        sig = v_ret[:].rearrange("p t n -> p (t n)")[:, 0:NT * D].rearrange("p (t n) -> p t n", t=NT)

        def gate_b(lap, feed, arrived):
            units = []
            for s, (block, n) in enumerate(BY_COLUMNS):
                def begin(s=s, n=n):
                    arrived(s)
                    if s == 0:
                        pe.wait("rot0", "rot1")
                    if s == 2:
                        pe.wait("gsl0", "gsl1")
                units += square_unit(s, block, KD, (h_hi, h_lo), [(0, 1), (2, 3)][n], begin)
            weave((units, 0, 1), (retention_steps(B_HEADS - 1, B_HEADS * 16), "rg_steps"), *feed.at("rg_feed"))
            for n in range(2):
                A.wait_ge(unit_done, unit_mark("gate_b", lap, 2 * n + 1))
                act.wait("o_done")
                for t in range(NT):
                    act.done(A.activation(chunk(sig, t, n), bank[2 * n + t][:, :], ACT.Sigmoid), f"sig{n}")
        stage("gate_b", gate_b)

        def br_b(lap, feed, arrived):
            for s in range(4):
                def begin(s=s):
                    arrived(s)
                    if s == 0 and lap == 0:
                        pe.wait("scr", "mid_lo")
                    if s == 0 and lap == 1:
                        pe.wait("ob")
                if s == 2 and lap == 1:
                    mix_ready.extend(turned(mix_marks, [(None, h_hi, h_lo)], range(2)))
                weave((square_unit(s, s, 2 * KD, (mid_hi, mid_lo), br_banks[lap], begin) + ([feed] if s < 3 else []), 0, 1))
            V.wait_ge(unit_done, unit_mark("br_b", lap, 3))
            dve.wait(f"sig{lap}")
            mixed = []
            for t in range(NT):
                mixed.append(dve.done(V.tensor_tensor(chunk(sig, t, lap), chunk(sig, t, lap), bank[br_banks[lap][t]][:, :], ALU.mult)))
            for t in range(NT):
                dve.wait(mixed[t])
                mixed[t] = dve.done(V.tensor_tensor(chunk(wide, t, lap), chunk(wide, t, lap), chunk(sig, t, lap), ALU.add))
            mix_marks.append(tuple(mixed))
        mix_marks, mix_ready = [], []
        stage("br_b", br_b)
        ret.close()
        b2.close()
        retention_over = everything()
        in_row = [phase_load(row_of(1), ["ob_turned"])]

        end = ExitStack()
        ctx.enter_context(end)
        junk = sb("junk", [P, NT, D], scope=end)

        def squares_of(chunks, banks, wait_ready):
            for t, n in chunks:
                wait_ready(act, t, n)
                m = act.done(A.activation(chunk(junk, t, n), bank[banks[n][t]][:, :], ACT.Square, scale=D ** -0.5,
                                          accum_out=small[:, 2 * t + n:2 * t + n + 1]), "squares")

        def add_normed(banks, keep=None):
            pool.wait("squares")
            dve.wait(rsqrt_col(4, 0, NT, halves=True))
            phase_ready(in_row[-1], dve)
            marks = {}
            for t, n in CHUNKS:
                m = dve.done(V.scalar_tensor_tensor(chunk(wide, t, n), bank[banks[n][t]][:, :], small[:, 4 + t:5 + t],
                                                    row[:, n * 512:(n + 1) * 512], ALU.mult, ALU.mult))
                dve.wait(m)
                marks[t, n] = dve.done(V.tensor_tensor(chunk(x, t, n), chunk(x, t, n), chunk(wide, t, n), ALU.add), "x")
                if keep:
                    keep(t, n)
            return marks
        marks = {}

        def w_out(lap, feed, arrived):
            banks = [(0, 1), (2, 3)]

            def ready(ln, t, n):
                ln.eng.wait_ge(unit_done, unit_mark("w_out", lap, 2 * n + 1))
            for s, (block, n) in enumerate(BY_COLUMNS):
                if s == 1:
                    mix_ready.extend(turned(mix_marks, [(None, h_hi, h_lo)], range(2, 4)))
                weave((square_unit(s, block, KD, (h_hi, h_lo), banks[n], lambda s=s: arrived(s),
                                   fresh=mix_ready if n == 0 else None) + [feed], 0, 1))
                if s == 2:
                    act.wait(*retention_over)
                    squares_of(CHUNKS[:2], banks, ready)
            squares_of(CHUNKS[2:], banks, ready)
            marks.update(add_normed(banks))
        stage("w_out", w_out)
        m = mean_squares(x, marks, junk)
        in_row.append(phase_load(row_of(2), ["x"]))
        ready = normed(x, m, [(6, h_hi, h_lo)])

        rl = sb("m_relu", [P, 2, 2 * S], scope=end)
        sq = sb("m_sq", [P, 2, 2 * S], scope=end)
        parts, last_parts = ([sb(f"m_{p}_{b}", [P, 4, S], F32R, scope=end) for p in ("hi", "lo")] for b in ("all", "last"))
        acc = [(4, 5), (6, 7)]
        zero_r = zeros(end)

        def m_up(arrived, fresh=None, b0=0):
            steps = []
            for s in range(2):
                def begin(s=s):
                    arrived(s)
                    if b0 == 0:
                        pe.wait_last_lap(f"sq{s}")
                steps += feature_major(s, b0 + s, 2, (h_hi, h_lo), begin, fresh=None if s else fresh)
            weave((steps, 0, 1))

        def m_post(st, j, feed, g, down_value=None, b0=0):
            for s in range(2):
                A.wait_ge(unit_done, unit_mark(st, j, s))
                act.wait_last_lap(f"sq{s}", "gm")
                m = act.done(A.activation(rl[:, s, :], bank[b0 + s][:, :], ACT.Relu))
                dve.wait(m)
                dve.done(V.scalar_tensor_tensor(sq[:, s, :], bank[b0 + s][:, :], 0.0, rl[:, s, :], ALU.max, ALU.mult), f"sq{s}")
                feed()
            if down_value is not None:
                feed()
                A.wait_ge(unit_done, down_value)
            act.wait("sq0", "sq1")
            sqv = sq[:].rearrange("p a (b n) -> p (a b) n", n=S)
            dve.wait(act.done(A.copy(g[0][:], sqv)))
            dve.done(V.tensor_tensor(g[1][:], sqv, g[0][:].bitcast(F32), ALU.subtract), "gm")

        def m_down(s0, g, arrived, marks=None):
            def product(kk, t, n):
                wh, wl = parts_of(s0 + kk // 2, 2, D)
                tk, nn = slice(t * P, (t + 1) * P), slice(n * 512, (n + 1) * 512)
                return three(bank[acc[t][n]][:, :], g[0][:, kk, tk], g[1][:, kk, tk], wh[:, kk % 2, nn], wl[:, kk % 2, nn],
                             False, True, skip_group_check=True)
            if marks is None:
                for kk in range(4):
                    if kk % 2 == 0:
                        arrived(s0 + kk // 2)
                    for t, n in CHUNKS:
                        mm = product(kk, t, n)
                    if kk % 2:
                        mm.then_inc(unit_done, 1)
                return
            arrived(s0)
            arrived(s0 + 1)
            for t, n in CHUNKS:
                for kk in range(4):
                    mm = product(kk, t, n)
                    if (t, n) == CHUNKS[-1] and kk % 2:
                        mm.then_inc(unit_done, 1)
                if (t, n) != CHUNKS[-1]:
                    marks[t, n] = pe.done(mm)

        def m_first(j, feed, arrived):
            feed(3)
            m_up(arrived, ready, 2)
            pe.wait("turned", "zeros")
            for t in range(NT):
                for n in range(2):
                    T.matmul(bank[acc[t][n]][:, :], zero_r[:, 0:P], zero_r[:], start=True, stop=True, skip_group_check=True)
            m_post("mlp_first", j, feed, parts, b0=2)
        stage("mlp_first", m_first)

        def m_middle(j, feed, arrived):
            m_up(arrived)
            pe.wait_last_lap("gm")
            m_down(2, parts, arrived)
            if isinstance(j, int) and j == info["mlp"].laps - 1:
                m_post("mlp", j, feed, last_parts)
            else:
                m_post("mlp", j, feed, parts, unit_mark("mlp", j, 3))
        stage("mlp", m_middle, peel=1)

        def m_last(j, feed, arrived):
            pe.wait("gm")
            done = {}
            m_down(0, last_parts, arrived, done)

            def wait_ready(ln, t, n):
                if (t, n) in done:
                    ln.wait(done[t, n])
                else:
                    ln.eng.wait_ge(unit_done, unit_mark("mlp_last", j, 1))

            def keep(t, n):
                act.wait("x")
                A.dma_start(out[t * P:(t + 1) * P, n * 512:(n + 1) * 512], chunk(x, t, n)).then_inc(out_done, 16)
            squares_of(CHUNKS, [(4, 6), (5, 7)], wait_ready)
            add_normed([(4, 6), (5, 7)], keep)
        stage("mlp_last", m_last)
        A.wait_ge(out_done, 16 * NT * 2)
    return new_plan


class FirstPass(dict):

    def __init__(self, lanes):
        super().__init__()
        self.lanes = lanes

    def __missing__(self, key):
        return self.lanes[0], 1


def arrays(i):
    def column(v):
        return v.reshape(KD, P).T
    out = {
        "x": i["x"][0], "positions": i["positions"], "stream": weight_stream(i),
        "gains": np.stack([column(v) for v in (
            i["attn_norm"][0], i["ffn_norm"][0], i["kv_norm"], i["attn_norm"][1], i["ffn_norm"][1],
            i["norm_mix_pre_2"][0], i["norm_mlp_pre_2"][0])], 1).reshape(P, -1),
        "rows": np.stack([i["final_norm"], i["norm_mix_post_2"][0], i["norm_mlp_post_2"][0]]),
        "norm_a": i["norm_a_2"], "norm_b": i["norm_b_2"],
        "sinks": i["sinks_b"], "a_log": i["a_log_2"], "dt_bias": i["dt_bias_2"],
        "w_ba": cols_unit(i["w_in_2"][0], (C_BA, 2 * A_HEADS)),
    }
    taps = np.concatenate([i["conv_w"], i["conv_b"][:, None, :]], 1)
    taps = taps.reshape(2, 4, 2, F_LAPS, 2, P)
    out["conv"] = taps.transpose(5, 0, 3, 2, 4, 1).reshape(P, -1)
    ca = i["conv_a_2"][0].reshape(4, 32, P)
    per_head = np.stack([ca[:, 0:8], ca[:, 8:16], ca[:, 16:32:2], ca[:, 17:32:2]], 2)
    out["conv_a"] = per_head.transpose(3, 1, 2, 0).reshape(P, -1)
    out.update(constants())
    return {k: np.ascontiguousarray(v) for k, v in out.items()}


def kernel(**inputs):
    import concourse.bacc as bacc
    from concourse.bass_utils import run_bass_kernel_spmd

    host = arrays({k: np.asarray(v) for k, v in inputs.items()})

    def build(plan):
        nc = bacc.Bacc("TRN2", target_bir_lowering=False, num_devices=1)
        dram = {n: nc.dram_tensor(n, v.shape, mybir.dt.from_np(v.dtype), kind="ExternalInput").ap()
                for n, v in host.items()}
        out = nc.dram_tensor("out", (S, D), F32, kind="ExternalOutput").ap()
        return nc, program(nc, dram, out, plan)

    _, plan = build({})
    nc, again = build(plan)
    assert plan == again
    r = run_bass_kernel_spmd(nc, [host], core_ids=[0])
    return r.results[0]["out"].reshape(1, S, D)
```
